# Optimizing a Trainium2 kernel written in Bass

```python
import math
import jax, jax.numpy as jnp
from jax import lax
import numpy as np

D_MODEL = 1024
BATCH = 1
SEQ = 256
DEPTH = 2

GRID_W = 64
CTX_LEN = 256
N_EVEN = (DEPTH + 1) // 2
N_ODD = DEPTH // 2
D_FF = 4 * D_MODEL
NORM_EPS = 1e-6
NEG_INF = -1e30

FNET_GROUPS = 8
FNET_GROUP_W = 64
FNET_W = FNET_GROUPS * FNET_GROUP_W
SSD_HEAD_DIM = 64
SSD_HEADS = 24
SSD_GROUPS = 4
SSD_HPG = SSD_HEADS // SSD_GROUPS
SSD_STATE = 128
SSD_INNER = SSD_HEADS * SSD_HEAD_DIM
SSD_CONV_DIM = SSD_INNER + 2 * SSD_GROUPS * SSD_STATE
SSD_CONV_W = 5
SSD_CHUNK = 128
EVEN_IN = FNET_W + SSD_INNER + SSD_CONV_DIM + 2 * SSD_HEADS
EVEN_MIX = FNET_W + SSD_INNER
HEAD_DIM = 64
WIN_Q_HEADS = 8
WIN_KV_HEADS = 2
WIN_GQA = WIN_Q_HEADS // WIN_KV_HEADS
WIN_RADIUS = 128
WIN_BLOCK = 128
NA_HEADS = 8
NA_ROWS = 8
NA_COLS = 16
ODD_IN = (WIN_Q_HEADS + 2 * WIN_KV_HEADS) * HEAD_DIM + 3 * NA_HEADS * HEAD_DIM
ODD_MIX = (WIN_Q_HEADS + NA_HEADS) * HEAD_DIM
ROPE_THETA = 10000.0

kernel_name = "hybrid_fourier_ssd_window_na_prefix_trunk"

def rms_norm(x, g):
    xf = x.astype(jnp.float32)
    y = xf * lax.rsqrt(jnp.mean(xf * xf, axis=-1, keepdims=True) + NORM_EPS)
    return (y * g.astype(jnp.float32)).astype(x.dtype)

def modulate(x, shift, scale):
    return x * (1 + scale) + shift

def sq_relu_mlp(x, w1, w2):
    return jnp.square(jax.nn.relu(x @ w1)) @ w2

def axial_rope_tables(n_tokens):
    pos = jnp.arange(n_tokens)
    row = (pos // GRID_W).astype(jnp.float32)
    col = (pos % GRID_W).astype(jnp.float32)
    n_freq = HEAD_DIM // 4
    inv = ROPE_THETA ** (-jnp.arange(n_freq, dtype=jnp.float32) / n_freq)
    ang = jnp.stack([row[:, None] * inv, col[:, None] * inv], axis=1)
    return jnp.cos(ang), jnp.sin(ang)

def apply_axial_rope(x, cos, sin):
    b, l, h, dh = x.shape
    xr = x.astype(jnp.float32).reshape(b, l, h, 2, 2, dh // 4)
    x1, x2 = xr[..., 0, :], xr[..., 1, :]
    cs, sn = cos[:, None], sin[:, None]
    out = jnp.stack([x1 * cs - x2 * sn, x2 * cs + x1 * sn], axis=-2)
    return out.reshape(b, l, h, dh).astype(x.dtype)

def centred_depthwise_conv(x, w, bias):
    k = w.shape[0]
    y = lax.conv_general_dilated(x, w[:, None, :].astype(x.dtype), window_strides=(1,),
                                 padding=[(k // 2, k // 2)], dimension_numbers=("NWC", "WIO", "NWC"),
                                 feature_group_count=x.shape[-1])
    return y + bias.astype(x.dtype)

def fourier_mix(u):
    b, l, _ = u.shape
    ug = u.astype(jnp.float32).reshape(b, l, FNET_GROUPS, FNET_GROUP_W)
    f = jnp.fft.fft2(ug, axes=(1, 3), norm="ortho")
    return jnp.real(f).reshape(b, l, FNET_W).astype(u.dtype)

def ssd_inputs(u_xbc, u_dt, conv_w, conv_b, dt_bias):
    b, l = u_xbc.shape[:2]
    xbc = jax.nn.silu(centred_depthwise_conv(u_xbc, conv_w, conv_b)).astype(jnp.float32)
    gn = SSD_GROUPS * SSD_STATE
    xs = xbc[..., :SSD_INNER].reshape(b, l, SSD_GROUPS, SSD_HPG, SSD_HEAD_DIM)
    bm = xbc[..., SSD_INNER:SSD_INNER + gn].reshape(b, l, SSD_GROUPS, SSD_STATE)
    cm = xbc[..., SSD_INNER + gn:].reshape(b, l, SSD_GROUPS, SSD_STATE)
    dt = jax.nn.softplus(u_dt.astype(jnp.float32).reshape(b, l, 2, SSD_GROUPS, SSD_HPG) + dt_bias)
    return xs, bm, cm, dt

def ssd_scan(xs, dt, a, bm, cm, h0):
    b, l = xs.shape[:2]
    nc, q = l // SSD_CHUNK, SSD_CHUNK
    xdt = (xs * dt[..., None]).reshape(b, nc, q, SSD_GROUPS, SSD_HPG, SSD_HEAD_DIM)
    a_cum = jnp.cumsum((dt * a).reshape(b, nc, q, SSD_GROUPS, SSD_HPG), axis=2)
    bc = bm.reshape(b, nc, q, SSD_GROUPS, SSD_STATE)
    cc = cm.reshape(b, nc, q, SSD_GROUPS, SSD_STATE)
    lower = jnp.tril(jnp.ones((q, q), dtype=bool))
    seg = a_cum[:, :, :, None] - a_cum[:, :, None, :]
    decay = jnp.exp(jnp.where(lower[:, :, None, None], seg, NEG_INF))
    cb = jnp.einsum("bclgn,bcsgn->bclsg", cc, bc)
    y_diag = jnp.einsum("bclsgr,bcsgrp->bclgrp", cb[..., None] * decay, xdt)
    decay_to_end = jnp.exp(a_cum[:, :, -1:] - a_cum)
    states = jnp.einsum("bcsgn,bcsgrp->bcgrpn", bc, xdt * decay_to_end[..., None])
    chunk_decay = jnp.exp(a_cum[:, :, -1])

    def carry_state(h, inp):
        s_c, d_c = inp
        return h * d_c[..., None, None] + s_c, h

    h_last, h_enter = lax.scan(carry_state, h0, (jnp.moveaxis(states, 1, 0), jnp.moveaxis(chunk_decay, 1, 0)))
    h_enter = jnp.moveaxis(h_enter, 0, 1)
    y_off = jnp.einsum("bclgn,bcgrpn->bclgrp", cc, h_enter) * jnp.exp(a_cum)[..., None]
    return (y_diag + y_off).reshape(b, l, SSD_GROUPS, SSD_HPG, SSD_HEAD_DIM), h_last

def bidir_ssd(xs, bm, cm, dt, a, h0_fwd, h0_bwd):
    y_f, h_f = ssd_scan(xs, dt[:, :, 0], a[0], bm, cm, h0_fwd)
    flip = lambda t: jnp.flip(t, axis=1)
    y_b, h_b = ssd_scan(flip(xs), flip(dt[:, :, 1]), a[1], flip(bm), flip(cm), h0_bwd)
    return y_f + flip(y_b), h_f, h_b

def ssd_output(y, xs, z, d_skip, norm_g):
    b, l = y.shape[:2]
    y = (y + d_skip[..., None] * xs).reshape(b, l, SSD_INNER) * jax.nn.silu(z.astype(jnp.float32))
    yg = y.reshape(b, l, SSD_GROUPS, SSD_INNER // SSD_GROUPS)
    yg = yg * lax.rsqrt(jnp.mean(yg * yg, axis=-1, keepdims=True) + NORM_EPS)
    return (yg.reshape(b, l, SSD_INNER) * norm_g.astype(jnp.float32)).astype(z.dtype)

def even_mixer(uc, ul, w_in, conv_w, conv_b, dt_bias, a_log, d_skip, ssd_norm_g, w_out, need_ctx):
    s1 = FNET_W
    s2 = s1 + SSD_INNER
    s3 = s2 + SSD_CONV_DIM
    fc, zc, xbcc, dtc = jnp.split(uc @ w_in, [s1, s2, s3], axis=-1)
    fl, zl, xbcl, dtl = jnp.split(ul @ w_in, [s1, s2, s3], axis=-1)
    a = -jnp.exp(a_log.astype(jnp.float32)).reshape(2, SSD_GROUPS, SSD_HPG)
    dtb = dt_bias.astype(jnp.float32).reshape(2, SSD_GROUPS, SSD_HPG)
    dsk = d_skip.astype(jnp.float32).reshape(SSD_GROUPS, SSD_HPG)
    xs_c, b_c, c_c, dt_c = ssd_inputs(xbcc, dtc, conv_w, conv_b, dtb)
    xs_l, b_l, c_l, dt_l = ssd_inputs(xbcl, dtl, conv_w, conv_b, dtb)
    h0 = jnp.zeros((uc.shape[0], SSD_GROUPS, SSD_HPG, SSD_HEAD_DIM, SSD_STATE), jnp.float32)
    y_c, h_f, h_b = bidir_ssd(xs_c, b_c, c_c, dt_c, a, h0, h0)
    y_l, _, _ = bidir_ssd(xs_l, b_l, c_l, dt_l, a, h_f, h_b)
    ol = jnp.concatenate([fourier_mix(fl), ssd_output(y_l, xs_l, zl, dsk, ssd_norm_g)], axis=-1) @ w_out
    oc = None
    if need_ctx:
        oc = jnp.concatenate([fourier_mix(fc), ssd_output(y_c, xs_c, zc, dsk, ssd_norm_g)], axis=-1) @ w_out
    return oc, ol

def context_attention(qc, kc, vc, sink):
    b, n = qc.shape[:2]
    s = jnp.einsum("bqhgd,bkhd->bhgqk", qc, kc).astype(jnp.float32) * (HEAD_DIM ** -0.5)
    if sink is not None:
        s_sink = jnp.broadcast_to(sink.astype(jnp.float32)[None, :, :, None, None], s.shape[:-1] + (1,))
        s = jnp.concatenate([s, s_sink], axis=-1)
    p = jax.nn.softmax(s, axis=-1)[..., :kc.shape[1]]
    o = jnp.einsum("bhgqk,bkhd->bqhgd", p.astype(vc.dtype), vc)
    return o.reshape(b, n, -1)

def window_attention(q, k, v, kc, vc, sink):
    b, l = q.shape[:2]
    nb = l // WIN_BLOCK
    n_ctx = kc.shape[1]
    qb = q.reshape(b, nb, WIN_BLOCK, WIN_KV_HEADS, WIN_GQA, HEAD_DIM)

    def band(t):
        tb = jnp.pad(t.reshape(b, nb, WIN_BLOCK, WIN_KV_HEADS, HEAD_DIM), ((0, 0), (1, 1), (0, 0), (0, 0), (0, 0)))
        return jnp.concatenate([tb[:, :-2], tb[:, 1:-1], tb[:, 2:]], axis=2)

    kb, vb = band(k), band(v)
    scale = HEAD_DIM ** -0.5
    s_loc = jnp.einsum("bnqhgd,bnshd->bnhgqs", qb, kb).astype(jnp.float32) * scale
    qpos = jnp.arange(nb)[:, None] * WIN_BLOCK + jnp.arange(WIN_BLOCK)[None]
    kpos = (jnp.arange(nb)[:, None] - 1) * WIN_BLOCK + jnp.arange(3 * WIN_BLOCK)[None]
    valid = ((jnp.abs(qpos[:, :, None] - kpos[:, None, :]) <= WIN_RADIUS)
             & (kpos[:, None, :] >= 0) & (kpos[:, None, :] < l))
    s_loc = jnp.where(valid[None, :, None, None], s_loc, NEG_INF)
    s_ctx = jnp.einsum("bnqhgd,bchd->bnhgqc", qb, kc).astype(jnp.float32) * scale
    s_sink = jnp.broadcast_to(sink.astype(jnp.float32).reshape(WIN_KV_HEADS, WIN_GQA)[None, None, :, :, None, None],
                              s_loc.shape[:-1] + (1,))
    p = jax.nn.softmax(jnp.concatenate([s_loc, s_ctx, s_sink], axis=-1), axis=-1)
    p_loc = p[..., :3 * WIN_BLOCK].astype(v.dtype)
    p_ctx = p[..., 3 * WIN_BLOCK:3 * WIN_BLOCK + n_ctx].astype(v.dtype)
    o = jnp.einsum("bnhgqs,bnshd->bnqhgd", p_loc, vb) + jnp.einsum("bnhgqc,bchd->bnqhgd", p_ctx, vc)
    return o.reshape(b, l, WIN_Q_HEADS * HEAD_DIM)

def neighbourhood_attention(q, k, v, kc, vc, rpb):
    b, l, h, dh = q.shape
    rows = l // GRID_W
    kr = min(NA_ROWS, rows)
    r = jnp.arange(rows)
    row_idx = jnp.clip(r - kr // 2, 0, rows - kr)[:, None] + jnp.arange(kr)[None]
    cols = jnp.arange(GRID_W)
    col_start = jnp.clip(cols - NA_COLS // 2, 0, GRID_W - NA_COLS)
    col_ok = (cols[None] >= col_start[:, None]) & (cols[None] < col_start[:, None] + NA_COLS)
    qg = q.reshape(b, rows, GRID_W, h, dh)
    kg = k.reshape(b, rows, GRID_W, h, dh)[:, row_idx]
    vg = v.reshape(b, rows, GRID_W, h, dh)[:, row_idx]
    scale = HEAD_DIM ** -0.5
    s_loc = jnp.einsum("brwhd,brkuhd->bhrwku", qg, kg).astype(jnp.float32) * scale
    row_off = row_idx - r[:, None] + (NA_ROWS - 1)
    col_off = jnp.clip(cols[None] - cols[:, None] + (NA_COLS - 1), 0, 2 * NA_COLS - 2)
    bias = rpb.astype(jnp.float32)[:, row_off[:, None, :, None], col_off[None, :, None, :]]
    s_loc = jnp.where(col_ok[:, None, :], s_loc + bias[None], NEG_INF)
    s_ctx = jnp.einsum("brwhd,bchd->bhrwc", qg, kc).astype(jnp.float32) * scale
    n_loc = kr * GRID_W
    p = jax.nn.softmax(jnp.concatenate([s_loc.reshape(b, h, rows, GRID_W, n_loc), s_ctx], axis=-1), axis=-1)
    p_loc = p[..., :n_loc].reshape(b, h, rows, GRID_W, kr, GRID_W).astype(v.dtype)
    p_ctx = p[..., n_loc:].astype(v.dtype)
    o = jnp.einsum("bhrwku,brkuhd->brwhd", p_loc, vg) + jnp.einsum("bhrwc,bchd->brwhd", p_ctx, vc)
    return o.reshape(b, l, h * dh)

def odd_mixer(uc, ul, w_in, q_norm_win, k_norm_win, sink_win, q_norm_na, k_norm_na, rpb_na, w_out, cos, sin, need_ctx):
    wq = WIN_Q_HEADS * HEAD_DIM
    wk = WIN_KV_HEADS * HEAD_DIM
    nh = NA_HEADS * HEAD_DIM
    splits = [wq, wq + wk, wq + 2 * wk, wq + 2 * wk + nh, wq + 2 * wk + 2 * nh]

    def heads(p):
        b, l = p.shape[:2]
        qw, kw, vw, qn, kn, vn = jnp.split(p, splits, axis=-1)
        qw = rms_norm(qw.reshape(b, l, WIN_Q_HEADS, HEAD_DIM), q_norm_win)
        kw = rms_norm(kw.reshape(b, l, WIN_KV_HEADS, HEAD_DIM), k_norm_win)
        vw = vw.reshape(b, l, WIN_KV_HEADS, HEAD_DIM)
        qn = rms_norm(qn.reshape(b, l, NA_HEADS, HEAD_DIM), q_norm_na)
        kn = rms_norm(kn.reshape(b, l, NA_HEADS, HEAD_DIM), k_norm_na)
        vn = vn.reshape(b, l, NA_HEADS, HEAD_DIM)
        return qw, kw, vw, qn, kn, vn

    qwc, kwc, vwc, qnc, knc, vnc = heads(uc @ w_in)
    qwl, kwl, vwl, qnl, knl, vnl = heads(ul @ w_in)
    qwl = apply_axial_rope(qwl, cos, sin)
    kwl = apply_axial_rope(kwl, cos, sin)
    ol = jnp.concatenate([window_attention(qwl, kwl, vwl, kwc, vwc, sink_win),
                          neighbourhood_attention(qnl, knl, vnl, knc, vnc, rpb_na)], axis=-1) @ w_out
    oc = None
    if need_ctx:
        b, n = uc.shape[:2]
        oc = jnp.concatenate([
            context_attention(qwc.reshape(b, n, WIN_KV_HEADS, WIN_GQA, HEAD_DIM), kwc, vwc,
                              sink_win.reshape(WIN_KV_HEADS, WIN_GQA)),
            context_attention(qnc.reshape(b, n, NA_HEADS, 1, HEAD_DIM), knc, vnc, None)], axis=-1) @ w_out
    return oc, ol

def setup_inputs(seed: int = 0) -> dict:
    key = jax.random.key(seed)
    ks = jax.random.split(key, 32)
    f32 = jnp.float32
    D = D_MODEL

    def nrm(k, shape, s):
        return jax.random.normal(k, shape, f32) * s

    dt0 = jnp.exp(jax.random.uniform(ks[14], (N_EVEN, 2, SSD_HEADS), f32, math.log(1e-3), math.log(1e-1)))
    return {
        "x": nrm(ks[0], (BATCH, SEQ, D), 1.0),
        "c": nrm(ks[1], (BATCH, D), 1.0),
        "ctx": nrm(ks[2], (BATCH, CTX_LEN, D), 1.0),
        "c_ctx": nrm(ks[3], (D,), 1.0),
        "w_mod": nrm(ks[4], (DEPTH, D, 6 * D), 0.5 * D ** -0.5),
        "b_mod": nrm(ks[5], (DEPTH, 6 * D), 0.01),
        "norm_mix_g": 1.0 + nrm(ks[6], (DEPTH, D), 0.02),
        "norm_ff_g": 1.0 + nrm(ks[7], (DEPTH, D), 0.02),
        "w_ff1": nrm(ks[8], (DEPTH, D, D_FF), D ** -0.5),
        "w_ff2": nrm(ks[9], (DEPTH, D_FF, D), D_FF ** -0.5),
        "w_in_even": nrm(ks[10], (N_EVEN, D, EVEN_IN), D ** -0.5),
        "conv_w": nrm(ks[11], (N_EVEN, SSD_CONV_W, SSD_CONV_DIM), SSD_CONV_W ** -0.5),
        "conv_b": nrm(ks[12], (N_EVEN, SSD_CONV_DIM), 0.01),
        "dt_bias": dt0 + jnp.log(-jnp.expm1(-dt0)),
        "a_log": jnp.log(jax.random.uniform(ks[15], (N_EVEN, 2, SSD_HEADS), f32, 1.0, 16.0)),
        "d_skip": 1.0 + nrm(ks[16], (N_EVEN, SSD_HEADS), 0.02),
        "ssd_norm_g": 1.0 + nrm(ks[17], (N_EVEN, SSD_INNER), 0.02),
        "w_out_even": nrm(ks[18], (N_EVEN, EVEN_MIX, D), EVEN_MIX ** -0.5),
        "w_in_odd": nrm(ks[19], (N_ODD, D, ODD_IN), D ** -0.5),
        "q_norm_win": 1.0 + nrm(ks[20], (N_ODD, HEAD_DIM), 0.02),
        "k_norm_win": 1.0 + nrm(ks[21], (N_ODD, HEAD_DIM), 0.02),
        "sink_win": nrm(ks[22], (N_ODD, WIN_Q_HEADS), 0.5),
        "q_norm_na": 1.0 + nrm(ks[23], (N_ODD, HEAD_DIM), 0.02),
        "k_norm_na": 1.0 + nrm(ks[24], (N_ODD, HEAD_DIM), 0.02),
        "rpb_na": nrm(ks[25], (N_ODD, NA_HEADS, 2 * NA_ROWS - 1, 2 * NA_COLS - 1), 0.02),
        "w_out_odd": nrm(ks[26], (N_ODD, ODD_MIX, D), ODD_MIX ** -0.5),
    }

def reference(x, c, ctx, c_ctx, w_mod, b_mod, norm_mix_g, norm_ff_g, w_ff1, w_ff2,
              w_in_even, conv_w, conv_b, dt_bias, a_log, d_skip, ssd_norm_g, w_out_even,
              w_in_odd, q_norm_win, k_norm_win, sink_win, q_norm_na, k_norm_na, rpb_na, w_out_odd):
    hl, hc = x, ctx
    cos, sin = axial_rope_tables(x.shape[1])
    silu_c = jax.nn.silu(c)
    silu_cc = jax.nn.silu(c_ctx)
    for i in range(DEPTH):
        need_ctx = i < DEPTH - 1
        mod_l = (silu_c @ w_mod[i] + b_mod[i])[:, None, :]
        mod_c = (silu_cc @ w_mod[i] + b_mod[i])[None, None, :]
        sh1_l, sc1_l, g1_l, sh2_l, sc2_l, g2_l = jnp.split(mod_l, 6, axis=-1)
        sh1_c, sc1_c, g1_c, sh2_c, sc2_c, g2_c = jnp.split(mod_c, 6, axis=-1)
        ul = modulate(rms_norm(hl, norm_mix_g[i]), sh1_l, sc1_l)
        uc = modulate(rms_norm(hc, norm_mix_g[i]), sh1_c, sc1_c)
        if i % 2 == 0:
            j = i // 2
            oc, ol = even_mixer(uc, ul, w_in_even[j], conv_w[j], conv_b[j], dt_bias[j], a_log[j],
                                d_skip[j], ssd_norm_g[j], w_out_even[j], need_ctx)
        else:
            j = i // 2
            oc, ol = odd_mixer(uc, ul, w_in_odd[j], q_norm_win[j], k_norm_win[j], sink_win[j],
                               q_norm_na[j], k_norm_na[j], rpb_na[j], w_out_odd[j], cos, sin, need_ctx)
        hl = hl + g1_l * ol
        hl = hl + g2_l * sq_relu_mlp(modulate(rms_norm(hl, norm_ff_g[i]), sh2_l, sc2_l), w_ff1[i], w_ff2[i])
        if need_ctx:
            hc = hc + g1_c * oc
            hc = hc + g2_c * sq_relu_mlp(modulate(rms_norm(hc, norm_ff_g[i]), sh2_c, sc2_c), w_ff1[i], w_ff2[i])
    return hl


_drawn_inputs = setup_inputs


def setup_inputs(seed=0):
    import zlib

    import numpy as np

    out = dict(_drawn_inputs(seed))
    spreads = {}
    factors = {'norm_mix_g': 7.014,
     'norm_ff_g': 4.619,
     'conv_b': 8.0,
     'd_skip': 64.0,
     'ssd_norm_g': 8.0,
     'q_norm_win': 24.086,
     'k_norm_win': 24.601,
     'sink_win': 8.0,
     'q_norm_na': 23.526,
     'k_norm_na': 8.0,
     'rpb_na': 64.0}
    for name, (base, spread) in spreads.items():
        noise = np.random.default_rng([zlib.crc32(name.encode()), seed]).standard_normal(out[name].shape)
        drawn = base * np.exp(spread * noise) if base else spread * noise
        out[name] = __import__('jax').numpy.asarray(drawn.astype(out[name].dtype))
    for name, factor in factors.items():
        out[name] = (out[name] * factor).astype(out[name].dtype)
    return out
```

```python
import math
from contextlib import ExitStack

import concourse.bass as bass
from concourse import mybir
import numpy as np

ALU = mybir.AluOpType
ACT = mybir.ActivationFunctionType
AX = mybir.AxisListType.X
F32 = mybir.dt.float32
F32R = mybir.dt.float32r

P = 128
D = 1024
SEQ = 256
CTX = 256
T = SEQ + CTX
NCH = T // P
KT = D // P
NMOD = 6 * KT
D_FF = 4 * D
EPS = 1e-6
NEG = -1e30
GRID_W = 64

FN_W = 512
FN_T = FN_W // P
G = 4
R = 6
HD = 64
GX = R * HD
XT = GX // P
NS = 128
NH = G * R
INNER = NH * HD
COL_Z = FN_W
COL_X = COL_Z + INNER
COL_B = COL_X + INNER
COL_C = COL_B + G * NS
COL_DT = COL_C + G * NS
CONV_T = (INNER + 2 * G * NS) // P
CONV_W = 5
PADW = SEQ + CONV_W - 1

RAW = 4
SPLIT = 2
MODS_FIRST = 2 * KT
MODS_LOOP = NMOD // 4
FF_CHUNKS = D_FF // D

B_GEMM = (0, 1)
B_TR = 2
B_AUX = (3, 7)
B_SEG = 4
B_Y = 6

SCAN_F = (2, 3, 0, 1)
SCAN_B = (3, 2, 1, 0)
STATES = [("f", 2), ("b", 3), ("f", 3), ("b", 2), ("f", 0), ("b", 1)]

NQ = 16
NKH = 10
ODD = ([("qn", i, 768 + P * i, SEQ) for i in range(4)] + [("kn", i, 1280 + P * i, T) for i in range(4)]
       + [("qw", i, P * i, SEQ) for i in range(4)] + [("kw", 0, 512, T)]
       + [("v", 0, 640, T)] + [("v", 1 + i, 1792 + P * i, T) for i in range(4)])


def constants():
    j = np.arange(P)[:, None].astype(np.float64)
    i = np.arange(P)[None, :].astype(np.float64)
    ident = (j == i)
    tri = [j <= i, j >= i, j > i, j < i]
    ones = np.ones((P, P))
    w = np.arange(64)
    ang = 2 * np.pi * np.outer(w, w) / 64
    norm = 1.0 / math.sqrt(SEQ * 64)
    dftw = np.zeros((P, 2 * P))
    for b in range(2):
        dftw[64 * b:64 * b + 64, 64 * b:64 * b + 64] = np.cos(ang) * norm
        dftw[64 * b:64 * b + 64, P + 64 * b:P + 64 * b + 64] = np.sin(ang) * norm
    t = np.arange(SEQ)
    angl = 2 * np.pi * (np.outer(t, t) % SEQ) / SEQ
    dfts = np.zeros((P, 2, 2, SEQ))
    for k in range(2):
        dfts[:, k, 0] = np.cos(angl)[k * P:(k + 1) * P]
        dfts[:, k, 1] = -np.sin(angl)[k * P:(k + 1) * P]
    c0 = np.concatenate([ident] + tri + [ones, dftw, dfts.reshape(P, -1)], axis=1).astype(np.float32)
    f = (10000.0 ** (-np.arange(16, dtype=np.float32) / 16)).astype(np.float32)
    pos = np.arange(SEQ)
    row, col = (pos // GRID_W).astype(np.float32), (pos % GRID_W).astype(np.float32)
    cos = np.zeros((P, SEQ)); sin = np.zeros((P, SEQ)); perm = np.zeros((P, P))
    for p in range(P):
        d = p % 64
        axis, half, n = d // 32, (d % 32) // 16, d % 16
        a = ((row, col)[axis] * f[n]).astype(np.float32)
        cos[p] = np.cos(a)
        sin[p] = np.sin(a) * (-1 if half == 0 else 1)
        perm[p + (16 if half == 0 else -16), p] = 1.0
    dup = np.zeros((2, P, P))
    for p in range(P):
        dup[0, p % 64, p] = 1.0
        dup[1, 64 + p % 64, p] = 1.0
    half = np.zeros((P, 2)); half[:64, 0] = 1; half[64:, 1] = 1
    selq = np.zeros((P, 8 * P)); selk = np.zeros((P, 5 * P))
    for tt in range(8):
        for p in range(P):
            selq[2 * tt + p // 64, tt * P + p] = 1
    for tt in range(5):
        for p in range(P):
            selk[2 * tt + p // 64, tt * P + p] = 1
    qq, kk = np.arange(P)[:, None], np.arange(P)[None, :]
    win = np.stack([np.where(kk <= qq, 0, NEG), np.where(kk >= qq, 0, NEG)], 1)
    cs = np.clip((63 - qq % 64) - 8, 0, 64 - 16)
    flip = (j // 64 == i // 64) & (j % 64 == 63 - i % 64)
    u = np.arange(SEQ)[None, :] % 64
    nam = np.where((u >= cs) & (u < cs + 16), 0, NEG)
    c1 = np.concatenate([cos, sin, perm, dup[0], dup[1], half, selq, selk,
                         win.reshape(P, -1), nam, flip], axis=1).astype(np.float32)
    return c0, c1


ATTN = [(t, par, qt) for t in range(8) for par in range(2) for qt in range(2)]

N_HEADS = 2 * NQ + NCH * NKH
N_VEC = 20
C0_W = 6 * P + 2 * P + 4 * SEQ
C1_W = 2 * SEQ + 3 * P + 2 + 13 * P + 2 * P + SEQ + P


def script():
    s = [("vecs",), ("mods", 0, 0, MODS_FIRST), ("xin",), ("norm", 0, "mix"), ("dt",)]
    pending = []

    def silu():
        while pending:
            s.append(("silu", pending.pop()))

    def gemm(kind, i):
        silu()
        s.append(("gemm", kind, i))
        if kind == "conv":
            pending.append(i)

    rest = list(range(MODS_FIRST, NMOD))
    dft = {1: [("dftw", 0)], 2: [("dfts", 0), ("dftw", 1)], 3: [("dfts", 1), ("dftw", 2)],
           4: [("dfts", 2), ("dftw", 3)], 5: [("dfts", 3)]}
    for n, (kind, t) in enumerate([("fn", t) for t in range(FN_T)] + [("conv", t) for t in conv_tiles(0)]):
        gemm(kind, t)
        if n < 8:
            s.append(("mods", 0, rest[4 * n], rest[4 * n] + 4))
        s.extend(dft.get(n, []))
    for g in range(G):
        fill = [("z", XT * g + i) for i in range(XT)]
        fill += [("conv", t) for t in conv_tiles(g + 1)] if g < G - 1 else [("outA", m) for m in range(KT)]
        fill = fill[::-1]

        def some():
            if fill:
                if fill[-1] == ("outA", 0):
                    s.append(("mixsplit", 0))
                gemm(*fill.pop())
        silu()
        for ch in SCAN_F:
            s.append(("toks", g, ch))
        if g:
            s.append(("ysum", g - 1))
        for d, ch in STATES:
            s.append(("state", g, d, ch))
        if g:
            s.append(("ynorm", g - 1))
        for n, ch in enumerate(SCAN_F):
            s.append(("cb", g, ch))
            s.append(("seg", g, "f", ch))
            some()
            if n:
                s.append(("yt", g, SCAN_F[n - 1]))
            s.append(("seg", g, "b", ch))
            some()
            s.append(("y", g, ch))
        s.append(("yt", g, SCAN_F[-1]))
        s.append(("ygate", g))
        if g == G - 1:
            some()
            s.append(("ysum", g))
            some()
            s.append(("ynorm", g))
        while fill:
            some()
    s.append(("mixsplit", 1))
    for m in range(KT):
        gemm("outB", m)
    s += [("norm", 0, "ff"), ("mlp", 0), ("norm", 1, "mix")]
    for n, (kind, i, _, _) in enumerate(ODD):
        gemm(kind, i)
        if n >= 1 and ODD[n - 1][0] != "v":
            s.append(("hstat",) + ODD[n - 1][:2])
        if n == 13:
            s.append(("hvar",))
        if n == 14:
            s.append(("htr",))
        if n >= 14:
            s.append(("vtok", ODD[n - 1][1]))
    s.append(("vtok", 4))
    hn = [o[:2] for o in ODD if o[0] != "v"]
    hn = hn[8:] + hn[:8]
    for n, o in enumerate(hn):
        s.append(("hnorm",) + o)
        if n and hn[n - 1][0][1] == "w":
            s.append(("rot",) + hn[n - 1])
    s.append(("dup",))
    s.append(("attn0",))
    n = len(ATTN)
    for j in range(-2, n + 1):
        for kind, i in (("S", j + 2), ("exp", j + 1), ("scale", j), ("PT", j), ("O", j - 1)):
            if 0 <= i < n:
                s.append((kind, i))
                if kind == "O" and i % 4 == 3:
                    s.append(("osplit", i // 4))
    for m in range(KT):
        gemm("outO", m)
    s += [("norm", 1, "ff"), ("mlp", 1), ("out",)]
    return s


def mlp_plan(layer):
    g = [("ff1", m) for m in range(KT)] + [("ff2", m) for m in range(KT)]
    plan = []
    for n, q in enumerate(g):
        plan.append(q)
        if layer == 0 and n < MODS_LOOP:
            plan.append(("mod", n))
    return plan


def conv_tiles(g):
    return [12 + g, 16 + g] + [XT * g + i for i in range(XT)]


def trunk(nc, x, c, ctx, c_ctx, w_mod, b_mod, norm_mix_g, norm_ff_g, w_ff1, w_ff2, w_in_even, conv_w,
          conv_b, dt_bias, a_log, d_skip, ssd_norm_g, w_out_even, w_in_odd, q_norm_win, k_norm_win,
          sink_win, q_norm_na, k_norm_na, rpb_na, w_out_odd, consts0, consts1, out):
    steps = script()

    def tile_of(w, row, col):
        return w[bass.ds(row, D), bass.ds(col, P)].rearrange("(k p) n -> p k n", p=P)

    def source(kind, i):
        if kind == "fn":
            return tile_of(w_in_even[0], 0, P * i)
        if kind == "z":
            return tile_of(w_in_even[0], 0, COL_Z + P * i)
        if kind == "conv":
            return tile_of(w_in_even[0], 0, COL_X + P * i)
        if kind in ("outA", "outB"):
            return tile_of(w_out_even[0], D * (kind == "outB"), P * i)
        if kind == "outO":
            return tile_of(w_out_odd[0], 0, P * i)
        return tile_of(w_in_odd[0], 0, {o[:2]: o[2] for o in ODD}[(kind, i)])

    after = {}
    unit, gnum, jobs, filled_by, freed_by, free_before = {}, {}, {}, {}, {}, {}
    n_unit = n_gemm = n_aux = n_mod = n_sq = n_var = n_h = n_mix = 0
    seen = {}
    in_full = {b: 0 for b in range(8)}
    in_free = {b: 0 for b in range(8)}
    last = {}
    used_by = {b: 0 for b in B_GEMM}
    slot_full = {}

    def job(key, bank, freed=None, filled=None, n=1):
        if not filled:
            in_full[bank] += n
        if not freed:
            in_free[bank] += n
        jobs[key] = (bank, in_full[bank] - n + 1)
        filled_by[key] = filled or (f"full{bank}", jobs[key][1])
        freed_by[key] = freed or (f"free{bank}", in_free[bank])
        free_before[key] = last.get(bank)
        last[bank] = freed_by[key]

    for st in steps:
        k = st[0]
        nk = seen[k] = seen.get(k, 0) + 1
        if k == "mods":
            n_mod += st[3] - st[2]
            job(st, B_AUX[1], filled=("mod_used", n_mod))
            for f in range(st[2], st[3]):
                unit[("mod", st[1], f)] = n_unit
                n_unit += 1
        elif k == "gemm":
            unit[st], gnum[st] = n_unit, n_gemm
            kind = {"fn": "uf_done", "conv": "pad_done", "z": "gate_done", "v": "vT_done"}.get(st[1])
            if kind:
                nk = seen[kind] = seen.get(kind, 0) + 1
            elif st[1][:3] == "out":
                kind, nk = "h_done", n_h + 1
                n_h += 1
            else:
                kind, nk = "sq_done", n_sq + 1
                n_sq += 1
            b = B_GEMM[n_gemm % 2]
            job(st, b, freed=(kind, nk))
            slot_full[st] = used_by[b]
            used_by[b] = jobs[st][1]
            n_unit += 1
            n_gemm += 1
        elif k == "mlp":
            unit[st], gnum[st] = n_unit, n_gemm
            assert n_gemm % 2 == 0
            n_h += FF_CHUNKS * KT
            for i, b in enumerate(B_GEMM):
                job(st + (b,), b, freed=("h_done", n_h - 1 + i), n=FF_CHUNKS * KT)
                if i == 0:
                    slot_full[st] = used_by[b]
                used_by[b] = in_full[b]
            if st[1] == 0:
                job(st + ("mods",), B_AUX[1], filled=("mod_used", n_mod), n=FF_CHUNKS)
                n_unit += NMOD
                n_mod += NMOD
            n_unit += FF_CHUNKS * 2 * KT
            n_gemm += FF_CHUNKS * 2 * KT
        elif k == "vecs":
            for q in range(4):
                job(st + (q,), B_TR, freed=("vt_done", 4) if q == 3 else None)
        elif k == "xin":
            for q in range(KT):
                n_h += 1
                job(st + (q,), B_TR, freed=("h_done", n_h))
        elif k == "norm":
            n_sq += KT
            n_var += 1
            job(st + ("sum",), B_AUX[0], freed=("var_done", n_var), filled=("sq_used", n_sq))
            job(st + ("bc",), B_TR, freed=("nt_done", KT * nk))
        elif k == "dt":
            job(st + ("raw",), B_AUX[0], freed=("dtv_done", 1))
            job(st + ("cum",), B_AUX[0], freed=("dtx_done", 2))
            job(st + ("tot",), B_AUX[0], freed=("dtx_done", 3))
        elif k == "dftw":
            for q in range(2):
                job(st + (q,), B_AUX[0], freed=("vf_done", 2 * st[1] + q + 1))
        elif k == "dfts":
            n_mix += 1
            job(st, B_TR, freed=("mix_done", n_mix))
        elif k == "toks":
            job(st, B_TR, freed=("xdt_done", nk))
        elif k == "yt":
            job(st, B_TR)
        elif k == "ynorm":
            n_mix += XT
            job(st, B_TR, freed=("mix_done", n_mix))
        elif k == "vtok":
            job(st, B_TR, freed=("vtok_done", nk))
        elif k in ("state", "cb", "ysum", "hnorm"):
            n_var += k == "ysum"
            job(st, B_AUX[n_aux % 2], freed={"state": ("ent_done", nk), "ysum": ("var_done", n_var),
                                             "hnorm": ("qn_done", nk)}.get(k))
            n_aux += 1
        elif k == "seg":
            job(st, B_SEG, freed=("seg_done", nk))
        elif k == "y":
            job(st + ("d",), B_Y, freed=("y_done", nk))
            for q, none in (("f", SCAN_F[0]), ("b", SCAN_B[0])):
                if st[2] != none:
                    job(st + (q,), B_AUX[n_aux % 2])
                    n_aux += 1
        elif k == "hstat" and nk == 1:
            job("hstat", B_AUX[0], freed=("var_done", n_var + 1), filled=("sq_used", n_sq + 2 * KT - 4))
        elif k == "hvar":
            n_aux = 0
            n_var += 1
            filled_by["hstat"] = ("sq_used", n_sq)
        elif k == "htr":
            job(st + ("q",), B_TR, freed=("rT_done", 1))
            job(st + ("k",), B_TR, freed=("rT_done", 2))
        elif k == "rot":
            job(st, B_Y)
        elif k == "dup":
            job(st + (0,), B_TR, freed=("kd_done", 1))
            job(st + (1,), B_TR, freed=("kd_done", 2))
        elif k == "S":
            job(st, B_GEMM[st[1] % 2])
        elif k == "PT":
            job(st, B_AUX[0] if st[1] % 2 else B_SEG, freed=("pT_done", st[1] + 1))
        elif k == "O" and st[1] % 4 == 0:
            t = st[1] // 4
            job(("Opair", t), (B_Y, B_AUX[1])[t % 2], freed=("split_done", 5 * KT + t + 1), filled=("pv_done", 4 * t + 4))
        elif k == "out":
            for q in range(4):
                job(st + (q,), (B_TR, B_Y)[q % 2], freed=(("finv_done", "fin_done")[q % 2], q // 2 + 1))
    steps_of = lambda kind: [q for q in steps if q[0] == kind]
    gemms = steps_of("gemm")
    order = [q for q in steps if q[0] in ("gemm", "mlp")]
    after = dict(zip(order, order[1:]))
    with ExitStack() as stack:
        at = [16512]

        def place(name, shape, dt=F32, offset=None):
            size = 4 * int(np.prod(shape[1:]))
            if offset is None:
                offset = at[0]
                at[0] += (size + 31) // 32 * 32
            assert offset + size <= 229344, (name, offset, size)
            return nc.alloc_sbuf_tensor_at(name, shape, dt, offset=offset)

        hT = place("hT", [P, KT, T])
        a_hi = place("a_hi", [P, KT, T], F32R)
        a_lo = place("a_lo", [P, KT, T], F32R)
        raw = place("raw", [P, RAW, KT, P])
        w_hi = place("w_hi", [P, SPLIT, KT, P], F32R)
        w_lo = place("w_lo", [P, SPLIT, KT, P], F32R)
        c0 = place("c0", [P, C0_W])
        vt = place("vt", [P, 3, P])
        bc = place("bc", [P, P])
        mod = place("mod", [P, 2, NMOD, 2])
        coefA = place("coefA", [P, KT, 2])
        silc = place("silc", [P, KT, 2])
        dsk = place("dsk", [P, NH // 2])
        nega = place("nega", [P, 2 * NH])
        var = place("var", [P, 128])
        rstd = place("rstd", [P, 128])
        mhalf = place("mhalf", [P, 128])
        out_at = at[0]
        mixF = place("mixF", [P, 2 * KT, T])
        region = at[0]
        b_hi = place("b_hi", [P, KT, T], F32R)
        b_lo = place("b_lo", [P, KT, T], F32R)
        sq = place("sq", [P, 2, T])
        nt = place("nt", [P, 2, T])
        u32 = place("u32", [P, 2, T])
        hr = place("hr", [P, 2, T])
        hq = place("hq", [P, 2, T])
        top = at[0]
        vrow = place("vrow", [P, 3, P], offset=out_at)
        rowv = place("rowv", [1, P], offset=out_at + 1536)
        sct = place("sct", [P, KT, 2], offset=out_at + 2048)
        xload = place("xload", [P, NCH, D], offset=out_at + 4096)
        at[0] = region
        xbc = place("xbc", [P, 2, 5, T])
        gate = place("gate", [P, XT, T])
        btok = place("btok", [P, NCH, NS])
        xdt = place("xdt", [P, 2, NCH, GX])
        xw = place("xw", [P, 2, GX])
        hent = place("hent", [P, 2, NCH - 1, GX])
        ey = place("ey", [P, 2, R, P])
        rr = place("rr", [P, R, P])
        cbm = place("cbm", [P, 2, P])
        ycomb = place("ycomb", [P, 2, GX])
        cpad = place("cpad", [P, 2, 2, PADW])
        cacc = place("cacc", [P, 2, T])
        cth = place("cth", [P, T])
        dts = {n: place("dt_" + n, [P, NCH, 2 * NH]) for n in ("dt", "dta", "ea", "dte", "tot")}
        zt = place("zt", [P, T])
        o = out_at + 4096 + 4 * NCH * D
        wdt = place("wdt", [P, KT, 2 * NH], offset=o)
        wdt_hi = place("wdt_hi", [P, KT, 2 * NH], F32R, offset=o + 1536)
        wdt_lo = place("wdt_lo", [P, KT, 2 * NH], F32R, offset=o + 3072)
        dts["tmp"] = place("dt_tmp", [P, NCH, 2 * NH], offset=o + 4608)
        dts["t2"] = place("dt_t2", [P, NCH, 2 * NH], offset=o + 5376)
        dts["t3"] = place("dt_t3", [P, NCH, 2 * NH], offset=o + 6144)
        o = region + 2 * 5 * T * 4 + XT * T * 4 + NCH * NS * 4
        uf = place("uf", [P, 2, T], offset=o)
        vf = place("vf", [P, NCH, 2 * P], offset=o + 4096)
        at[0] = out_at
        c1 = place("c1", [P, C1_W])
        qT = place("qT", [P, 8, SEQ])
        kT = place("kT", [P, 5, T])
        kdup = place("kdup", [P, 2, T])
        vtok = place("vtok", [P, NCH, 5 * P])
        at[0] = max(at[0], region + 2 * 16384)
        at[0] = max(at[0], top)
        vT = place("vT", [P, T])
        rT = place("rT", [NQ, SEQ])
        rTk = place("rTk", [NKH, T])
        rp = place("rp", [P, 2, SEQ])
        sm = place("sm", [P, 8, 2])
        bias = place("bias", [P, 2, 8, SEQ], offset=region + 16384)
        prob = place("prob", [P, 2, T], offset=region + 32768 + 4096)
        pT = place("pT", [P, 2, T], offset=region + 32768 + 8192)
        fin = place("fin", [P, 2, D], offset=out_at)

        ident, tle, tge, tgt, tlt, ones = (c0[:, P * i:P * i + P] for i in range(6))
        dftw = c0[:, 6 * P:8 * P]
        dfts = c0[:, 8 * P:8 * P + 4 * SEQ].rearrange("p (k c l) -> p k c l", k=2, c=2)
        cw = 0
        cuts = {}
        for name, w in (("cos", SEQ), ("sin", SEQ), ("perm", P), ("dup0", P), ("dup1", P), ("half", 2),
                        ("selq", 8 * P), ("selk", 5 * P), ("win", 2 * P), ("nam", SEQ), ("flip", P)):
            cuts[name] = c1[:, cw:cw + w]
            cw += w
        bmod1 = vt[:, 0, NMOD:2 * NMOD]
        bmodT = vt[:, 0, 0:2 * NMOD].rearrange("p (l f) -> p l f", l=2)
        gmixT = vt[:, 0, 96:112].rearrange("p (l f) -> p l f", l=2)
        gffT = vt[:, 0, 112:128].rearrange("p (l f) -> p l f", l=2)
        convwT = vt[:, 1, 0:100].rearrange("p (k t) -> p k t", k=CONV_W)
        convbT = vt[:, 1, 100:120]
        gssdT = vt[:, 2, 0:12]
        g_q = {"qw": 28, "kw": 29, "qn": 30, "kn": 31}

        ps = stack.enter_context(nc.psum_tensor("ps", [P, 8, 512], F32))
        sem = lambda n: stack.enter_context(nc.semaphore(n))
        bank_full = [sem(f"bank_full{b}") for b in range(8)]
        bank_free = [sem(f"bank_free{b}") for b in range(8)]
        raw_in = [sem(f"raw_in{i}") for i in range(RAW)]

        names = ("mod_used hi_done lo_done c0_in c1_in vec_in wdt_in bias_in dve_seq act_seq pool_seq consts_set vt_done "
                 "silc_done th0_done h_done sq_done sq_used var_done rstd_done nt_done u_done split_done coef_done "
                 "wdthi_done wdtlo_done dtv_done dte_done dtln_done dt_done dtx_done uf_done vf_done pad_done acc_done "
                 "th_done xbc_done xdt_done xw_done ent_done rr_done seg_done g_done y_done zt_done gate_done gated "
                 "ysq_done mix_done mixhi_done hr_done hq_done hidhi_done hid_done qraw_done rT_done qn_done rope_done "
                 "vT_done vtok_done kd_done bias_done max_done exp_done rs_done prob_done pT_done pv_done ohi_done "
                 "fin_done finv_done out_in").split()
        S = {n: sem(n) for n in names}
        (mod_used, hi_done, lo_done, c0_in, c1_in, vec_in, wdt_in, bias_in, dve_seq, act_seq, pool_seq,
         consts_set, vt_done, silc_done, th0_done, h_done, sq_done, sq_used, var_done, rstd_done, nt_done,
         u_done, split_done, coef_done, wdthi_done, wdtlo_done, dtv_done, dte_done, dtln_done, dt_done, dtx_done,
         uf_done, vf_done, pad_done, acc_done, th_done, xbc_done, xdt_done, xw_done, ent_done, rr_done, seg_done,
         g_done, y_done, zt_done, gate_done, gated, ysq_done, mix_done, mixhi_done, hr_done, hq_done, hidhi_done,
         hid_done, qraw_done, rT_done, qn_done, rope_done, vT_done, vtok_done, kd_done, bias_done, max_done,
         exp_done, rs_done, prob_done, pT_done, pv_done, ohi_done, fin_done, finv_done, out_in) = (S[n] for n in names)
        x_in = [sem(f"x_in{t}") for t in range(NCH)]

        def signalled(what):
            return S[what] if what in S else (bank_full if what[:4] == "full" else bank_free)[int(what[-1])]

        def filled(key):
            what, n = filled_by[key]
            return signalled(what), n

        def emptied(key):
            what, n = free_before[key]
            return signalled(what), n

        def filling(key):
            return bank_full[jobs[key][0]]

        def ledger():
            counts, last_result = {}, []

            def signal(s_):
                counts[s_] = counts.get(s_, 0) + 1
                last_result[:] = [s_, counts[s_]]
                return s_

            def freeing(key):
                what, n = freed_by[key]
                last_result[:] = [signalled(what), n]
                return signalled(what)

            def latest():
                return tuple(last_result)
            return signal, freeing, latest, counts

        odd_tokens = {o[:2]: o[3] for o in ODD}

        def tokens(st):
            return odd_tokens.get(st[1:], SEQ if st[1] == "outO" else T)

        norms = steps_of("norm")
        norm_n = {st: i for i, st in enumerate(norms)}
        h_before = {("norm", 0, "mix"): KT, ("norm", 0, "ff"): 3 * KT,
                    ("norm", 1, "mix"): (3 + FF_CHUNKS) * KT, ("norm", 1, "ff"): (4 + FF_CHUNKS) * KT}
        mlp_h = {0: 3 * KT, 1: (4 + FF_CHUNKS) * KT}
        count = lambda kind, which=None: {q: i for i, q in enumerate([q for q in steps if q[0] == kind and (which is None or q[1] in which)])}
        conv_n, z_n = count("gemm", ("conv",)), count("gemm", ("z",))
        tok_n, seg_n, st_n, y_n = count("toks"), count("seg"), count("state"), count("y")
        seg_l, st_l = steps_of("seg"), steps_of("state")
        qk_n = {q[1:]: i for q, i in count("gemm", ("qn", "kn", "qw", "kw")).items()}
        hn_n, rot_n = count("hnorm"), count("rot")
        cb_n = count("cb")
        dirs = {"f": 0, "b": 1}
        scans = {"f": SCAN_F, "b": SCAN_B}
        split_at = {("norm", 0, "mix"): 0, ("mixsplit", 0): KT, ("mixsplit", 1): 2 * KT,
                    ("norm", 0, "ff"): 3 * KT, ("norm", 1, "mix"): 4 * KT, "attn": 5 * KT, ("norm", 1, "ff"): 6 * KT}
        starts = {("gemm", "fn", 0): 0, ("gemm", "outA", 0): KT, ("gemm", "outB", 0): 2 * KT,
                  ("gemm", ODD[0][0], ODD[0][1]): 4 * KT, ("gemm", "outO", 0): 5 * KT}
        reader = {("mixsplit", 0): ("gemm", "z", G * XT - 1), ("norm", 0, "ff"): ("gemm", "outA", KT - 1),
                  ("norm", 1, "mix"): ("mlp", 0), "attn": ("gemm", "v", 4), ("norm", 1, "ff"): ("gemm", "outO", KT - 1)}

        def readers(st):
            r = reader.get(st)
            if r and r[0] == "mlp":
                return [(bank_full[b], jobs[r + (b,)][1] - 1 + FF_CHUNKS * KT) for b in B_GEMM]
            return [filled(r)] if r else []

        def entering(d, ch):
            i = scans[d].index(ch) - 1
            return None if i < 0 else i

        def y_jobs(g, ch):
            return [("y", g, ch, q) for q in "dfb" if ("y", g, ch, q) in jobs]

        def ktile(kind, i):
            if kind[0] == "q":
                return qT[:, i + 4 * (kind == "qn"), :], i + 4 * (kind == "qn")
            return kT[:, i + (kind == "kn"), :], i + (kind == "kn")

        def first_tile(st):
            return gnum[st], unit[st], slot_full[st]

        heads = lambda ap: ap.rearrange("p (r d) -> p r d", r=R)

        block = stack.enter_context(nc.Block())

        @block.sync
        def _(sp):
            vec = [(vrow[0:96, 0, :], b_mod.rearrange("l (f p) -> (l f) p", p=P)),
                   (vrow[96:112, 0, :], norm_mix_g.rearrange("l (f p) -> (l f) p", p=P)),
                   (vrow[112:128, 0, :], norm_ff_g.rearrange("l (f p) -> (l f) p", p=P)),
                   (vrow[0:100, 1, :], conv_w[0].rearrange("k (t p) -> (k t) p", p=P)),
                   (vrow[100:120, 1, :], conv_b[0].rearrange("(t p) -> t p", p=P)),
                   (vrow[0:12, 2, :], ssd_norm_g[0].rearrange("(t p) -> t p", p=P)),
                   (vrow[12:20, 2, :], c.rearrange("b (t p) -> (b t) p", p=P)),
                   (vrow[20:28, 2, :], c_ctx.rearrange("(t p) -> t p", p=P)),
                   (rowv[:, 0:48], a_log.rearrange("a b c -> a (b c)")),
                   (rowv[:, 48:96], dt_bias.rearrange("a b c -> a (b c)")),
                   (rowv[:, 96:120], d_skip), (rowv[:, 120:128], sink_win)]
            for n, g in enumerate((q_norm_win, k_norm_win, q_norm_na, k_norm_na)):
                vec += [(vrow[28 + n:29 + n, 2, HD * i:HD * i + HD], g) for i in range(2)]
            assert len(vec) == N_VEC
            for dst, src in vec:
                sp.dma_start(dst, src).then_inc(vec_in, 16)
            sp.dma_start(c0[:, :], consts0).then_inc(c0_in, 16)

            def load(u, src, prev):
                if prev is not None:
                    sp.wait_ge(*prev)
                sp.dma_start(raw[:, u % RAW, :, :], src).then_inc(raw_in[u % RAW], 16)

            used = []
            n_mod = 0
            for st in steps:
                if st[0] == "mods":
                    for f in range(st[2], st[3]):
                        u = unit[("mod", st[1], f)]
                        load(u, tile_of(w_mod[st[1]], 0, P * f), used[u - RAW] if u >= RAW else None)
                        n_mod += 1
                        used.append((mod_used, n_mod))
                        if u == RAW - 1:
                            for t in range(NCH):
                                src = (x, ctx)[t // 2][0, P * (t % 2):P * (t % 2) + P, :]
                                sp.dma_start(xload[:, t, :], src).then_inc(x_in[t], 16)
                elif st[0] == "dt":
                    sp.dma_start(wdt[:, :, :], w_in_even[0][:, COL_DT:COL_DT + 2 * NH].rearrange("(k p) n -> p k n", p=P))\
                        .then_inc(wdt_in, 16)
                elif st[0] == "gemm":
                    u = unit[st]
                    load(u, source(st[1], st[2]), used[u - RAW])
                    used.append((lo_done, gnum[st] + 1))
                elif st == ("norm", 0, "ff"):
                    sp.wait_ge(split_done, split_at[("mixsplit", 1)] + KT)
                    sp.dma_start(c1[:, :], consts1).then_inc(c1_in, 16)
                elif st == ("norm", 1, "mix"):
                    for last_read in readers(st):
                        sp.wait_ge(*last_read)
                    for r in range(SEQ // GRID_W):
                        for kr in range(SEQ // GRID_W):
                            src = bass.AP(tensor=rpb_na.tensor, offset=rpb_na.offset + (kr - r + 7) * 31 + 15 - 63,
                                          ap=[[1, 64], [465, 8], [1, 64]])
                            dst = bias[64 * (r % 2):64 * (r % 2) + 64, r // 2, :, 64 * kr:64 * kr + 64]
                            sp.dma_start(dst, src).then_inc(bias_in, 16)
                elif st[0] == "mlp":
                    L = st[1]
                    u0, g0 = unit[st], gnum[st]
                    plan = mlp_plan(L)
                    with sp.Fori(0, FF_CHUNKS, 1) as cc:
                        where = []
                        for i, (kind, m) in enumerate(plan):
                            what, n = where[i - RAW] if i >= RAW else ("product", i - RAW)
                            if what == "mod":
                                sp.wait_ge(mod_used, NMOD + n + 1 + cc * MODS_LOOP)
                            else:
                                sp.wait_ge(lo_done, g0 + n + 1 + cc * (2 * KT))
                            if kind == "mod":
                                src = tile_of(w_mod[1], 0, cc * (MODS_LOOP * P) + P * m)
                                where.append(("mod", sum(q == "mod" for q, _ in where)))
                            else:
                                src = tile_of(w_ff1[L], 0, cc * D + P * m) if kind == "ff1" else tile_of(w_ff2[L], cc * D, P * m)
                                where.append(("product", sum(q == "product" for q, _ in where)))
                            slot = (u0 + i) % RAW
                            sp.dma_start(raw[:, slot, :, :], src).then_inc(raw_in[slot], 16)
                    end = g0 + FF_CHUNKS * 2 * KT
                    used += [None] * (FF_CHUNKS * len(plan) - RAW) + [(lo_done, end - RAW + 1 + i) for i in range(RAW)]
            sp.wait_ge(fin_done, 2)
            sp.wait_ge(finv_done, 2)
            sp.dma_start(out[0].rearrange("(t p) d -> p t d", p=P), fin[:, :, :]).then_inc(out_in, 16)
            sp.wait_ge(out_in, 16)

        @block.gpsimd
        def _(pool):
            pool.memset(mhalf[:, :], -0.5).then_inc(pool_seq, 1)
            pool.memset(cpad[:, :, :, :], 0.0).then_inc(consts_set, 1)
            pool.wait_ge(pool_seq, 1)
            n_var = 0
            for st in steps:
                if st[0] in ("norm", "ysum", "hvar"):
                    n_var += 1
                    n = {"norm": 2 if st == ("norm", 1, "ff") else NCH, "ysum": NCH, "hvar": N_HEADS}[st[0]]
                    pool.wait_ge(var_done, n_var)
                    pool.tensor_tensor(rstd[:, 0:n], var[:, 0:n], mhalf[:, 0:n], ALU.pow).then_inc(rstd_done, 1)
                    if st == ("norm", 1, "mix"):
                        pool.wait_ge(bias_in, 16 * 16)
                        pool.wait_ge(c1_in, 16)
                        for qt in range(2):
                            pool.tensor_tensor(bias[:, qt, :, :], bias[:, qt, :, :], cuts["nam"][:, None, :].broadcast_to([P, 8, SEQ]),
                                               ALU.add).then_inc(bias_done, 1)
                elif st[0] == "state":
                    _, g, d, ch = st
                    n, di = st_n[st], dirs[d]
                    pool.wait_ge(xdt_done, tok_n[("toks", g, SCAN_F[-1])] + 1)
                    pool.wait_ge(dtx_done, 3)
                    if n >= 2:
                        pool.wait_ge(*filled(st_l[n - 2]))
                    pool.tensor_tensor(heads(xw[:, n % 2, :]), heads(xdt[:, di, ch, :]),
                                       dts["dte"][:, ch, NH * di + R * g:NH * di + R * g + R].unsqueeze(2).broadcast_to([P, R, HD]),
                                       ALU.mult).then_inc(xw_done, 1)
                elif st[0] == "seg":
                    _, g, d, ch = st
                    n, di = seg_n[st], dirs[d]
                    if n == 0:
                        pool.wait_ge(dt_done, 1)
                        pool.wait_ge(c0_in, 16)
                    else:
                        pool.wait_ge(*filled(seg_l[n - 1]))
                    pool.tensor_tensor(rr[:, :, :],
                                       dts["dta"][:, ch, NH * di + R * g:NH * di + R * g + R].unsqueeze(2).broadcast_to([P, R, P]),
                                       (tle, tge)[di][:, None, :].broadcast_to([P, R, P]), ALU.mult).then_inc(rr_done, 1)

        @block.scalar
        def _(act):
            signal, freeing, latest, counts = ledger()

            def high(n, u, k, pass_u=0, pass_b=0):
                act.wait_ge(raw_in[u % RAW], 16 * (u // RAW + 1) + pass_u)
                if n >= SPLIT:
                    act.wait_ge(bank_full[B_GEMM[n % 2]], k + pass_b)
                nc.scalar.activation(w_hi[:, n % SPLIT, :, :], raw[:, u % RAW, :, :], ACT.Copy).then_inc(hi_done, 1)

            n_sq = 0
            for st in steps:
                k = st[0]
                if k == "vecs":
                    act.wait_ge(vt_done, 3)
                    nc.scalar.activation(sct[:, :, :], vt[:, 2, 12:28].rearrange("p (s t) -> p t s", s=2), ACT.Tanh,
                                             scale=0.5).then_inc(signal(th0_done), 1)
                    act.wait_ge(vt_done, 4)
                    nc.scalar.activation(nega[:, :], bc[:, 0:48], ACT.Exp).then_inc(signal(th0_done), 1)
                elif k == "norm":
                    ntok = SEQ if st == ("norm", 1, "ff") else T
                    for f in range(KT):
                        act.wait_ge(h_done, h_before[st] - KT + f + 1)
                        if n_sq >= 2:
                            act.wait_ge(sq_used, n_sq - 1)
                        nc.scalar.activation(sq[:, n_sq % 2, 0:ntok], hT[:, f, 0:ntok], ACT.Square).then_inc(signal(sq_done), 1)
                        n_sq += 1
                    if st == norms[0]:
                        high(*first_tile(gemms[0]))
                    act.wait_ge(coef_done, norm_n[st] + 1)
                    for last_read in readers(st):
                        act.wait_ge(*last_read)
                    for f in range(KT):
                        n = KT * norm_n[st] + f
                        act.wait_ge(nt_done, n + 1)
                        if n >= 2:
                            act.wait_ge(split_done, split_at[st] + f - 1 if f >= 2 else split_at[norms[norm_n[st] - 1]] + KT - 1 + f)
                        sh = f + (0 if st[2] == "mix" else 3 * KT)
                        for i in range(ntok // SEQ):
                            nc.scalar.activation(u32[:, f % 2, SEQ * i:SEQ * i + SEQ], nt[:, f % 2, SEQ * i:SEQ * i + SEQ],
                                                     ACT.Identity, bias=mod[:, st[1], sh, i:i + 1], scale=coefA[:, f, i:i + 1]).then_inc(signal(act_seq), 1)
                        act.wait_ge(*latest())
                        nc.scalar.activation(a_hi[:, f, 0:ntok], u32[:, f % 2, 0:ntok], ACT.Copy).then_inc(signal(u_done), 1)
                elif k == "dt":
                    act.wait_ge(wdt_in, 16)
                    nc.scalar.activation(wdt_hi[:, :, :], wdt[:, :, :], ACT.Copy).then_inc(signal(wdthi_done), 1)
                    act.wait_ge(dtv_done, 1)
                    nc.scalar.activation(dts["t2"][:, :, :], dts["tmp"][:, :, :], ACT.Abs).then_inc(signal(act_seq), 1)
                    act.wait_ge(*latest())
                    nc.scalar.activation(dts["t3"][:, :, :], dts["t2"][:, :, :], ACT.Exp, scale=-1.0).then_inc(signal(dte_done), 1)
                    act.wait_ge(*latest())
                    nc.scalar.activation(dts["ea"][:, :, :], dts["t3"][:, :, :], ACT.Ln, bias=1.0).then_inc(signal(dtln_done), 1)
                    b = jobs[st + ("cum",)][0]
                    act.wait_ge(*filled(st + ("cum",)))
                    act.wait_ge(dt_done, 1)
                    nc.scalar.activation(dts["ea"][:, :, :], ps[:, b, 0:192].rearrange("p (c h) -> p c h", c=NCH), ACT.Exp).then_inc(signal(dtx_done), 1)
                    nc.scalar.activation(dts["dte"][:, :, :], ps[:, b, 192:384].rearrange("p (c h) -> p c h", c=NCH), ACT.Exp).then_inc(signal(dtx_done), 1)
                    b = jobs[st + ("tot",)][0]
                    act.wait_ge(*filled(st + ("tot",)))
                    nc.scalar.activation(dts["tot"][:, :, :], ps[:, b, 0:192].rearrange("p (c h) -> p c h", c=NCH), ACT.Exp).then_inc(signal(dtx_done), 1)
                elif k == "gemm":
                    if st in after:
                        high(*first_tile(after[st]))
                    b, _ = jobs[st]
                    if st[1] == "conv":
                        n = conv_n[st]
                        if n == 0:
                            act.wait_ge(consts_set, 1)
                        if n >= 2:
                            act.wait_ge(acc_done, n - 1)
                        act.wait_ge(*filled(st))
                        nc.scalar.activation(cpad[:, n % 2, :, 2:2 + SEQ], ps[:, b, :].rearrange("p (s t) -> p s t", s=2), ACT.Copy).then_inc(signal(pad_done), 1)
                    elif st[1] == "z":
                        n = z_n[st]
                        act.wait_ge(*filled(st))
                        if n >= 1:
                            act.wait_ge(gate_done, n)
                        nc.scalar.activation(zt[:, :], ps[:, b, :], ACT.Tanh, scale=0.5).then_inc(signal(zt_done), 1)
                    elif st[1] in ("qn", "kn", "qw", "kw"):
                        ntok = tokens(st)
                        act.wait_ge(*filled(st))
                        nc.scalar.activation(ktile(*st[1:])[0], ps[:, b, 0:ntok], ACT.Copy).then_inc(signal(qraw_done), 1)
                        act.wait_ge(sq_used, n_sq - 1)
                        nc.scalar.activation(sq[:, n_sq % 2, 0:ntok], ps[:, b, 0:ntok], ACT.Square).then_inc(signal(sq_done), 1)
                        n_sq += 1
                    elif st[1] == "v":
                        act.wait_ge(*filled(st))
                        if st[2] >= 1:
                            act.wait_ge(*filled(("vtok", st[2] - 1)))
                        nc.scalar.activation(vT[:, :], ps[:, b, :], ACT.Copy).then_inc(signal(vT_done), 1)
                elif k == "silu":
                    n = conv_n[("gemm", "conv", st[1])]
                    act.wait_ge(acc_done, n + 1)
                    if n >= 1:
                        act.wait_ge(xbc_done, n)
                    nc.scalar.activation(cth[:, :], cacc[:, n % 2, :], ACT.Tanh).then_inc(signal(th_done), 1)
                elif k == "vtok":
                    b = jobs[st][0]
                    act.wait_ge(*filled(st))
                    nc.scalar.activation(vtok[:, :, P * st[1]:P * st[1] + P], ps[:, b, :].rearrange("p (c d) -> p c d", c=NCH), ACT.Copy).then_inc(signal(vtok_done), 1)
                elif k == "seg":
                    n, di = seg_n[st], dirs[st[2]]
                    if n >= 2:
                        act.wait_ge(*filled(("y", seg_l[n - 2][1], seg_l[n - 2][3], "d")))
                    b = jobs[st][0]
                    act.wait_ge(*filled(st))
                    nc.scalar.activation(ey[:, di, :, :].rearrange("p (a h) l -> p a (h l)", a=2), ps[:, b:b + 2, 0:GX], ACT.Exp).then_inc(signal(seg_done), 1)
                elif k == "ygate":
                    g = st[1]
                    act.wait_ge(gated, g + 1)
                    nc.scalar.activation(gate[:, :, :], mixF[:, FN_T + XT * g:FN_T + XT * g + XT, :], ACT.Square).then_inc(signal(ysq_done), 1)
                elif k == "mixsplit":
                    hi = (a_hi, b_hi)[st[1]]
                    for last_read in readers(st):
                        act.wait_ge(*last_read)
                    for f in range(KT):
                        t = KT * st[1] + f
                        act.wait_ge(mix_done, t + 1)
                        if st[1] == 1 and f == 0:
                            act.wait_ge(mix_done, 2 * KT)
                            for q in y_jobs(G - 1, SCAN_F[-1]):
                                act.wait_ge(*filled(q))
                        nc.scalar.activation(hi[:, f, :], mixF[:, t, :], ACT.Copy).then_inc(signal(mixhi_done), 1)
                elif k == "mlp":
                    L = st[1]
                    ntok = T if L == 0 else SEQ
                    u0, g0 = unit[st], gnum[st]
                    j0 = jobs[st + (B_GEMM[0],)][1], jobs[st + (B_GEMM[1],)][1]
                    plan = mlp_plan(L)
                    where = [i for i, q in enumerate(plan) if q[0] != "mod"] + [len(plan)]

                    def one_pass(cc, last):
                        for n in range(2 * KT):
                            kind, m = plan[where[n]]
                            if not (last and n == 2 * KT - 1):
                                high(g0 + n + 1, u0 + where[n + 1], j0[(n + 1) % 2] + (n + 1) // 2 - 1,
                                     cc * (16 * len(plan) // RAW), cc * KT)
                            if kind == "ff1":
                                b = B_GEMM[n % 2]
                                act.wait_ge(bank_full[b], j0[n % 2] + n // 2 + cc * KT)
                                act.wait_ge(hid_done, FF_CHUNKS * KT * L + m + 1 + cc * KT)
                                nc.scalar.activation(hr[:, m % 2, 0:ntok], ps[:, b, 0:ntok], ACT.Relu)\
                                    .then_inc(hr_done, 1)
                    if L == 0:
                        with act.Fori(0, FF_CHUNKS, 1) as cc:
                            one_pass(cc, False)
                    else:
                        with act.Fori(0, FF_CHUNKS - 1, 1) as cc:
                            one_pass(cc, False)
                        one_pass(FF_CHUNKS - 1, True)
                elif k == "exp":
                    i = st[1]
                    t, par, qt = ATTN[i]
                    act.wait_ge(max_done, i + 1)
                    b, _ = jobs[("S", i)]
                    if i >= 2:
                        act.wait_ge(*filled(("PT", i - 2)))
                    else:
                        act.wait_ge(split_done, split_at[("norm", 1, "mix")] + KT)
                    nc.scalar.activation(prob[:, i % 2, :], ps[:, b, :], ACT.Exp, bias=sm[:, 0, i % 2:i % 2 + 1],
                                                  accum_out=sm[:, 1, i % 2:i % 2 + 1]).then_inc(freeing(("S", i)), 1)
                    h = 2 * (t % 4) + par
                    nc.scalar.activation(sm[:, 2, i % 2:i % 2 + 1], bc[:, 120 + h:121 + h], ACT.Exp,
                                             bias=sm[:, 0, i % 2:i % 2 + 1]).then_inc(signal(exp_done), 1)
                elif k == "scale":
                    i = st[1]
                    act.wait_ge(rs_done, i + 1)
                    act.wait_ge(*latest())
                    nc.scalar.activation(prob[:, i % 2, :], prob[:, i % 2, :], ACT.Copy, scale=sm[:, 4, i % 2:i % 2 + 1]).then_inc(signal(prob_done), 1)
                elif k == "osplit":
                    b = jobs[("Opair", st[1])][0]
                    act.wait_ge(*filled(("Opair", st[1])))
                    nc.scalar.activation(a_hi[:, st[1], 0:SEQ], ps[:, b, 0:SEQ], ACT.Copy).then_inc(signal(ohi_done), 1)
                elif k == "out":
                    for q in (1, 3):
                        b = jobs[st + (q,)][0]
                        act.wait_ge(*filled(st + (q,)))
                        nc.scalar.activation(fin[:, q // 2, 512:1024], ps[:, b, :], ACT.Copy).then_inc(signal(fin_done), 1)

        @block.vector
        def _(dve):
            v = nc.vector
            signal, freeing, latest, counts = ledger()

            def low(n, u, passes=0):
                dve.wait_ge(hi_done, n + 1 + passes)
                v.tensor_tensor(w_lo[:, n % SPLIT, :, :], raw[:, u % RAW, :, :], w_hi[:, n % SPLIT, :, :].bitcast(F32),
                                ALU.subtract).then_inc(lo_done, 1)

            def residual(st, key, m, L, gate_tile):
                b = jobs[key][0]
                dve.wait_ge(*filled(key))
                halves = tokens(st) // SEQ
                for i in range(halves):
                    hs = hT[:, m, SEQ * i:SEQ * i + SEQ]
                    v.scalar_tensor_tensor(out=hs, in0=ps[:, b, SEQ * i:SEQ * i + SEQ],
                                               scalar=mod[:, L, gate_tile, i:i + 1], in1=hs, op0=ALU.mult, op1=ALU.add).then_inc(signal(h_done if i == halves - 1 else dve_seq), 1)

            n_var = 0
            v.memset(rstd[:, 0:1], 0.0).then_inc(signal(hid_done), 1)
            v.memset(var[:, 0:1], 0.0).then_inc(signal(hid_done), 1)
            for st in steps:
                k = st[0]
                if k == "vecs":
                    for q in range(3):
                        b = jobs[st + (q,)][0]
                        dve.wait_ge(*filled(st + (q,)))
                        n = (P, 120, 32)[q]
                        v.tensor_copy(vt[:, q, 0:n], ps[:, b, 0:n]).then_inc(freeing(st + (q,)), 1)
                        dve.wait_ge(*latest())
                        if q == 1:
                            v.tensor_scalar(vt[:, 1, 0:120], vt[:, 1, 0:120], 0.5, None, ALU.mult).then_inc(signal(dve_seq), 1)
                        if q == 2:
                            v.tensor_scalar(gssdT, gssdT, 0.5, None, ALU.mult).then_inc(signal(dve_seq), 1)
                            v.tensor_scalar(vt[:, 2, 28:29], vt[:, 2, 28:29], HD ** -0.5, None, ALU.mult).then_inc(signal(dve_seq), 1)
                            v.tensor_scalar(vt[:, 2, 30:31], vt[:, 2, 30:31], HD ** -0.5, None, ALU.mult).then_inc(signal(dve_seq), 1)
                        dve.wait_ge(*latest())
                        v.tensor_copy(var[:, 0:1], vt[:, q, 0:1]).then_inc(signal(vt_done), 1)
                        dve.wait_ge(*latest())
                    b = jobs[st + (3,)][0]
                    dve.wait_ge(*filled(st + (3,)))
                    v.tensor_copy(bc[:, :], ps[:, b, 0:P]).then_inc(signal(vt_done), 1)
                    dve.wait_ge(*latest())
                    pairs = bc[:, 96:120].rearrange("p (t h) -> p t h", h=2)
                    for i in range(2):
                        v.tensor_copy(dsk[HD * i:HD * i + HD, :], pairs[HD * i:HD * i + HD, :, i]).then_inc(signal(dve_seq), 1)
                    dve.wait_ge(th0_done, 2)
                    v.tensor_scalar(nega[:, :], nega[:, :], -1.0, None, ALU.mult).then_inc(signal(dve_seq), 1)
                    v.tensor_scalar(silc[:, :, :], vt[:, 2, 12:28].rearrange("p (s t) -> p t s", s=2), 0.5, None, ALU.mult).then_inc(signal(dve_seq), 1)
                    dve.wait_ge(*latest())
                    v.scalar_tensor_tensor(out=silc[:, :, :], in0=sct[:, :, :], scalar=1.0, in1=silc[:, :, :],
                                               op0=ALU.add, op1=ALU.mult).then_inc(signal(silc_done), 1)
                elif k == "mods":
                    b = jobs[st][0]
                    dve.wait_ge(*filled(st))
                    n = st[3] - st[2]
                    v.tensor_tensor(mod[:, st[1], st[2]:st[3], :], ps[:, b, 0:2 * n].rearrange("p (f s) -> p f s", s=2),
                                             bmodT[:, st[1], st[2]:st[3]].unsqueeze(2).broadcast_to([P, n, 2]), ALU.add).then_inc(freeing(st), 1)
                elif k == "xin":
                    for f in range(KT):
                        b = jobs[st + (f,)][0]
                        dve.wait_ge(*filled(st + (f,)))
                        v.tensor_copy(hT[:, f, :], ps[:, b, :]).then_inc(signal(h_done), 1)
                elif k == "norm":
                    L = st[1]
                    ntok = SEQ if st == ("norm", 1, "ff") else T
                    if st == norms[0]:
                        low(*first_tile(gemms[0])[:2])
                    dve.wait_ge(*latest())
                    sc = (1 if st[2] == "mix" else 4) * KT
                    gains = (gmixT if st[2] == "mix" else gffT)[:, L, :]
                    if norm_n[st]:
                        dve.wait_ge(u_done, KT * norm_n[st])
                    v.scalar_tensor_tensor(out=coefA[:, :, :], in0=mod[:, L, sc:sc + KT, :], scalar=1.0,
                                               in1=gains.unsqueeze(2).broadcast_to([P, KT, 2]), op0=ALU.add, op1=ALU.mult).then_inc(signal(coef_done), 1)
                    b = jobs[st + ("sum",)][0]
                    dve.wait_ge(*filled(st + ("sum",)))
                    if n_var:
                        dve.wait_ge(rstd_done, n_var)
                    v.tensor_scalar(var[:, 0:ntok // P], ps[:, b, 0:ntok // P], 1.0 / D, EPS, ALU.mult, ALU.add).then_inc(signal(var_done), 1)
                    n_var += 1
                    b = jobs[st + ("bc",)][0]
                    dve.wait_ge(*filled(st + ("bc",)))

                    def scaled(f):
                        n = KT * norm_n[st] + f
                        if n >= 2:
                            dve.wait_ge(u_done, n - 1)
                        ins = v.tensor_tensor(nt[:, f % 2, 0:ntok], hT[:, f, 0:ntok], ps[:, b, 0:ntok], ALU.mult).then_inc(signal(nt_done), 1)
                    scaled(0)
                    scaled(1)
                    for f in range(KT):
                        dve.wait_ge(u_done, KT * norm_n[st] + f + 1)
                        v.tensor_tensor(a_lo[:, f, 0:ntok], u32[:, f % 2, 0:ntok], a_hi[:, f, 0:ntok].bitcast(F32), ALU.subtract).then_inc(signal(split_done), 1)
                        if f + 2 < KT:
                            scaled(f + 2)
                elif k == "dt":
                    dve.wait_ge(wdthi_done, 1)
                    v.tensor_tensor(wdt_lo[:, :, :], wdt[:, :, :], wdt_hi[:, :, :].bitcast(F32), ALU.subtract).then_inc(signal(wdtlo_done), 1)
                    b = jobs[st + ("raw",)][0]
                    dve.wait_ge(*filled(st + ("raw",)))
                    v.tensor_tensor(dts["tmp"][:, :, :], ps[:, b, 0:192].rearrange("p (c h) -> p c h", c=NCH),
                                             bc[:, None, 48:96].broadcast_to([P, NCH, 48]), ALU.add).then_inc(signal(dtv_done), 1)
                    dve.wait_ge(dte_done, 1)
                    v.tensor_scalar(dts["dt"][:, :, :], dts["t3"][:, :, :], 1.0, None, ALU.add).then_inc(signal(dve_seq), 1)
                    dve.wait_ge(*latest())
                    v.tensor_scalar(dts["dt"][:, :, :], dts["dt"][:, :, :], -1.0, None, ALU.add).then_inc(signal(dve_seq), 1)
                    dve.wait_ge(*latest())
                    v.tensor_tensor(dts["dt"][:, :, :], dts["t3"][:, :, :], dts["dt"][:, :, :], ALU.subtract).then_inc(signal(dve_seq), 1)
                    dve.wait_ge(dtln_done, 1)
                    dve.wait_ge(*latest())
                    v.tensor_tensor(dts["dt"][:, :, :], dts["dt"][:, :, :], dts["ea"][:, :, :], ALU.add).then_inc(signal(dve_seq), 1)
                    dve.wait_ge(*latest())
                    v.scalar_tensor_tensor(out=dts["dt"][:, :, :], in0=dts["tmp"][:, :, :], scalar=0.0, in1=dts["dt"][:, :, :],
                                               op0=ALU.max, op1=ALU.add).then_inc(signal(dve_seq), 1)
                    dve.wait_ge(*latest())
                    v.tensor_tensor(dts["dta"][:, :, :], dts["dt"][:, :, :], nega[:, None, :].broadcast_to([P, NCH, 48]), ALU.mult).then_inc(signal(dt_done), 1)
                elif k == "gemm":
                    if st in after:
                        low(*first_tile(after[st])[:2])
                    b, _ = jobs[st]
                    if st[1] == "fn":
                        dve.wait_ge(*filled(st))
                        if st[2] >= 2:
                            dve.wait_ge(*filled(("dftw", st[2] - 2, 1)))
                        v.tensor_copy(uf[:, st[2] % 2, :], ps[:, b, :]).then_inc(signal(uf_done), 1)
                    elif st[1] == "conv":
                        n, t = conv_n[st], st[2]
                        dve.wait_ge(pad_done, n + 1)
                        if n >= 2:
                            dve.wait_ge(th_done, n - 1)
                        acc = cacc[:, n % 2, :].rearrange("p (s t) -> p s t", s=2)
                        dve.wait_ge(*latest())
                        v.tensor_scalar(acc, cpad[:, n % 2, :, 0:SEQ], convwT[:, 0, t:t + 1], convbT[:, t:t + 1], ALU.mult, ALU.add).then_inc(signal(dve_seq), 1)
                        for w in range(1, CONV_W):
                            dve.wait_ge(*latest())
                            v.scalar_tensor_tensor(out=acc, in0=cpad[:, n % 2, :, w:w + SEQ], scalar=convwT[:, w, t:t + 1],
                                                       in1=acc, op0=ALU.mult, op1=ALU.add).then_inc(signal(acc_done if w == CONV_W - 1 else dve_seq), 1)
                    elif st[1] == "z":
                        n, i = z_n[st], st[2] % XT
                        dve.wait_ge(zt_done, n + 1)
                        if i == 0 and n:
                            dve.wait_ge(*filled(("ysum", n // XT - 1)))
                        v.scalar_tensor_tensor(out=gate[:, i, :], in0=zt[:, :], scalar=1.0, in1=ps[:, b, :],
                                                        op0=ALU.add, op1=ALU.mult).then_inc(signal(gate_done), 1)
                    elif st[1] in ("outA", "outB", "outO"):
                        dve.wait_ge(*latest())
                        residual(st, st, st[2], 1 if st[1] == "outO" else 0, 2 * KT + st[2])
                elif k == "silu":
                    t = st[1]
                    n = conv_n[("gemm", "conv", t)]
                    g = [t in conv_tiles(g) for g in range(G)].index(True)
                    slot = conv_tiles(g).index(t)
                    dve.wait_ge(th_done, n + 1)
                    if slot == 0 and g >= 2:
                        for q in y_jobs(g - 2, SCAN_F[-1]):
                            dve.wait_ge(*filled(q))
                    dve.wait_ge(*latest())
                    v.scalar_tensor_tensor(out=xbc[:, g % 2, slot, :], in0=cth[:, :], scalar=1.0, in1=cacc[:, n % 2, :],
                                               op0=ALU.add, op1=ALU.mult).then_inc(signal(xbc_done), 1)
                elif k == "dftw":
                    if st[1]:
                        dve.wait_ge(*filled(("dfts", st[1] - 1)))
                    for q in range(2):
                        b = jobs[st + (q,)][0]
                        dve.wait_ge(*filled(st + (q,)))
                        v.tensor_copy(vf[:, 2 * q:2 * q + 2, :], ps[:, b, :].rearrange("p (c f) -> p c f", c=2)).then_inc(signal(vf_done), 1)
                elif k == "dfts":
                    b = jobs[st][0]
                    dve.wait_ge(*filled(st))
                    v.tensor_copy(mixF[:, st[1], :], ps[:, b, :]).then_inc(signal(mix_done), 1)
                elif k == "toks":
                    _, g, ch = st
                    if ch == SCAN_F[0]:
                        if g == 0:
                            dve.wait_ge(*filled(("dfts", FN_T - 1)))
                        else:
                            for q in y_jobs(g - 1, SCAN_F[-1]):
                                dve.wait_ge(*filled(q))
                    b = jobs[st][0]
                    dve.wait_ge(*filled(st))
                    v.tensor_copy(btok[:, ch, :], ps[:, b, GX:GX + NS]).then_inc(signal(dve_seq), 1)
                    for di in range(2):
                        v.tensor_tensor(heads(xdt[:, di, ch, :]), heads(ps[:, b, 0:GX]),
                                            dts["dt"][:, ch, NH * di + R * g:NH * di + R * g + R].unsqueeze(2).broadcast_to([P, R, HD]),
                                            ALU.mult).then_inc(signal(xdt_done if di else dve_seq), 1)
                elif k == "state":
                    _, g, d, ch = st
                    di = dirs[d]
                    old, new = entering(d, ch), scans[d].index(ch)
                    b = jobs[st][0]
                    dve.wait_ge(*filled(st))
                    dve.wait_ge(*latest())
                    if st_n[st] % len(STATES) == 0:
                        dve.wait_ge(dtx_done, 3)
                    if old is None:
                        v.tensor_copy(hent[:, di, new, :], ps[:, b, 0:GX]).then_inc(signal(ent_done), 1)
                    else:
                        v.tensor_tensor(heads(hent[:, di, new, :]), heads(hent[:, di, old, :]),
                                            dts["tot"][:, ch, NH * di + R * g:NH * di + R * g + R].unsqueeze(2).broadcast_to([P, R, HD]), ALU.mult).then_inc(signal(dve_seq), 1)
                        dve.wait_ge(*latest())
                        v.tensor_tensor(hent[:, di, new, :], hent[:, di, new, :], ps[:, b, 0:GX], ALU.add).then_inc(signal(ent_done), 1)
                elif k == "cb":
                    b = jobs[st][0]
                    dve.wait_ge(*filled(st))
                    dve.wait_ge(*latest())
                    v.tensor_tensor(cbm[:, 0, :], ps[:, b, 0:P], tle, ALU.mult).then_inc(signal(dve_seq), 1)
                    v.tensor_tensor(cbm[:, 1, :], ps[:, b, 0:P], tge, ALU.mult).then_inc(freeing(st), 1)
                elif k == "seg":
                    di = dirs[st[2]]
                    dve.wait_ge(seg_done, seg_n[st] + 1)
                    dve.wait_ge(*latest())
                    v.tensor_tensor(ey[:, di, :, :], ey[:, di, :, :], cbm[:, di, None, :].broadcast_to([P, R, P]), ALU.mult).then_inc(signal(g_done), 1)
                elif k == "y":
                    _, g, ch = st
                    if y_n[st]:
                        prev = steps_of("y")[y_n[st] - 1]
                        dve.wait_ge(*filled(("yt",) + prev[1:]))
                    parts = []
                    for di, q in enumerate("fb"):
                        if st + (q,) in jobs:
                            b = jobs[st + (q,)][0]
                            dve.wait_ge(*filled(st + (q,)))
                            v.tensor_tensor(heads(ycomb[:, di, :]), heads(ps[:, b, 0:GX]),
                                                     dts["ea"][:, ch, NH * di + R * g:NH * di + R * g + R].unsqueeze(2).broadcast_to([P, R, HD]),
                                                     ALU.mult).then_inc(freeing(st + (q,)), 1)
                            parts.append(di)
                    dve.wait_ge(*latest())
                    if len(parts) == 2:
                        v.tensor_tensor(ycomb[:, 0, :], ycomb[:, 0, :], ycomb[:, 1, :], ALU.add).then_inc(signal(dve_seq), 1)
                        dve.wait_ge(*latest())
                    b = jobs[st + ("d",)][0]
                    dve.wait_ge(*filled(st + ("d",)))
                    src = parts[0]
                    v.tensor_tensor(ycomb[:, 0, :], ycomb[:, src, :], ps[:, b, 0:GX], ALU.add).then_inc(signal(y_done), 1)
                elif k == "yt":
                    _, g, ch = st
                    b = jobs[st][0]
                    dve.wait_ge(*filled(st))
                    for i in range(XT):
                        v.scalar_tensor_tensor(out=mixF[:, FN_T + XT * g + i, P * ch:P * ch + P],
                                                   in0=xbc[:, g % 2, 2 + i, P * ch:P * ch + P],
                                                   scalar=dsk[:, XT * g + i:XT * g + i + 1],
                                                   in1=ps[:, b, P * i:P * i + P], op0=ALU.mult, op1=ALU.add).then_inc(freeing(st) if i == XT - 1 else signal(dve_seq), 1)
                elif k == "ygate":
                    g = st[1]
                    dve.wait_ge(*latest())
                    mg = mixF[:, FN_T + XT * g:FN_T + XT * g + XT, :]
                    v.tensor_tensor(mg, mg, gate[:, :, :], ALU.mult).then_inc(signal(gated), 1)
                elif k == "ysum":
                    b = jobs[st][0]
                    dve.wait_ge(*filled(st))
                    dve.wait_ge(rstd_done, n_var)
                    v.tensor_scalar(var[:, 0:NCH], ps[:, b, 0:NCH], 0.25 / GX, EPS, ALU.mult, ALU.add).then_inc(signal(var_done), 1)
                    n_var += 1
                elif k == "ynorm":
                    g = st[1]
                    b = jobs[st][0]
                    dve.wait_ge(*filled(st))
                    dve.wait_ge(ysq_done, g + 1)
                    dve.wait_ge(*latest())
                    for i in range(XT):
                        mi = mixF[:, FN_T + XT * g + i, :]
                        ins = v.scalar_tensor_tensor(out=mi, in0=mi, scalar=gssdT[:, XT * g + i:XT * g + i + 1], in1=ps[:, b, :],
                                                         op0=ALU.mult, op1=ALU.mult).then_inc(signal(mix_done), 1)
                elif k == "mixsplit":
                    hi, lo = ((a_hi, a_lo), (b_hi, b_lo))[st[1]]
                    for f in range(KT):
                        t = KT * st[1] + f
                        dve.wait_ge(mixhi_done, t + 1)
                        dve.wait_ge(*latest())
                        v.tensor_tensor(lo[:, f, :], mixF[:, t, :], hi[:, f, :].bitcast(F32), ALU.subtract).then_inc(signal(split_done), 1)
                elif k == "mlp":
                    L = st[1]
                    ntok = T if L == 0 else SEQ
                    u0, g0 = unit[st], gnum[st]
                    j0 = jobs[st + (B_GEMM[0],)][1], jobs[st + (B_GEMM[1],)][1]
                    plan = mlp_plan(L)
                    where = [i for i, q in enumerate(plan) if q[0] != "mod"] + [len(plan)]
                    h0 = FF_CHUNKS * KT * L

                    def one_pass(cc, last):
                        for n in range(2 * KT):
                            kind, m = plan[where[n]]
                            if not (last and n == 2 * KT - 1):
                                low(g0 + n + 1, u0 + where[n + 1], cc * (2 * KT))
                            b = B_GEMM[n % 2]
                            if kind == "ff1":
                                dve.wait_ge(hr_done, h0 + m + 1 + cc * KT)
                                v.tensor_tensor(hq[:, m % 2, 0:ntok], hr[:, m % 2, 0:ntok], hr[:, m % 2, 0:ntok], ALU.mult).then_inc(hq_done, 1)
                                dve.wait_ge(hq_done, h0 + m + 1 + cc * KT)
                                v.tensor_copy(b_hi[:, m, 0:ntok], hq[:, m % 2, 0:ntok]).then_inc(hidhi_done, 1)
                                dve.wait_ge(hidhi_done, h0 + m + 1 + cc * KT)
                                v.tensor_tensor(b_lo[:, m, 0:ntok], hq[:, m % 2, 0:ntok], b_hi[:, m, 0:ntok].bitcast(F32),
                                                ALU.subtract).then_inc(hid_done, 1)
                            else:
                                dve.wait_ge(bank_full[b], j0[n % 2] + n // 2 + cc * KT)
                                dve.wait_ge(h_done, mlp_h[L] + m - KT + 1 + cc * KT)
                                for i in range(ntok // SEQ):
                                    hs = hT[:, m, SEQ * i:SEQ * i + SEQ]
                                    ins = v.scalar_tensor_tensor(out=hs, in0=ps[:, b, SEQ * i:SEQ * i + SEQ],
                                                                 scalar=mod[:, L, 5 * KT + m, i:i + 1], in1=hs, op0=ALU.mult, op1=ALU.add)
                                ins.then_inc(h_done, 1)
                            if L == 0 and n == MODS_LOOP:
                                bb = B_AUX[1]
                                dve.wait_ge(mod_used, NMOD + MODS_LOOP + cc * MODS_LOOP)
                                v.tensor_tensor(mod[:, 1, bass.ds(cc * MODS_LOOP, MODS_LOOP), :],
                                                ps[:, bb, 0:2 * MODS_LOOP].rearrange("p (f s) -> p f s", s=2),
                                                bmod1[:, bass.ds(cc * MODS_LOOP, MODS_LOOP)].unsqueeze(2).broadcast_to([P, MODS_LOOP, 2]),
                                                ALU.add).then_inc(bank_free[bb], 1)
                    if L == 0:
                        with dve.Fori(0, FF_CHUNKS, 1) as cc:
                            one_pass(cc, False)
                        what, n = freed_by[st + ("mods",)]
                        dve.wait_ge(signalled(what), n)
                    else:
                        with dve.Fori(0, FF_CHUNKS - 1, 1) as cc:
                            one_pass(cc, False)
                        one_pass(FF_CHUNKS - 1, True)
                    counts[h_done] += FF_CHUNKS * KT
                elif k == "hvar":
                    b = jobs["hstat"][0]
                    dve.wait_ge(*filled("hstat"))
                    dve.wait_ge(rstd_done, n_var)
                    v.tensor_scalar(var[:, 0:N_HEADS], ps[:, b, 0:N_HEADS], 1.0 / HD, EPS, ALU.mult, ALU.add).then_inc(signal(var_done), 1)
                    n_var += 1
                elif k == "htr":
                    b = jobs[st + ("q",)][0]
                    dve.wait_ge(*filled(st + ("q",)))
                    v.tensor_copy(rT[:, :], ps[0:NQ, b, 0:SEQ]).then_inc(signal(rT_done), 1)
                    b = jobs[st + ("k",)][0]
                    dve.wait_ge(*filled(st + ("k",)))
                    v.tensor_copy(rTk[:, :], ps[0:NKH, b, :]).then_inc(signal(rT_done), 1)
                elif k == "hnorm":
                    b = jobs[st][0]
                    dve.wait_ge(*filled(st))
                    ntok = odd_tokens[st[1:]]
                    x_ = ktile(*st[1:])[0]
                    v.scalar_tensor_tensor(out=x_, in0=x_, scalar=vt[:, 2, g_q[st[1]]:g_q[st[1]] + 1], in1=ps[:, b, 0:ntok],
                                                    op0=ALU.mult, op1=ALU.mult).then_inc(signal(qn_done), 1)
                elif k == "rot":
                    x_ = ktile(*st[1:])[0][:, 0:SEQ]
                    b = jobs[st][0]
                    dve.wait_ge(*filled(st))
                    dve.wait_ge(*latest())
                    v.tensor_tensor(rp[:, 0, :], x_, cuts["cos"], ALU.mult).then_inc(signal(dve_seq), 1)
                    v.tensor_tensor(rp[:, 1, :], ps[:, b, 0:SEQ], cuts["sin"], ALU.mult).then_inc(freeing(st), 1)
                    dve.wait_ge(*latest())
                    v.tensor_tensor(x_, rp[:, 0, :], rp[:, 1, :], ALU.add).then_inc(signal(rope_done), 1)
                elif k == "dup":
                    for q in range(2):
                        b = jobs[st + (q,)][0]
                        dve.wait_ge(*filled(st + (q,)))
                        v.tensor_copy(kdup[:, q, :], ps[:, b, :]).then_inc(signal(kd_done), 1)
                elif k == "exp":
                    i = st[1]
                    t, par, qt = ATTN[i]
                    b = jobs[("S", i)][0]
                    dve.wait_ge(*filled(("S", i)))
                    col = lambda r: sm[:, r, i % 2:i % 2 + 1]
                    dve.wait_ge(*latest())
                    v.tensor_reduce(col(3), ps[:, b, :], AX, ALU.max).then_inc(signal(dve_seq), 1)
                    dve.wait_ge(*latest())
                    if t < 4:
                        h = 2 * t + par
                        v.tensor_scalar(col(0), col(3), bc[:, 120 + h:121 + h], -1.0, ALU.max, ALU.mult).then_inc(signal(max_done), 1)
                    else:
                        v.tensor_scalar(col(0), col(3), -1.0, None, ALU.mult).then_inc(signal(max_done), 1)
                elif k == "scale":
                    i = st[1]
                    t, par, qt = ATTN[i]
                    col = lambda r: sm[:, r, i % 2:i % 2 + 1]
                    dve.wait_ge(exp_done, i + 1)
                    src = col(1)
                    if t < 4:
                        v.tensor_tensor(col(5), col(1), col(2), ALU.add).then_inc(signal(dve_seq), 1)
                        dve.wait_ge(*latest())
                        src = col(5)
                    v.reciprocal(col(4), src).then_inc(signal(rs_done), 1)
                elif k == "PT":
                    i = st[1]
                    b = jobs[st][0]
                    dve.wait_ge(*filled(st))
                    if i >= 2:
                        dve.wait_ge(pv_done, i - 1)
                    v.tensor_copy(pT[:, i % 2, :], ps[:, b, :]).then_inc(signal(pT_done), 1)
                elif k == "osplit":
                    t = st[1]
                    dve.wait_ge(ohi_done, t + 1)
                    b, _ = jobs[("Opair", t)]
                    v.tensor_tensor(a_lo[:, t, 0:SEQ], ps[:, b, 0:SEQ], a_hi[:, t, 0:SEQ].bitcast(F32), ALU.subtract).then_inc(signal(split_done), 1)
                elif k == "out":
                    for q in (0, 2):
                        b = jobs[st + (q,)][0]
                        dve.wait_ge(*filled(st + (q,)))
                        v.tensor_copy(fin[:, q // 2, 0:512], ps[:, b, :]).then_inc(signal(finv_done), 1)

        @block.tensor
        def _(pe):
            mm = nc.tensor.matmul

            def product(out_ap, n, hi, lo, ntok, ready=None):
                for k in range(KT):
                    if ready:
                        pe.wait_ge(ready[0], ready[1] + k)
                    for j, (w_, x_) in enumerate(((w_hi, hi), (w_hi, lo), (w_lo, hi))):
                        ins = mm(out_ap, w_[:, n % SPLIT, k, :], x_[:, k, 0:ntok], start=(k == 0 and j == 0), stop=(k == KT - 1 and j == 2))
                return ins

            def spread(key, n):
                b = jobs[key][0]
                if free_before[key]:
                    pe.wait_ge(*emptied(key))
                for ch in range(n):
                    ins = mm(ps[:, b, P * ch:P * ch + P], rstd[:, ch:ch + 1].broadcast_to([P, P]), ident, start=True, stop=True)
                ins.then_inc(filling(key), 1)

            n_sq = n_var = n_mod = 0
            for st in steps:
                k = st[0]
                if k == "vecs":
                    pe.wait_ge(vec_in, 16 * N_VEC)
                    pe.wait_ge(c0_in, 16)
                    for q in range(3):
                        n = (P, 120, 32)[q]
                        b = jobs[st + (q,)][0]
                        if free_before[st + (q,)]:
                            pe.wait_ge(*emptied(st + (q,)))
                        nc.tensor.transpose(ps[:, b, 0:n], vrow[0:n, q, :], ident[0:n, 0:n]).then_inc(filling(st + (q,)), 1)
                    b = jobs[st + (3,)][0]
                    if free_before[st + (3,)]:
                        pe.wait_ge(*emptied(st + (3,)))
                    mm(ps[:, b, 0:P], ones[0:1, :], rowv[:, :], start=True, stop=True).then_inc(filling(st + (3,)), 1)
                    pe.wait_ge(silc_done, 1)
                elif k == "mods":
                    b = jobs[st][0]
                    if free_before[st]:
                        pe.wait_ge(*emptied(st))
                    for i, f in enumerate(range(st[2], st[3])):
                        u = unit[("mod", st[1], f)]
                        pe.wait_ge(raw_in[u % RAW], 16 * (u // RAW + 1))
                        for kk in range(KT):
                            ins = mm(ps[:, b, 2 * i:2 * i + 2], raw[:, u % RAW, kk, :], silc[:, kk, :], start=(kk == 0), stop=(kk == KT - 1))
                        ins.then_inc(mod_used, 1)
                elif k == "xin":
                    for t in range(NCH):
                        pe.wait_ge(x_in[t], 16)
                    for f in range(KT):
                        b = jobs[st + (f,)][0]
                        if free_before[st + (f,)]:
                            pe.wait_ge(*emptied(st + (f,)))
                        for t in range(NCH):
                            ins = nc.tensor.transpose(ps[:, b, P * t:P * t + P], xload[:, t, P * f:P * f + P], ident)
                        ins.then_inc(filling(st + (f,)), 1)
                elif k == "norm":
                    n = 2 if st == ("norm", 1, "ff") else NCH
                    b = jobs[st + ("sum",)][0]
                    if free_before[st + ("sum",)]:
                        pe.wait_ge(*emptied(st + ("sum",)))
                    for f in range(KT):
                        n_sq += 1
                        pe.wait_ge(sq_done, n_sq)
                        for ch in range(n):
                            ins = mm(ps[:, b, ch:ch + 1], sq[:, (n_sq - 1) % 2, P * ch:P * ch + P], ones[:, 0:1],
                                     start=(f == 0 and ch == 0), stop=(f == KT - 1), skip_group_check=True)
                        ins.then_inc(sq_used, 1)
                    n_var += 1
                    pe.wait_ge(rstd_done, n_var)
                    spread(st + ("bc",), n)
                elif k == "dt":
                    pe.wait_ge(wdtlo_done, 1)
                    pe.wait_ge(split_done, KT)
                    b = jobs[st + ("raw",)][0]
                    if free_before[st + ("raw",)]:
                        pe.wait_ge(*emptied(st + ("raw",)))
                    for ch in range(NCH):
                        for kk in range(KT):
                            for j, (x_, w_) in enumerate(((a_hi, wdt_hi), (a_lo, wdt_hi), (a_hi, wdt_lo))):
                                ins = mm(ps[:, b, 48 * ch:48 * ch + 48], x_[:, kk, P * ch:P * ch + P], w_[:, kk, :],
                                         start=(kk == 0 and j == 0), stop=(kk == KT - 1 and j == 2))
                    ins.then_inc(filling(st + ("raw",)), 1)
                    pe.wait_ge(dt_done, 1)
                    b = jobs[st + ("cum",)][0]
                    if free_before[st + ("cum",)]:
                        pe.wait_ge(*emptied(st + ("cum",)))
                    for ch in range(NCH):
                        for o, (tf, tb) in ((0, (tle, tge)), (192, (tgt, tlt))):
                            for di, tri in enumerate((tf, tb)):
                                c_ = o + 48 * ch + NH * di
                                ins = mm(ps[:, b, c_:c_ + NH], tri, dts["dta"][:, ch, NH * di:NH * di + NH], start=True, stop=True)
                    ins.then_inc(filling(st + ("cum",)), 1)
                    b = jobs[st + ("tot",)][0]
                    if free_before[st + ("tot",)]:
                        pe.wait_ge(*emptied(st + ("tot",)))
                    mm(ps[:, b, 0:192], ones, dts["dta"][:, :, :].rearrange("p c h -> p (c h)"), start=True, stop=True).then_inc(filling(st + ("tot",)), 1)
                elif k == "gemm":
                    n = gnum[st]
                    b = jobs[st][0]
                    if free_before[st]:
                        pe.wait_ge(*emptied(st))
                    hi, lo = (b_hi, b_lo) if st[1] == "outB" else (a_hi, a_lo)
                    ready = None
                    if st in starts:
                        ready = split_done, starts[st] + 1
                    pe.wait_ge(lo_done, n + 1)
                    product(ps[:, b, 0:tokens(st)], n, hi, lo, tokens(st), ready).then_inc(filling(st), 1)
                elif k == "dftw":
                    pe.wait_ge(uf_done, st[1] + 1)
                    for q in range(2):
                        b = jobs[st + (q,)][0]
                        if free_before[st + (q,)]:
                            pe.wait_ge(*emptied(st + (q,)))
                        for i in range(2):
                            ch = 2 * q + i
                            ins = mm(ps[:, b, 256 * i:256 * i + 256], uf[:, st[1] % 2, P * ch:P * ch + P], dftw, start=True, stop=True)
                        ins.then_inc(filling(st + (q,)), 1)
                elif k == "dfts":
                    pe.wait_ge(vf_done, 2 * st[1] + 2)
                    b = jobs[st][0]
                    if free_before[st]:
                        pe.wait_ge(*emptied(st))
                    for s_ in range(2):
                        for kk in range(2):
                            for c_ in range(2):
                                ins = mm(ps[:, b, SEQ * s_:SEQ * s_ + SEQ], vf[:, 2 * s_ + kk, P * c_:P * c_ + P], dfts[:, kk, c_, :],
                                         start=(kk == 0 and c_ == 0), stop=(kk == 1 and c_ == 1))
                    ins.then_inc(filling(st), 1)
                elif k == "toks":
                    _, g, ch = st
                    pe.wait_ge(xbc_done, 5 * (g + 1))
                    b = jobs[st][0]
                    if free_before[st]:
                        pe.wait_ge(*emptied(st))
                    for i in range(XT):
                        nc.tensor.transpose(ps[:, b, P * i:P * i + P], xbc[:, g % 2, 2 + i, P * ch:P * ch + P], ident)
                    nc.tensor.transpose(ps[:, b, GX:GX + NS], xbc[:, g % 2, 0, P * ch:P * ch + P], ident).then_inc(filling(st), 1)
                elif k == "state":
                    _, g, d, ch = st
                    n = st_n[st]
                    pe.wait_ge(xw_done, n + 1)
                    b = jobs[st][0]
                    if free_before[st]:
                        pe.wait_ge(*emptied(st))
                    mm(ps[:, b, 0:GX], btok[:, ch, :], xw[:, n % 2, :], start=True, stop=True).then_inc(filling(st), 1)
                elif k == "cb":
                    _, g, ch = st
                    b = jobs[st][0]
                    if free_before[st]:
                        pe.wait_ge(*emptied(st))
                    mm(ps[:, b, 0:P], xbc[:, g % 2, 0, P * ch:P * ch + P], xbc[:, g % 2, 1, P * ch:P * ch + P], start=True, stop=True).then_inc(filling(st), 1)
                elif k == "seg":
                    pe.wait_ge(rr_done, seg_n[st] + 1)
                    b = jobs[st][0]
                    if free_before[st]:
                        pe.wait_ge(*emptied(st))
                    for i in range(2):
                        ins = mm(ps[:, b + i, 0:GX], (tgt, tlt)[dirs[st[2]]], rr[:, 3 * i:3 * i + 3, :].rearrange("p h l -> p (h l)"),
                                 start=True, stop=True)
                    ins.then_inc(filling(st), 1)
                elif k == "y":
                    _, g, ch = st
                    pe.wait_ge(ent_done, len(STATES) * (g + 1))
                    for d, di in (("f", 0), ("b", 1)):
                        e = entering(d, ch)
                        if e is not None:
                            b = jobs[st + (d,)][0]
                            if free_before[st + (d,)]:
                                pe.wait_ge(*emptied(st + (d,)))
                            mm(ps[:, b, 0:GX], xbc[:, g % 2, 1, P * ch:P * ch + P], hent[:, di, e, :], start=True, stop=True).then_inc(filling(st + (d,)), 1)
                    pe.wait_ge(g_done, 2 * (y_n[st] + 1))
                    b = jobs[st + ("d",)][0]
                    if free_before[st + ("d",)]:
                        pe.wait_ge(*emptied(st + ("d",)))
                    for r in range(R):
                        for di in range(2):
                            ins = mm(ps[:, b, HD * r:HD * r + HD], ey[:, di, r, :], xdt[:, di, ch, HD * r:HD * r + HD], start=(di == 0), stop=(di == 1))
                    ins.then_inc(filling(st + ("d",)), 1)
                elif k == "yt":
                    pe.wait_ge(y_done, y_n[("y",) + st[1:]] + 1)
                    b = jobs[st][0]
                    if free_before[st]:
                        pe.wait_ge(*emptied(st))
                    for i in range(XT):
                        ins = nc.tensor.transpose(ps[:, b, P * i:P * i + P], ycomb[:, 0, P * i:P * i + P], ident)
                    ins.then_inc(filling(st), 1)
                elif k == "ysum":
                    pe.wait_ge(ysq_done, st[1] + 1)
                    b = jobs[st][0]
                    if free_before[st]:
                        pe.wait_ge(*emptied(st))
                    for i in range(XT):
                        for ch in range(NCH):
                            ins = mm(ps[:, b, ch:ch + 1], gate[:, i, P * ch:P * ch + P], ones[:, 0:1], start=(i == 0 and ch == 0),
                                     stop=(i == XT - 1), skip_group_check=True)
                    ins.then_inc(filling(st), 1)
                    n_var += 1
                elif k == "ynorm":
                    pe.wait_ge(rstd_done, n_var)
                    spread(st, NCH)
                elif k == "mlp":
                    L = st[1]
                    ntok = T if L == 0 else SEQ
                    u0, g0 = unit[st], gnum[st]
                    j0 = jobs[st + (B_GEMM[0],)][1], jobs[st + (B_GEMM[1],)][1]
                    base = split_at[("norm", L, "ff")]
                    h0 = 2 + FF_CHUNKS * KT * L
                    if L == 0:
                        if free_before[st + ("mods",)]:
                            pe.wait_ge(*emptied(st + ("mods",)))
                    mods_free0 = freed_by[("mlp", 0, "mods")][1] - FF_CHUNKS
                    with pe.Fori(0, FF_CHUNKS, 1) as cc:
                        n = q = 0
                        for i, (kind, m) in enumerate(mlp_plan(L)):
                            if kind == "mod":
                                bb, j = jobs[st + ("mods",)]
                                if m == 0:
                                    pe.wait_ge(bank_free[bb], mods_free0 + cc * 1)
                                pe.wait_ge(raw_in[(u0 + i) % RAW], 16 * ((u0 + i) // RAW + 1) + cc * (16 * len(mlp_plan(L)) // RAW))
                                for kk in range(KT):
                                    ins = mm(ps[:, bb, 2 * m:2 * m + 2], raw[:, (u0 + i) % RAW, kk, :], silc[:, kk, :],
                                             start=(kk == 0), stop=(kk == KT - 1))
                                ins.then_inc(mod_used, 1)
                                continue
                            b = B_GEMM[n % 2]
                            pe.wait_ge(lo_done, g0 + n + 1 + cc * (2 * KT))
                            if 2 <= n < KT + 2:
                                pe.wait_ge(hr_done, FF_CHUNKS * KT * L + n - 1 + cc * KT)
                            else:
                                pe.wait_ge(h_done, mlp_h[L] + (n - 1 - KT if n >= KT else n - 1) + cc * KT)
                            ready = None
                            if kind == "ff1" and m == 0:
                                ready = split_done, base + 1
                            if kind == "ff2" and m == 0:
                                ready = hid_done, h0 + 1 + cc * KT
                            hi, lo = (a_hi, a_lo) if kind == "ff1" else (b_hi, b_lo)
                            product(ps[:, b, 0:ntok], g0 + n, hi, lo, ntok, ready).then_inc(bank_full[b], 1)
                            n += 1
                elif k == "hstat":
                    ntok = odd_tokens[st[1:]]
                    tile = ktile(*st[1:])[1]
                    n_sq += 1
                    pe.wait_ge(sq_done, n_sq)
                    if qk_n[st[1:]] == 0:
                        if free_before["hstat"]:
                            pe.wait_ge(*emptied("hstat"))
                        pe.wait_ge(c1_in, 16)
                    b = jobs["hstat"][0]
                    for ch in range(ntok // P):
                        col = NQ * ch + 2 * tile if st[1][0] == "q" else 2 * NQ + NKH * ch + 2 * tile
                        ins = mm(ps[:, b, col:col + 2], sq[:, (n_sq - 1) % 2, P * ch:P * ch + P], cuts["half"],
                                 start=(qk_n[st[1:]] == 0 and ch == 0), stop=True, skip_group_check=True)
                    ins.then_inc(sq_used, 1)
                elif k == "hvar":
                    n_var += 1
                elif k == "htr":
                    pe.wait_ge(rstd_done, n_var)
                    b = jobs[st + ("q",)][0]
                    if free_before[st + ("q",)]:
                        pe.wait_ge(*emptied(st + ("q",)))
                    for ch in range(2):
                        ins = nc.tensor.transpose(ps[0:NQ, b, P * ch:P * ch + P], rstd[:, NQ * ch:NQ * ch + NQ], ident)
                    ins.then_inc(filling(st + ("q",)), 1)
                    b = jobs[st + ("k",)][0]
                    if free_before[st + ("k",)]:
                        pe.wait_ge(*emptied(st + ("k",)))
                    for ch in range(NCH):
                        o = 2 * NQ + NKH * ch
                        ins = nc.tensor.transpose(ps[0:NKH, b, P * ch:P * ch + P], rstd[:, o:o + NKH], ident)
                    ins.then_inc(filling(st + ("k",)), 1)
                elif k == "vtok":
                    pe.wait_ge(vT_done, st[1] + 1)
                    b = jobs[st][0]
                    if free_before[st]:
                        pe.wait_ge(*emptied(st))
                    for ch in range(NCH):
                        ins = nc.tensor.transpose(ps[:, b, P * ch:P * ch + P], vT[:, P * ch:P * ch + P], ident)
                    ins.then_inc(filling(st), 1)
                elif k == "hnorm":
                    pe.wait_ge(rT_done, 2)
                    b = jobs[st][0]
                    if free_before[st]:
                        pe.wait_ge(*emptied(st))
                    tile = ktile(*st[1:])[1]
                    if st[1][0] == "q":
                        mm(ps[:, b, 0:SEQ], cuts["selq"][0:NQ, P * tile:P * tile + P], rT[:, :], start=True, stop=True).then_inc(filling(st), 1)
                    else:
                        mm(ps[:, b, :], cuts["selk"][0:NKH, P * tile:P * tile + P], rTk[:, :], start=True, stop=True).then_inc(filling(st), 1)
                elif k == "rot":
                    pe.wait_ge(qn_done, hn_n[("hnorm",) + st[1:]] + 1)
                    b = jobs[st][0]
                    if free_before[st]:
                        pe.wait_ge(*emptied(st))
                    mm(ps[:, b, 0:SEQ], cuts["perm"], ktile(*st[1:])[0][:, 0:SEQ], start=True, stop=True).then_inc(filling(st), 1)
                elif k == "dup":
                    pe.wait_ge(rope_done, len(rot_n))
                    for q in range(2):
                        b = jobs[st + (q,)][0]
                        if free_before[st + (q,)]:
                            pe.wait_ge(*emptied(st + (q,)))
                        mm(ps[:, b, :], cuts[f"dup{q}"], kT[:, 0, :], start=True, stop=True).then_inc(filling(st + (q,)), 1)
                elif k == "attn0":
                    pe.wait_ge(kd_done, 2)
                    pe.wait_ge(qn_done, len(hn_n))
                    pe.wait_ge(bias_done, 2)
                    pe.wait_ge(vtok_done, 5)
                elif k == "S":
                    i = st[1]
                    t, par, qt = ATTN[i]
                    b = jobs[st][0]
                    if free_before[st]:
                        pe.wait_ge(*emptied(st))
                    r0 = HD * par
                    key = kdup[r0:r0 + HD, t // 2, :] if t < 4 else kT[r0:r0 + HD, 1 + t - 4, :]
                    mm(ps[:, b, :], qT[r0:r0 + HD, t, P * qt:P * qt + P], key, start=True, stop=True)
                    if t < 4:
                        o = P * (1 - qt)
                        ins = mm(ps[:, b, o:o + P], ident, cuts["win"][:, P * qt:P * qt + P], start=False, stop=True, skip_group_check=True)
                    else:
                        ins = mm(ps[:, b, 0:SEQ], cuts["flip"], bias[:, qt, 2 * (t - 4) + par, :], start=False, stop=True, skip_group_check=True)
                    ins.then_inc(filling(st), 1)
                elif k == "PT":
                    i = st[1]
                    pe.wait_ge(prob_done, i + 1)
                    b = jobs[st][0]
                    if free_before[st]:
                        pe.wait_ge(*emptied(st))
                    for kk in range(NCH):
                        ins = nc.tensor.transpose(ps[:, b, P * kk:P * kk + P], prob[:, i % 2, P * kk:P * kk + P], ident)
                    ins.then_inc(filling(st), 1)
                elif k == "O":
                    i = st[1]
                    t, par, qt = ATTN[i]
                    pe.wait_ge(pT_done, i + 1)
                    if i % 4 == 0:
                        if free_before[("Opair", t)]:
                            pe.wait_ge(*emptied(("Opair", t)))
                    b = jobs[("Opair", t)][0]
                    col = HD * (t // 2) if t < 4 else P + HD * (2 * (t - 4) + par)
                    for kk in range(NCH):
                        ins = mm(ps[HD * par:HD * par + HD, b, P * qt:P * qt + P], vtok[:, kk, col:col + HD], pT[:, i % 2, P * kk:P * kk + P],
                                 start=(kk == 0), stop=(kk == NCH - 1))
                    ins.then_inc(pv_done, 1)
                elif k == "out":
                    pe.wait_ge(h_done, mlp_h[1] + FF_CHUNKS * KT)
                    for q in range(4):
                        b = jobs[st + (q,)][0]
                        if free_before[st + (q,)]:
                            pe.wait_ge(*emptied(st + (q,)))
                        for i in range(4):
                            f = 4 * (q % 2) + i
                            ins = nc.tensor.transpose(ps[:, b, P * i:P * i + P], hT[:, f, P * (q // 2):P * (q // 2) + P], ident)
                        ins.then_inc(filling(st + (q,)), 1)


_INS = ["x", "c", "ctx", "c_ctx", "w_mod", "b_mod", "norm_mix_g", "norm_ff_g", "w_ff1", "w_ff2", "w_in_even", "conv_w",
        "conv_b", "dt_bias", "a_log", "d_skip", "ssd_norm_g", "w_out_even", "w_in_odd", "q_norm_win", "k_norm_win",
        "sink_win", "q_norm_na", "k_norm_na", "rpb_na", "w_out_odd"]


def kernel(**inputs):
    import numpy as _np
    import concourse.bacc as _bacc
    from concourse import mybir as _mybir
    from concourse.bass_utils import run_bass_kernel_spmd as _run

    nc = _bacc.Bacc("TRN2", target_bir_lowering=False, num_devices=1)
    arrays = {name: _np.ascontiguousarray(inputs[name]) for name in _INS}
    arrays["tables0"], arrays["tables1"] = constants()
    args, maps = [], {}
    for name, a in arrays.items():
        maps[f"in_{name}"] = a
        args.append(nc.dram_tensor(f"in_{name}", a.shape, _mybir.dt.from_np(a.dtype), kind="ExternalInput").ap())
    args.append(nc.dram_tensor("out_0", (1, SEQ, D), _mybir.dt.float32, kind="ExternalOutput").ap())
    trunk(nc, *args)
    r = _run(nc, [maps], core_ids=[0])
    return r.results[0]["out_0"]
```

```python
import math
from contextlib import ExitStack

import concourse.bass as bass
from concourse import mybir
import numpy as np

ALU = mybir.AluOpType
ACT = mybir.ActivationFunctionType
AX = mybir.AxisListType.X
F32 = mybir.dt.float32
F32R = mybir.dt.float32r

P = 128
D = 1024
SEQ = 256
CTX = 256
T = SEQ + CTX
NCH = T // P
KT = D // P
NMOD = 6 * KT
D_FF = 4 * D
EPS = 1e-6
NEG = -1e30
GRID_W = 64

FN_W = 512
FN_T = FN_W // P
G = 4
R = 6
HD = 64
GX = R * HD
XT = GX // P
NS = 128
NH = G * R
INNER = NH * HD
COL_Z = FN_W
COL_X = COL_Z + INNER
COL_B = COL_X + INNER
COL_C = COL_B + G * NS
COL_DT = COL_C + G * NS
CONV_T = (INNER + 2 * G * NS) // P
CONV_W = 5
PADW = SEQ + CONV_W - 1

RING = 4
AHEAD = 2
MB = 4
KQ = 4
MBLOCKS = NMOD // MB
MBLOCKS_FIRST = 2 * KT // MB
FF_CHUNKS = D_FF // D
MODS_LOOP = MBLOCKS // FF_CHUNKS * KQ

B_GEMM = (0, 1)
B_TR = 2
B_AUX = (3, 7)
B_SEG = 4
B_Y = 6

SCAN_F = (2, 3, 0, 1)
SCAN_B = (3, 2, 1, 0)
STATES = [("f", 2), ("b", 3), ("f", 3), ("b", 2), ("f", 0), ("b", 1)]

NQ = 16
NKH = 10
ODD = ([("qn", i, 768 + P * i, SEQ) for i in range(4)] + [("kn", i, 1280 + P * i, T) for i in range(4)]
       + [("qw", i, P * i, SEQ) for i in range(4)] + [("kw", 0, 512, T)]
       + [("v", 0, 640, T)] + [("v", 1 + i, 1792 + P * i, T) for i in range(4)])


def constants():
    j = np.arange(P)[:, None].astype(np.float64)
    i = np.arange(P)[None, :].astype(np.float64)
    ident = (j == i)
    tri = [j <= i, j >= i, j > i, j < i]
    ones = np.ones((P, P))
    w = np.arange(64)
    ang = 2 * np.pi * np.outer(w, w) / 64
    norm = 1.0 / math.sqrt(SEQ * 64)
    dftw = np.zeros((P, 2 * P))
    for b in range(2):
        dftw[64 * b:64 * b + 64, 64 * b:64 * b + 64] = np.cos(ang) * norm
        dftw[64 * b:64 * b + 64, P + 64 * b:P + 64 * b + 64] = np.sin(ang) * norm
    t = np.arange(SEQ)
    angl = 2 * np.pi * (np.outer(t, t) % SEQ) / SEQ
    dfts = np.zeros((P, 2, 2, SEQ))
    for k in range(2):
        dfts[:, k, 0] = np.cos(angl)[k * P:(k + 1) * P]
        dfts[:, k, 1] = -np.sin(angl)[k * P:(k + 1) * P]
    pairs4 = np.zeros((P, 2)); pairs4[[0, 2], 0] = 1; pairs4[[1, 3], 1] = 1
    c0 = np.concatenate([ident] + tri + [ones, dftw, dfts.reshape(P, -1), pairs4], axis=1).astype(np.float32)
    f = (10000.0 ** (-np.arange(16, dtype=np.float32) / 16)).astype(np.float32)
    pos = np.arange(SEQ)
    row, col = (pos // GRID_W).astype(np.float32), (pos % GRID_W).astype(np.float32)
    cos = np.zeros((P, SEQ)); sin = np.zeros((P, SEQ)); perm = np.zeros((P, P))
    for p in range(P):
        d = p % 64
        axis, half, n = d // 32, (d % 32) // 16, d % 16
        a = ((row, col)[axis] * f[n]).astype(np.float32)
        cos[p] = np.cos(a)
        sin[p] = np.sin(a) * (-1 if half == 0 else 1)
        perm[p + (16 if half == 0 else -16), p] = 1.0
    dup = np.zeros((2, P, P))
    for p in range(P):
        dup[0, p % 64, p] = 1.0
        dup[1, 64 + p % 64, p] = 1.0
    heads = (j // 64 == i // 64)
    qq, kk = np.arange(P)[:, None], np.arange(P)[None, :]
    win = np.stack([np.where(kk <= qq, 0, NEG), np.where(kk >= qq, 0, NEG)], 1)
    cs = np.clip((63 - qq % 64) - 8, 0, 64 - 16)
    flip = (j // 64 == i // 64) & (j % 64 == 63 - i % 64)
    u = np.arange(SEQ)[None, :] % 64
    nam = np.where((u >= cs) & (u < cs + 16), 0, NEG)
    c1 = np.concatenate([cos, sin, perm, dup[0], dup[1], heads,
                         win.reshape(P, -1), nam, flip], axis=1).astype(np.float32)
    return c0, c1


ATTN = [(t, par, qt) for t in range(8) for par in range(2) for qt in range(2)]

N_VEC = 16
C0_W = 6 * P + 2 * P + 4 * SEQ + 2
C1_W = 2 * SEQ + 4 * P + 2 * P + SEQ + P


def script():
    s = [("vecs",)]
    pending, due = [], []

    def unit_done():
        for d in due:
            d[0] -= 1
        while due and due[0][0] <= 0:
            s.append(due.pop(0)[1])

    def mods(j, q):
        s.append(("mu", j, q))
        unit_done()
        if q == KQ - 1:
            due.extend([[1, ("mrow", j)], [3, ("mcol", j)]])

    for j in range(MBLOCKS_FIRST):
        for q in range(KQ):
            mods(j, q)
            f = KQ * j + q - 3
            if 0 <= f < KT:
                s.append(("xin", f))
    s.extend(d[1] for d in due)
    due.clear()
    s.append(("norm", 0, "mix"))

    def gemm(kind, i):
        for t in pending:
            s.append(("silu" if ("taps", t) in s else "taps", t))
        s.append(("gemm", kind, i))
        pending[:] = [t for t in pending if ("silu", t) not in s]
        unit_done()
        if kind == "conv":
            pending.append(i)

    rest = [(j, q) for j in range(MBLOCKS_FIRST, MBLOCKS) for q in range(KQ)]
    dft = {2: [("dtraw",)], 3: [("dtcol",)], 4: [("dtcum",)], 6: [("dftw", 0)], 7: [("dfts", 0), ("dftw", 1)], 8: [("dfts", 1), ("dftw", 2)]}
    for n, (kind, t) in enumerate([("conv", t) for t in conv_tiles(0)] + [("fn", t) for t in range(FN_T)]):
        gemm(kind, t)
        for j, q in rest[4 * n:4 * n + 4]:
            mods(j, q)
        s.extend(dft.get(n, []))
    gemm("conv", conv_tiles(1)[0])
    s += [("dfts", 2), ("dftw", 3)]
    gemm("conv", conv_tiles(1)[1])
    s.append(("dfts", 3))
    for g in range(G):
        fill = [("conv", t) for t in conv_tiles(g + 1)[2 * (g == 0):]] if g < G - 1 else []
        fill += [("z", XT * g + i) for i in range(XT)]
        fill += [("outA", m) for m in range(KT)] if g == G - 1 else []
        fill = fill[::-1]

        def some():
            if fill:
                if fill[-1] == ("outA", 0):
                    s.append(("mixsplit", 0))
                gemm(*fill.pop())
        for n, ch in enumerate(SCAN_F):
            s.append(("toks", g, ch))
            if g and n == 1:
                s.append(("ysum", g - 1))
        for d, ch in STATES:
            s.append(("state", g, d, ch))
        if g == G - 1:
            s.append(("ynorm", g - 1))
        for n, ch in enumerate(SCAN_F):
            s.append(("cb", g, ch))
            s.append(("seg", g, "f", ch))
            some()
            if n:
                s.append(("yt", g, SCAN_F[n - 1]))
            s.append(("seg", g, "b", ch))
            some()
            if g and g < G - 1 and n == 0:
                s.append(("ynorm", g - 1))
            s.append(("y", g, ch))
        s.append(("yt", g, SCAN_F[-1]))
        s.append(("ygate", g))
        if g == G - 1:
            some()
            s.append(("ysum", g))
            some()
            s.append(("ynorm", g))
        while fill:
            some()
    s.append(("mixsplit", 1))
    for m in range(KT):
        gemm("outB", m)
    s += [("norm", 0, "ff"), ("mlp", 0), ("norm", 1, "mix")]
    for n, (kind, i, _, _) in enumerate(ODD):
        gemm(kind, i)
        for back, stage in ((1, "hstat"), (2, "hnorm"), (3, "rot")):
            if n >= back:
                o = ODD[n - back][:2]
                if o[0] != "v" and (stage != "rot" or o[0][1] == "w"):
                    s.append((stage,) + o)
        if n >= 14:
            s.append(("vtok", ODD[n - 1][1]))
        if n == 16:
            s.append(("dup",))
    s.append(("vtok", 4))
    s.append(("attn0",))
    n = len(ATTN)
    for j in range(-2, n + 1):
        for kind, i in (("S", j + 2), ("scale", j), ("exp", j + 1), ("PT", j), ("O", j - 1)):
            if 0 <= i < n:
                s.append((kind, i))
                if kind == "O" and i % 4 == 3:
                    s.append(("osplit", i // 4))
    for m in range(KT):
        gemm("outO", m)
    s += [("norm", 1, "ff"), ("mlp", 1), ("out",)]
    return s


def mlp_plan(layer):
    g = [("ff1", m) for m in range(KT)] + [("ff2", m) for m in range(KT)]
    plan = []
    for n, q in enumerate(g):
        plan.append(q)
        if layer == 0 and n < MODS_LOOP:
            plan.append(("mod", n))
    return plan


def conv_tiles(g):
    return [12 + g, 16 + g] + [XT * g + i for i in range(XT)]


def trunk(nc, x, c, ctx, c_ctx, w_mod, b_mod, norm_mix_g, norm_ff_g, w_ff1, w_ff2, w_in_even, conv_w,
          conv_b, dt_bias, a_log, d_skip, ssd_norm_g, w_out_even, w_in_odd, q_norm_win, k_norm_win,
          sink_win, q_norm_na, k_norm_na, rpb_na, w_out_odd, consts0, consts1, out):
    steps = script()

    def tile_of(w, row, col):
        return w[bass.ds(row, D), bass.ds(col, P)].rearrange("(k p) n -> p k n", p=P)

    def mod_tile(layer, row, col):
        return w_mod[layer][bass.ds(row, 2 * P), bass.ds(col, MB * P)].rearrange("(a p) n -> p a n", p=P)

    def mod_view(tiles, slot):
        return tiles[:, slot, :, :].rearrange("p (a b) n -> p a (b n)", a=2)

    def source(kind, i):
        if kind == "fn":
            return tile_of(w_in_even[0], 0, P * i)
        if kind == "z":
            return tile_of(w_in_even[0], 0, COL_Z + P * i)
        if kind == "conv":
            return tile_of(w_in_even[0], 0, COL_X + P * i)
        if kind in ("outA", "outB"):
            return tile_of(w_out_even[0], D * (kind == "outB"), P * i)
        if kind == "outO":
            return tile_of(w_out_odd[0], 0, P * i)
        return tile_of(w_in_odd[0], 0, {o[:2]: o[2] for o in ODD}[(kind, i)])

    unit, jobs, filled_by, freed_by, free_before = {}, {}, {}, {}, {}
    n_gemm = n_aux = n_mod = n_sq = n_var = n_h = n_mix = 0
    seen = {}
    in_full = {b: 0 for b in range(8)}
    in_free = {b: 0 for b in range(8)}
    last = {}
    consumed = []

    def job(key, bank, freed=None, filled=None, n=1):
        if not filled:
            in_full[bank] += n
        if not freed:
            in_free[bank] += n
        jobs[key] = (bank, in_full[bank] - n + 1)
        filled_by[key] = filled or (f"full{bank}", jobs[key][1])
        freed_by[key] = freed or (f"free{bank}", in_free[bank])
        free_before[key] = last.get(bank)
        last[bank] = freed_by[key]

    for st in steps:
        k = st[0]
        nk = seen[k] = seen.get(k, 0) + 1
        if k == "mu":
            if st[2] == 0:
                job(("mrow", st[1]), (B_AUX[1], B_SEG)[st[1] % 2], filled=("mu_used", KQ * (st[1] + 1)), freed=("row_done", st[1] + 1))
            unit[st] = len(consumed)
            n_mod += 1
            consumed.append(("mu_used", n_mod))
        elif k == "mcol":
            job(st, B_TR, filled=("mcol_done", st[1] + 1), freed=("modc_done", st[1] + 1))
        elif k == "gemm":
            unit[st] = len(consumed)
            kind = {"fn": "uf_done", "conv": "pad_done", "z": "gate_done", "v": "vT_done"}.get(st[1])
            if kind:
                nk = seen[kind] = seen.get(kind, 0) + 1
            elif st[1][:3] == "out":
                kind, nk = "h_done", n_h + 1
                n_h += 1
            else:
                kind, nk = "sq_done", n_sq + 1
                n_sq += 1
            b = B_GEMM[n_gemm % 2]
            job(st, b, freed=(kind, nk))
            consumed.append(filled_by[st])
            n_gemm += 1
        elif k == "mlp":
            unit[st] = len(consumed)
            assert n_gemm % 2 == 0
            n_h += FF_CHUNKS * KT
            for i, b in enumerate(B_GEMM):
                job(st + (b,), b, freed=("h_done", n_h - 1 + i), n=FF_CHUNKS * KT)
            if st[1] == 0:
                job(st + ("mrow",), B_AUX[1], filled=("mu_used", 2 * MBLOCKS * KQ), freed=("row_done", 2 * MBLOCKS))
                job(st + ("mcol",), B_TR, filled=("mcol_done", 2 * MBLOCKS), freed=("modc_done", 2 * MBLOCKS))
                n_mod += MBLOCKS * KQ
            consumed += [None] * (FF_CHUNKS * len(mlp_plan(st[1])) - 4) + [(f"full{b}", in_full[b] - i) for i in (1, 0) for b in B_GEMM]
        elif k == "vecs":
            for q in range(4):
                job(st + (q,), B_TR, freed=("vt_done", 4) if q == 3 else None)
        elif k == "xin":
            n_h += 1
            job(st, (B_TR, B_Y)[st[1] % 2], freed=("h_done", n_h))
        elif k == "norm":
            n_sq += 1
            n_var += 1
            job(st, B_AUX[0], freed=("var_done", n_var))
        elif k == "dtraw":
            job(st, B_AUX[0], freed=("dtrow_done", 1))
        elif k == "dtcol":
            job(st, B_AUX[0], freed=("dtv_done", 1))
        elif k == "dtcum":
            job(st, B_AUX[0], freed=("dtx_done", 2))
            job(st + ("tot",), B_AUX[0], freed=("dtx_done", 3))
        elif k == "dftw":
            for q in range(2):
                job(st + (q,), B_AUX[0], freed=("vf_done", 2 * st[1] + q + 1))
        elif k == "dfts":
            n_mix += 1
            job(st, B_TR, freed=("mix_done", n_mix))
        elif k == "toks":
            job(st, (B_TR, B_Y)[nk % 2], freed=("xdt_done", nk))
        elif k == "yt":
            job(st, B_TR)
        elif k == "ynorm":
            n_mix += XT
        elif k == "vtok":
            job(st, B_TR, freed=("vtok_done", nk))
        elif k in ("state", "cb", "ysum", "hstat"):
            n_var += k in ("ysum", "hstat")
            job(st, B_AUX[n_aux % 2], freed={"state": ("ent_done", nk), "ysum": ("var_done", n_var),
                                             "hstat": ("var_done", n_var)}.get(k))
            n_aux += 1
        elif k == "seg":
            job(st, B_SEG, freed=("seg_done", nk))
        elif k == "y":
            job(st + ("d",), B_Y, freed=("y_done", nk))
            for q, none in (("f", SCAN_F[0]), ("b", SCAN_B[0])):
                if st[2] != none:
                    job(st + (q,), B_AUX[n_aux % 2])
                    n_aux += 1
        elif k == "rot":
            job(st, B_Y)
        elif k == "dup":
            job(st + (0,), B_TR, freed=("kd_done", 1))
            job(st + (1,), B_TR, freed=("kd_done", 2))
        elif k == "S":
            job(st, B_GEMM[st[1] % 2])
        elif k == "PT":
            job(st, B_AUX[0] if st[1] % 2 else B_SEG, freed=("pT_done", st[1] + 1))
        elif k == "O" and st[1] % 4 == 0:
            t = st[1] // 4
            job(("Opair", t), (B_Y, B_AUX[1])[t % 2], freed=("split_done", 5 * KT + t + 1), filled=("pv_done", 4 * t + 4))
        elif k == "out":
            for q in range(4):
                job(st + (q,), (B_TR, B_Y)[q % 2], freed=(("finv_done", "fin_done")[q % 2], q // 2 + 1))
    steps_of = lambda kind: [q for q in steps if q[0] == kind]
    gemms = steps_of("gemm")
    order = [q for q in steps if q[0] in ("mu", "gemm", "mlp")]
    with ExitStack() as stack:
        at = [16512]

        def place(name, shape, dt=F32, offset=None):
            size = 4 * int(np.prod(shape[1:]))
            if offset is None:
                offset = at[0]
                at[0] += (size + 31) // 32 * 32
            assert offset + size <= 229344, (name, offset, size)
            return nc.alloc_sbuf_tensor_at(name, shape, dt, offset=offset)

        hT = place("hT", [P, KT, T])
        a_hi = place("a_hi", [P, KT, T], F32R)
        a_lo = place("a_lo", [P, KT, T], F32R)
        raw_at = at[0]
        raw = place("raw", [P, RING, KT, P])
        w_hi = place("w_hi", [P, RING, KT, P], F32R)
        w_lo = place("w_lo", [P, RING, KT, P], F32R, offset=raw_at)
        c0 = place("c0", [P, C0_W])
        vt = place("vt", [P, 3, P])
        bc = place("bc", [P, P])
        mod = place("mod", [P, 2, NMOD, 2])
        coefA = place("coefA", [P, KT, 2])
        silc = place("silc", [P, KT, 2])
        sil4 = place("sil4", [P, KT, 4], F32R)
        mrow = place("mrow", [4, MB * P])
        dsk = place("dsk", [P, NH // 2])
        nega = place("nega", [P, 2 * NH])
        eps = place("eps", [P, 8])
        out_at = at[0]
        mixF = place("mixF", [P, 2 * KT, T])
        region = at[0]
        b_hi = place("b_hi", [P, KT, T], F32R)
        b_lo = place("b_lo", [P, KT, T], F32R)
        sq = place("sq", [P, 2, T])
        nt = place("nt", [P, 2, T])
        u32 = place("u32", [P, 2, T])
        hr = place("hr", [P, 2, T])
        hq = place("hq", [P, 2, T])
        top = at[0]
        vrow = place("vrow", [P, 3, P], offset=out_at)
        rowv = place("rowv", [1, P], offset=out_at + 1536)
        sct = place("sct", [P, KT, 2], offset=out_at + 2048)
        xload = place("xload", [P, NCH, D], offset=out_at + 4096)
        at[0] = region
        xbc = place("xbc", [P, 2, 5, T])
        gate = place("gate", [P, XT, T])
        btok = place("btok", [P, NCH, NS])
        xdt = place("xdt", [P, 2, NCH, GX])
        xw = place("xw", [P, 2, GX])
        hent = place("hent", [P, 2, NCH - 1, GX])
        ey = place("ey", [P, 2, R, P])
        rr = place("rr", [P, R, P])
        cbm = place("cbm", [P, 2, P])
        ycomb = place("ycomb", [P, 2, GX])
        cpad = place("cpad", [P, 2, 2, PADW])
        cacc = place("cacc", [P, 2, T])
        cth = place("cth", [P, T])
        dts = {n: place("dt_" + n, [P, NCH, 2 * NH]) for n in ("dt", "dta", "ea", "dte", "tot")}
        zt = place("zt", [P, T])
        o = out_at + 4096 + 4 * NCH * D
        wdt = place("wdt", [P, KT, 2 * NH], offset=o)
        wdt_hi = place("wdt_hi", [P, KT, 2 * NH], F32R, offset=o + 1536)
        wdt_lo = place("wdt_lo", [P, KT, 2 * NH], F32R, offset=o + 3072)
        dtrow = place("dtrow", [2 * NH, T], offset=o + 6912)
        dts["tmp"] = place("dt_tmp", [P, NCH, 2 * NH], offset=o + 4608)
        dts["t2"] = place("dt_t2", [P, NCH, 2 * NH], offset=o + 5376)
        dts["t3"] = place("dt_t3", [P, NCH, 2 * NH], offset=o + 6144)
        o = region + 2 * 5 * T * 4 + XT * T * 4 + NCH * NS * 4
        uf = place("uf", [P, 2, T], offset=o)
        vf = place("vf", [P, NCH, 2 * P], offset=o + 4096)
        at[0] = out_at
        c1 = place("c1", [P, C1_W])
        qT = place("qT", [P, 8, SEQ])
        kT = place("kT", [P, 5, T])
        kdup = place("kdup", [P, 2, T])
        vtok = place("vtok", [P, NCH, 5 * P])
        at[0] = max(at[0], region + 2 * 16384)
        at[0] = max(at[0], top)
        vT = place("vT", [P, T])
        rp = place("rp", [P, 2, SEQ])
        sm = place("sm", [P, 8, 2])
        bias = place("bias", [P, 2, 8, SEQ], offset=region + 16384)
        prob = place("prob", [P, 2, T], offset=region + 32768 + 4096)
        pT = place("pT", [P, 2, T], offset=region + 32768 + 8192)
        fin = place("fin", [P, 2, D], offset=out_at)

        ident, tle, tge, tgt, tlt, ones = (c0[:, P * i:P * i + P] for i in range(6))
        pairs4 = c0[0:4, C0_W - 2:C0_W]
        dftw = c0[:, 6 * P:8 * P]
        dfts = c0[:, 8 * P:8 * P + 4 * SEQ].rearrange("p (k c l) -> p k c l", k=2, c=2)
        cw = 0
        cuts = {}
        for name, w in (("cos", SEQ), ("sin", SEQ), ("perm", P), ("dup0", P), ("dup1", P), ("heads", P),
                        ("win", 2 * P), ("nam", SEQ), ("flip", P)):
            cuts[name] = c1[:, cw:cw + w]
            cw += w
        bmod1 = vt[:, 0, NMOD:2 * NMOD]
        bmodT = vt[:, 0, 0:2 * NMOD].rearrange("p (l f) -> p l f", l=2)
        gmixT = vt[:, 0, 96:112].rearrange("p (l f) -> p l f", l=2)
        gffT = vt[:, 0, 112:128].rearrange("p (l f) -> p l f", l=2)
        convwT = vt[:, 1, 0:100].rearrange("p (k t) -> p k t", k=CONV_W)
        convbT = vt[:, 1, 100:120]
        gssdT = vt[:, 2, 0:12]
        g_q = {"qw": 28, "kw": 29, "qn": 30, "kn": 31}

        ps = stack.enter_context(nc.psum_tensor("ps", [P, 8, 512], F32))
        sem = lambda n: stack.enter_context(nc.semaphore(n))
        bank_full = [sem(f"bank_full{b}") for b in range(8)]
        bank_free = [sem(f"bank_free{b}") for b in range(8)]
        raw_in = [sem(f"raw_in{i}") for i in range(RING)]

        names = ("dtrow_done acc_sq tmp_sq mu_used row_done mcol_done modc_done sil4_done hi_done lo_done c0_in c1_in vec_in wdt_in bias_in dve_seq act_seq consts_set vt_done "
                 "silc_done th0_done h_done sq_done var_done rstd_done nt_done u_done split_done coef_done "
                 "wdthi_done wdtlo_done dtv_done dte_done dtln_done dt_done dtx_done uf_done vf_done pad_done acc_done "
                 "th_done xbc_done xdt_done xw_done ent_done rr_done seg_done g_done y_done zt_done gate_done gated "
                 "ysq_done mix_done mixhi_done hr_done hq_done hidhi_done hid_done qraw_done qn_done rope_done "
                 "vT_done vtok_done kd_done bias_done max_done exp_done rs_done prob_done pT_done pv_done ohi_done "
                 "fin_done finv_done out_in").split()
        S = {n: sem(n) for n in names}
        (dtrow_done, acc_sq, tmp_sq, mu_used, row_done, mcol_done, modc_done, sil4_done, hi_done, lo_done, c0_in, c1_in, vec_in, wdt_in, bias_in, dve_seq, act_seq,
         consts_set, vt_done, silc_done, th0_done, h_done, sq_done, var_done, rstd_done, nt_done,
         u_done, split_done, coef_done, wdthi_done, wdtlo_done, dtv_done, dte_done, dtln_done, dt_done, dtx_done,
         uf_done, vf_done, pad_done, acc_done, th_done, xbc_done, xdt_done, xw_done, ent_done, rr_done, seg_done,
         g_done, y_done, zt_done, gate_done, gated, ysq_done, mix_done, mixhi_done, hr_done, hq_done, hidhi_done,
         hid_done, qraw_done, qn_done, rope_done, vT_done, vtok_done, kd_done, bias_done, max_done,
         exp_done, rs_done, prob_done, pT_done, pv_done, ohi_done, fin_done, finv_done, out_in) = (S[n] for n in names)
        x_in = [sem(f"x_in{t}") for t in range(NCH)]

        def signalled(what):
            return S[what] if what in S else (bank_full if what[:4] == "full" else bank_free)[int(what[-1])]

        def filled(key):
            what, n = filled_by[key]
            return signalled(what), n

        def emptied(key):
            what, n = free_before[key]
            return signalled(what), n

        def filling(key):
            return bank_full[jobs[key][0]]

        def ledger():
            counts, last_result = {}, []

            def signal(s_):
                counts[s_] = counts.get(s_, 0) + 1
                last_result[:] = [s_, counts[s_]]
                return s_

            def freeing(key):
                what, n = freed_by[key]
                last_result[:] = [signalled(what), n]
                return signalled(what)

            def latest():
                return tuple(last_result)
            return signal, freeing, latest, counts

        odd_tokens = {o[:2]: o[3] for o in ODD}

        def tokens(st):
            return odd_tokens.get(st[1:], SEQ if st[1] == "outO" else T)

        norms = steps_of("norm")
        norm_n = {st: i for i, st in enumerate(norms)}
        h_before = {("norm", 0, "mix"): KT, ("norm", 0, "ff"): 3 * KT,
                    ("norm", 1, "mix"): (3 + FF_CHUNKS) * KT, ("norm", 1, "ff"): (4 + FF_CHUNKS) * KT}
        mlp_h = {0: 3 * KT, 1: (4 + FF_CHUNKS) * KT}
        count = lambda kind, which=None: {q: i for i, q in enumerate([q for q in steps if q[0] == kind and (which is None or q[1] in which)])}
        conv_n, z_n = count("gemm", ("conv",)), count("gemm", ("z",))
        tok_n, seg_n, st_n, y_n = count("toks"), count("seg"), count("state"), count("y")
        seg_l, st_l = steps_of("seg"), steps_of("state")
        qk_n = {q[1:]: i for q, i in count("gemm", ("qn", "kn", "qw", "kw")).items()}
        hn_n, rot_n = count("hnorm"), count("rot")
        cb_n, hstats = count("cb"), steps_of("hstat")
        dirs = {"f": 0, "b": 1}
        scans = {"f": SCAN_F, "b": SCAN_B}
        rms_n = {q: i + 1 for i, q in enumerate([q for q in steps if q[0] in ("norm", "ysum", "hstat")])}
        split_at = {("norm", 0, "mix"): 0, ("mixsplit", 0): KT, ("mixsplit", 1): 2 * KT,
                    ("norm", 0, "ff"): 3 * KT, ("norm", 1, "mix"): 4 * KT, "attn": 5 * KT, ("norm", 1, "ff"): 6 * KT}
        starts = {gemms[0]: 0, ("gemm", "outA", 0): KT, ("gemm", "outB", 0): 2 * KT,
                  ("gemm", ODD[0][0], ODD[0][1]): 4 * KT, ("gemm", "outO", 0): 5 * KT}
        reader = {("mixsplit", 0): ("gemm", "z", G * XT - 1), ("norm", 0, "ff"): ("gemm", "outA", KT - 1),
                  ("norm", 1, "mix"): ("mlp", 0), "attn": ("gemm", "v", 4), ("norm", 1, "ff"): ("gemm", "outO", KT - 1)}

        def readers(st):
            r = reader.get(st)
            if r and r[0] == "mlp":
                return [(bank_full[b], jobs[r + (b,)][1] - 1 + FF_CHUNKS * KT) for b in B_GEMM]
            return [filled(r)] if r else []

        def entering(d, ch):
            i = scans[d].index(ch) - 1
            return None if i < 0 else i

        def y_jobs(g, ch):
            return [("y", g, ch, q) for q in "dfb" if ("y", g, ch, q) in jobs]

        def rms_of(st):
            if st[0] == "norm":
                return sq[:, 0, 0:SEQ] if st == ("norm", 1, "ff") else sq[:, 0, :]
            if st[0] == "ysum":
                return gate[:, 0, :]
            return nt[:, qk_n[st[1:]] % 2, 0:odd_tokens[st[1:]]]

        def ktile(kind, i):
            if kind[0] == "q":
                return qT[:, i + 4 * (kind == "qn"), :]
            return kT[:, i + (kind == "kn"), :]

        def slot_free(u):
            what, n = consumed[u - RING]
            return signalled(what), n

        def loop_slot_free(st, plan, i):
            k, back = (i - RING, 0) if i >= RING else (i - RING + len(plan), 1)
            kind, m = plan[k]
            if kind == "mod":
                return mu_used, MBLOCKS * KQ + m + 1 - back * MODS_LOOP, MODS_LOOP
            b, first = jobs[st + (B_GEMM[m % 2],)]
            return bank_full[b], first + (m + KT * (kind == "ff2")) // 2 - back * KT, KT

        heads = lambda ap: ap.rearrange("p (r d) -> p r d", r=R)

        block = stack.enter_context(nc.Block())

        @block.sync
        def _(sp):
            vec = [(vrow[0:96, 0, :], b_mod.rearrange("l (f p) -> (l f) p", p=P)),
                   (vrow[96:112, 0, :], norm_mix_g.rearrange("l (f p) -> (l f) p", p=P)),
                   (vrow[112:128, 0, :], norm_ff_g.rearrange("l (f p) -> (l f) p", p=P)),
                   (vrow[0:100, 1, :], conv_w[0].rearrange("k (t p) -> (k t) p", p=P)),
                   (vrow[100:120, 1, :], conv_b[0].rearrange("(t p) -> t p", p=P)),
                   (vrow[0:12, 2, :], ssd_norm_g[0].rearrange("(t p) -> t p", p=P)),
                   (vrow[12:20, 2, :], c.rearrange("b (t p) -> (b t) p", p=P)),
                   (vrow[20:28, 2, :], c_ctx.rearrange("(t p) -> t p", p=P)),
                   (rowv[:, 0:48], a_log.rearrange("a b c -> a (b c)")),
                   (rowv[:, 48:96], dt_bias.rearrange("a b c -> a (b c)")),
                   (rowv[:, 96:120], d_skip), (rowv[:, 120:128], sink_win)]
            for n, g in enumerate((q_norm_win, k_norm_win, q_norm_na, k_norm_na)):
                vec.append((vrow[28 + n:29 + n, 2, :].rearrange("o (i d) -> o i d", i=2), g.unsqueeze(1).broadcast_to([1, 2, HD])))
            assert len(vec) == N_VEC
            sp.dma_start(c0[:, :], consts0).then_inc(c0_in, 16)
            for dst, src in vec:
                sp.dma_start(dst, src).then_inc(vec_in, 16)

            def load(u, src):
                if u >= RING:
                    sp.wait_ge(*slot_free(u))
                dst = raw[:, u % RING, :, :] if src.shape[1] == KT else mod_view(raw, u % RING)
                sp.dma_start(dst, src).then_inc(raw_in[u % RING], 16)

            for st in steps:
                if st[0] == "mu":
                    _, j, q = st
                    load(unit[st], mod_tile(0, 2 * P * q, MB * P * j))
                elif st == ("xin", 0):
                    for t in range(NCH):
                        src = (x, ctx)[t // 2][0, P * (t % 2):P * (t % 2) + P, :]
                        sp.dma_start(xload[:, t, :], src).then_inc(x_in[t], 16)
                elif st[0] == "dtraw":
                    sp.dma_start(wdt[:, :, :], w_in_even[0][:, COL_DT:COL_DT + 2 * NH].rearrange("(k p) n -> p k n", p=P))\
                        .then_inc(wdt_in, 16)
                elif st[0] == "gemm":
                    load(unit[st], source(st[1], st[2]))
                    if st[1] in ("qn", "kn"):
                        for last_read in readers(("norm", 1, "mix")):
                            sp.wait_ge(*last_read)
                        at_ = qk_n[st[1:]]
                        for r, kr in ((at_ // 2, 2 * (at_ % 2)), (at_ // 2, 2 * (at_ % 2) + 1)):
                            src = bass.AP(tensor=rpb_na.tensor, offset=rpb_na.offset + (kr - r + 7) * 31 + 15 - 63,
                                          ap=[[1, 64], [465, 8], [1, 64]])
                            dst = bias[64 * (r % 2):64 * (r % 2) + 64, r // 2, :, 64 * kr:64 * kr + 64]
                            sp.dma_start(dst, src).then_inc(bias_in, 16)
                elif st == ("norm", 0, "ff"):
                    sp.wait_ge(split_done, split_at[("mixsplit", 1)] + KT)
                    sp.dma_start(c1[:, :], consts1).then_inc(c1_in, 16)
                elif st[0] == "mlp":
                    L = st[1]
                    u0, plan = unit[st], mlp_plan(L)
                    with sp.Fori(0, FF_CHUNKS, 1) as cc:
                        for i, (kind, m) in enumerate(plan):
                            s_, first, step = loop_slot_free(st, plan, i)
                            sp.wait_ge(s_, first + cc * step)
                            slot = (u0 + i) % RING
                            if kind == "mod":
                                src = mod_tile(1, 2 * P * (m % KQ), cc * (MODS_LOOP // KQ * MB * P) + MB * P * (m // KQ))
                                sp.dma_start(mod_view(raw, slot), src).then_inc(raw_in[slot], 16)
                            else:
                                src = tile_of(w_ff1[L], 0, cc * D + P * m) if kind == "ff1" else tile_of(w_ff2[L], cc * D, P * m)
                                sp.dma_start(raw[:, slot, :, :], src).then_inc(raw_in[slot], 16)
            sp.wait_ge(fin_done, 2)
            sp.wait_ge(finv_done, 2)
            sp.dma_start(out[0].rearrange("(t p) d -> p t d", p=P), fin[:, :, :]).then_inc(out_in, 16)
            sp.wait_ge(out_in, 16)

        @block.gpsimd
        def _(pool):
            pool.memset(eps[:, :], EPS).then_inc(consts_set, 1)
            pool.memset(cpad[:, :, :, :], 0.0).then_inc(consts_set, 1)
            n_acc = n_tmp = 0
            for st in steps:
                if st[0] == "norm":
                    ntok = SEQ if st == ("norm", 1, "ff") else T
                    acc, tmp = sq[:, 0, 0:ntok], nt[:, 0, 0:ntok]
                    for f in range(KT - 1):
                        hs = hT[:, f, 0:ntok]
                        pool.wait_ge(h_done, h_before[st] - KT + f + 1)
                        if f:
                            pool.wait_ge(acc_sq, n_acc)
                            pool.tensor_tensor(tmp, hs, hs, ALU.mult).then_inc(tmp_sq, 1)
                            n_tmp += 1
                            pool.wait_ge(tmp_sq, n_tmp)
                            pool.tensor_tensor(acc, acc, tmp, ALU.add).then_inc(acc_sq, 1)
                        else:
                            pool.tensor_tensor(acc, hs, hs, ALU.mult).then_inc(acc_sq, 1)
                        n_acc += 1
                elif st == ("dup",):
                    pool.wait_ge(bias_in, 16 * 16)
                    pool.wait_ge(c1_in, 16)
                    for qt in range(2):
                        pool.tensor_tensor(bias[:, qt, :, :], bias[:, qt, :, :], cuts["nam"][:, None, :].broadcast_to([P, 8, SEQ]),
                                           ALU.add).then_inc(bias_done, 1)
                elif st[0] == "state":
                    _, g, d, ch = st
                    n, di = st_n[st], dirs[d]
                    pool.wait_ge(xdt_done, tok_n[("toks", g, SCAN_F[-1])] + 1)
                    pool.wait_ge(dtx_done, 3)
                    if n >= 2:
                        pool.wait_ge(*filled(st_l[n - 2]))
                    pool.tensor_tensor(heads(xw[:, n % 2, :]), heads(xdt[:, di, ch, :]),
                                       dts["dte"][:, ch, NH * di + R * g:NH * di + R * g + R].unsqueeze(2).broadcast_to([P, R, HD]),
                                       ALU.mult).then_inc(xw_done, 1)
                elif st[0] == "seg":
                    _, g, d, ch = st
                    n, di = seg_n[st], dirs[d]
                    if n == 0:
                        pool.wait_ge(dt_done, 1)
                        pool.wait_ge(c0_in, 16)
                    else:
                        pool.wait_ge(*filled(seg_l[n - 1]))
                    pool.tensor_tensor(rr[:, :, :],
                                       dts["dta"][:, ch, NH * di + R * g:NH * di + R * g + R].unsqueeze(2).broadcast_to([P, R, P]),
                                       (tle, tge)[di][:, None, :].broadcast_to([P, R, P]), ALU.mult).then_inc(rr_done, 1)

        @block.scalar
        def _(act):
            signal, freeing, latest, counts = ledger()

            def high(u, passes=0):
                act.wait_ge(raw_in[u % RING], 16 * (u // RING + 1) + passes)
                nc.scalar.activation(w_hi[:, u % RING, :, :], raw[:, u % RING, :, :], ACT.Copy).then_inc(hi_done, 1)

            for st in steps:
                k = st[0]
                if k == "vecs":
                    act.wait_ge(vt_done, 3)
                    nc.scalar.activation(sct[:, :, :], vt[:, 2, 12:28].rearrange("p (s t) -> p t s", s=2), ACT.Tanh,
                                             scale=0.5).then_inc(signal(th0_done), 1)
                    act.wait_ge(vt_done, 4)
                    nc.scalar.activation(nega[:, :], bc[:, 0:48], ACT.Exp).then_inc(signal(th0_done), 1)
                elif k == "norm":
                    ntok = SEQ if st == ("norm", 1, "ff") else T
                    act.wait_ge(h_done, h_before[st])
                    nc.scalar.activation(sq[:, 1, 0:ntok], hT[:, KT - 1, 0:ntok], ACT.Square).then_inc(signal(sq_done), 1)
                    b = jobs[st][0]
                    act.wait_ge(consts_set, 2)
                    act.wait_ge(*filled(st))
                    nc.scalar.activation(rms_of(st), ps[:, b, 0:ntok], ACT.Sqrt, scale=1.0 / D, bias=eps[:, 0:1]).then_inc(signal(var_done), 1)
                    act.wait_ge(coef_done, norm_n[st] + 1)
                    for last_read in readers(st):
                        act.wait_ge(*last_read)
                    for f in range(KT):
                        n = KT * norm_n[st] + f
                        act.wait_ge(nt_done, n + 1)
                        if n >= 2:
                            act.wait_ge(split_done, split_at[st] + f - 1 if f >= 2 else split_at[norms[norm_n[st] - 1]] + KT - 1 + f)
                        sh = f + (0 if st[2] == "mix" else 3 * KT)
                        for i in range(ntok // SEQ):
                            nc.scalar.activation(u32[:, f % 2, SEQ * i:SEQ * i + SEQ], nt[:, f % 2, SEQ * i:SEQ * i + SEQ],
                                                     ACT.Identity, bias=mod[:, st[1], sh, i:i + 1], scale=coefA[:, f, i:i + 1]).then_inc(signal(act_seq), 1)
                        act.wait_ge(*latest())
                        nc.scalar.activation(a_hi[:, f, 0:ntok], u32[:, f % 2, 0:ntok], ACT.Copy).then_inc(signal(u_done), 1)
                elif k == "dtraw":
                    act.wait_ge(wdt_in, 16)
                    nc.scalar.activation(wdt_hi[:, :, :], wdt[:, :, :], ACT.Copy).then_inc(signal(wdthi_done), 1)
                elif k == "dtcol":
                    act.wait_ge(dtv_done, 1)
                    nc.scalar.activation(dts["t2"][:, :, :], dts["tmp"][:, :, :], ACT.Abs).then_inc(signal(act_seq), 1)
                    act.wait_ge(*latest())
                    nc.scalar.activation(dts["t3"][:, :, :], dts["t2"][:, :, :], ACT.Exp, scale=-1.0).then_inc(signal(dte_done), 1)
                    act.wait_ge(*latest())
                    nc.scalar.activation(dts["ea"][:, :, :], dts["t3"][:, :, :], ACT.Ln, bias=1.0).then_inc(signal(dtln_done), 1)
                elif k == "dtcum":
                    b = jobs[st][0]
                    act.wait_ge(*filled(st))
                    nc.scalar.activation(dts["ea"][:, :, :], ps[:, b, 0:192].rearrange("p (c h) -> p c h", c=NCH), ACT.Exp).then_inc(signal(dtx_done), 1)
                    nc.scalar.activation(dts["dte"][:, :, :], ps[:, b, 192:384].rearrange("p (c h) -> p c h", c=NCH), ACT.Exp).then_inc(signal(dtx_done), 1)
                    b = jobs[st + ("tot",)][0]
                    act.wait_ge(*filled(st + ("tot",)))
                    nc.scalar.activation(dts["tot"][:, :, :], ps[:, b, 0:192].rearrange("p (c h) -> p c h", c=NCH), ACT.Exp).then_inc(signal(dtx_done), 1)
                elif k == "mu":
                    if st == order[0]:
                        for u in range(AHEAD):
                            high(u)
                    high(unit[st] + AHEAD)
                elif k == "mrow":
                    j = st[1]
                    if j >= 1:
                        act.wait_ge(mcol_done, j)
                    b = jobs[st][0]
                    act.wait_ge(*filled(st))
                    nc.scalar.activation(mrow[:, :], ps[0:4, b, :], ACT.Copy).then_inc(signal(row_done), 1)
                elif k == "gemm":
                    high(unit[st] + AHEAD)
                    b, _ = jobs[st]
                    if st[1] == "conv":
                        n = conv_n[st]
                        if n == 0:
                            act.wait_ge(consts_set, 2)
                        if n >= 2:
                            act.wait_ge(acc_done, n - 1)
                        act.wait_ge(*filled(st))
                        nc.scalar.activation(cpad[:, n % 2, :, 2:2 + SEQ], ps[:, b, :].rearrange("p (s t) -> p s t", s=2), ACT.Copy).then_inc(signal(pad_done), 1)
                    elif st[1] == "z":
                        n = z_n[st]
                        act.wait_ge(*filled(st))
                        if n >= 1:
                            act.wait_ge(gate_done, n)
                        nc.scalar.activation(zt[:, :], ps[:, b, :], ACT.Tanh, scale=0.5).then_inc(signal(zt_done), 1)
                    elif st[1] in ("qn", "kn", "qw", "kw"):
                        ntok = tokens(st)
                        act.wait_ge(*filled(st))
                        nc.scalar.activation(ktile(*st[1:]), ps[:, b, 0:ntok], ACT.Copy).then_inc(signal(qraw_done), 1)
                        n_sq = qk_n[st[1:]]
                        if n_sq >= 2:
                            act.wait_ge(*filled(hstats[n_sq - 2]))
                        nc.scalar.activation(sq[:, n_sq % 2, 0:ntok], ps[:, b, 0:ntok], ACT.Square).then_inc(signal(sq_done), 1)
                    elif st[1] == "v":
                        act.wait_ge(*filled(st))
                        if st[2] >= 1:
                            act.wait_ge(*filled(("vtok", st[2] - 1)))
                        nc.scalar.activation(vT[:, :], ps[:, b, :], ACT.Copy).then_inc(signal(vT_done), 1)
                elif k == "silu":
                    n = conv_n[("gemm", "conv", st[1])]
                    act.wait_ge(acc_done, n + 1)
                    if n >= 1:
                        act.wait_ge(xbc_done, n)
                    nc.scalar.activation(cth[:, :], cacc[:, n % 2, :], ACT.Tanh).then_inc(signal(th_done), 1)
                elif k == "vtok":
                    b = jobs[st][0]
                    act.wait_ge(*filled(st))
                    nc.scalar.activation(vtok[:, :, P * st[1]:P * st[1] + P], ps[:, b, :].rearrange("p (c d) -> p c d", c=NCH), ACT.Copy).then_inc(signal(vtok_done), 1)
                elif k == "seg":
                    n, di = seg_n[st], dirs[st[2]]
                    if n >= 2:
                        act.wait_ge(*filled(("y", seg_l[n - 2][1], seg_l[n - 2][3], "d")))
                    b = jobs[st][0]
                    act.wait_ge(*filled(st))
                    nc.scalar.activation(ey[:, di, :, :].rearrange("p (a h) l -> p a (h l)", a=2), ps[:, b:b + 2, 0:GX], ACT.Exp).then_inc(signal(seg_done), 1)
                elif k == "ygate":
                    g = st[1]
                    act.wait_ge(gated, g + 1)
                    nc.scalar.activation(gate[:, :, :], mixF[:, FN_T + XT * g:FN_T + XT * g + XT, :], ACT.Square).then_inc(signal(ysq_done), 1)
                elif k == "ysum":
                    b = jobs[st][0]
                    act.wait_ge(*filled(st))
                    nc.scalar.activation(rms_of(st), ps[:, b, :], ACT.Sqrt, scale=0.25 / GX, bias=eps[:, 0:1]).then_inc(signal(var_done), 1)
                elif k == "hstat":
                    if qk_n[st[1:]] >= 2:
                        act.wait_ge(qn_done, qk_n[st[1:]] - 1)
                    b = jobs[st][0]
                    act.wait_ge(*filled(st))
                    nc.scalar.activation(rms_of(st), ps[:, b, 0:odd_tokens[st[1:]]], ACT.Sqrt, scale=1.0 / HD,
                                         bias=eps[:, 0:1]).then_inc(signal(var_done), 1)
                elif k == "mixsplit":
                    hi = (a_hi, b_hi)[st[1]]
                    for last_read in readers(st):
                        act.wait_ge(*last_read)
                    for f in range(KT):
                        t = KT * st[1] + f
                        act.wait_ge(mix_done, t + 1)
                        if st[1] == 1 and f == 0:
                            act.wait_ge(mix_done, 2 * KT)
                            for q in y_jobs(G - 1, SCAN_F[-1]):
                                act.wait_ge(*filled(q))
                        nc.scalar.activation(hi[:, f, :], mixF[:, t, :], ACT.Copy).then_inc(signal(mixhi_done), 1)
                elif k == "mlp":
                    L = st[1]
                    ntok = T if L == 0 else SEQ
                    j0 = jobs[st + (B_GEMM[0],)][1], jobs[st + (B_GEMM[1],)][1]
                    u0, plan = unit[st], mlp_plan(L)

                    def one_pass(cc, last):
                        n = 0
                        for i, (kind, m) in enumerate(plan):
                            if not (last and i >= len(plan) - AHEAD):
                                high(u0 + i + AHEAD, cc * (16 * len(plan) // RING))
                            if kind == "ff1":
                                b = B_GEMM[n % 2]
                                act.wait_ge(bank_full[b], j0[n % 2] + n // 2 + cc * KT)
                                act.wait_ge(hid_done, FF_CHUNKS * KT * L + m + 1 + cc * KT)
                                nc.scalar.activation(hr[:, m % 2, 0:ntok], ps[:, b, 0:ntok], ACT.Relu)\
                                    .then_inc(hr_done, 1)
                            n += kind != "mod"
                            if i and plan[i - 1][0] == "mod" and plan[i - 1][1] % KQ == KQ - 1:
                                j = MBLOCKS + plan[i - 1][1] // KQ
                                act.wait_ge(mcol_done, j + cc * (MODS_LOOP // KQ))
                                act.wait_ge(mu_used, KQ * (j + 1) + cc * MODS_LOOP)
                                nc.scalar.activation(mrow[:, :], ps[0:4, B_AUX[1], :], ACT.Copy).then_inc(row_done, 1)
                    if L == 0:
                        with act.Fori(0, FF_CHUNKS, 1) as cc:
                            one_pass(cc, False)
                    else:
                        with act.Fori(0, FF_CHUNKS - 1, 1) as cc:
                            one_pass(cc, False)
                        one_pass(FF_CHUNKS - 1, True)
                elif k == "exp":
                    i = st[1]
                    t, par, qt = ATTN[i]
                    act.wait_ge(max_done, i + 1)
                    b, _ = jobs[("S", i)]
                    if i >= 2:
                        act.wait_ge(*filled(("PT", i - 2)))
                    else:
                        act.wait_ge(split_done, split_at[("norm", 1, "mix")] + KT)
                    nc.scalar.activation(prob[:, i % 2, :], ps[:, b, :], ACT.Exp, bias=sm[:, 0, i % 2:i % 2 + 1],
                                                  accum_out=sm[:, 1, i % 2:i % 2 + 1]).then_inc(freeing(("S", i)), 1)
                    h = 2 * (t % 4) + par
                    nc.scalar.activation(sm[:, 2, i % 2:i % 2 + 1], bc[:, 120 + h:121 + h], ACT.Exp,
                                             bias=sm[:, 0, i % 2:i % 2 + 1]).then_inc(signal(exp_done), 1)
                elif k == "scale":
                    i = st[1]
                    act.wait_ge(rs_done, i + 1)
                    act.wait_ge(exp_done, i + 1)
                    nc.scalar.activation(prob[:, i % 2, :], prob[:, i % 2, :], ACT.Copy, scale=sm[:, 4, i % 2:i % 2 + 1]).then_inc(signal(prob_done), 1)
                elif k == "PT":
                    i = st[1]
                    b = jobs[st][0]
                    act.wait_ge(*filled(st))
                    if i >= 2:
                        act.wait_ge(pv_done, i - 1)
                    nc.scalar.activation(pT[:, i % 2, :], ps[:, b, :], ACT.Copy).then_inc(signal(pT_done), 1)
                elif k == "osplit":
                    b = jobs[("Opair", st[1])][0]
                    act.wait_ge(*filled(("Opair", st[1])))
                    nc.scalar.activation(a_hi[:, st[1], 0:SEQ], ps[:, b, 0:SEQ], ACT.Copy).then_inc(signal(ohi_done), 1)
                elif k == "out":
                    for q in (1, 3):
                        b = jobs[st + (q,)][0]
                        act.wait_ge(*filled(st + (q,)))
                        nc.scalar.activation(fin[:, q // 2, 512:1024], ps[:, b, :], ACT.Copy).then_inc(signal(fin_done), 1)

        @block.vector
        def _(dve):
            v = nc.vector
            signal, freeing, latest, counts = ledger()

            def low(u, passes=0):
                dve.wait_ge(hi_done, u + 1 + passes)
                v.tensor_tensor(w_lo[:, u % RING, :, :], raw[:, u % RING, :, :], w_hi[:, u % RING, :, :].bitcast(F32),
                                ALU.subtract).then_inc(lo_done, 1)

            def residual(st, key, m, L, gate_tile):
                b = jobs[key][0]
                dve.wait_ge(*filled(key))
                halves = tokens(st) // SEQ
                for i in range(halves):
                    hs = hT[:, m, SEQ * i:SEQ * i + SEQ]
                    v.scalar_tensor_tensor(out=hs, in0=ps[:, b, SEQ * i:SEQ * i + SEQ],
                                               scalar=mod[:, L, gate_tile, i:i + 1], in1=hs, op0=ALU.mult, op1=ALU.add).then_inc(signal(h_done if i == halves - 1 else dve_seq), 1)

            v.memset(coefA[:, 0, 0:1], 0.0).then_inc(signal(hid_done), 1)
            v.memset(coefA[:, 0, 1:2], 0.0).then_inc(signal(hid_done), 1)
            for st in steps:
                k = st[0]
                if k == "vecs":
                    for q in range(3):
                        b = jobs[st + (q,)][0]
                        dve.wait_ge(*filled(st + (q,)))
                        n = (P, 120, 32)[q]
                        v.tensor_copy(vt[:, q, 0:n], ps[:, b, 0:n]).then_inc(freeing(st + (q,)), 1)
                        dve.wait_ge(*latest())
                        if q == 1:
                            v.tensor_scalar(vt[:, 1, 0:120], vt[:, 1, 0:120], 0.5, None, ALU.mult).then_inc(signal(dve_seq), 1)
                        if q == 2:
                            v.tensor_scalar(gssdT, gssdT, 0.5, None, ALU.mult).then_inc(signal(dve_seq), 1)
                            v.tensor_scalar(vt[:, 2, 28:29], vt[:, 2, 28:29], HD ** -0.5, None, ALU.mult).then_inc(signal(dve_seq), 1)
                            v.tensor_scalar(vt[:, 2, 30:31], vt[:, 2, 30:31], HD ** -0.5, None, ALU.mult).then_inc(signal(dve_seq), 1)
                        dve.wait_ge(*latest())
                        v.tensor_copy(coefA[:, q, 0:1], vt[:, q, 0:1]).then_inc(signal(vt_done), 1)
                        dve.wait_ge(*latest())
                    b = jobs[st + (3,)][0]
                    dve.wait_ge(*filled(st + (3,)))
                    v.tensor_copy(bc[:, :], ps[:, b, 0:P]).then_inc(signal(vt_done), 1)
                    dve.wait_ge(*latest())
                    pairs = bc[:, 96:120].rearrange("p (t h) -> p t h", h=2)
                    for i in range(2):
                        v.tensor_copy(dsk[HD * i:HD * i + HD, :], pairs[HD * i:HD * i + HD, :, i]).then_inc(signal(dve_seq), 1)
                    dve.wait_ge(th0_done, 2)
                    v.tensor_scalar(nega[:, :], nega[:, :], -1.0, None, ALU.mult).then_inc(signal(dve_seq), 1)
                    v.tensor_scalar(silc[:, :, :], vt[:, 2, 12:28].rearrange("p (s t) -> p t s", s=2), 0.5, None, ALU.mult).then_inc(signal(dve_seq), 1)
                    dve.wait_ge(*latest())
                    v.scalar_tensor_tensor(out=silc[:, :, :], in0=sct[:, :, :], scalar=1.0, in1=silc[:, :, :],
                                               op0=ALU.add, op1=ALU.mult).then_inc(signal(silc_done), 1)
                    dve.wait_ge(silc_done, 1)
                    v.tensor_copy(sil4[:, :, 0:2], silc[:, :, :]).then_inc(signal(silc_done), 1)
                    dve.wait_ge(silc_done, 2)
                    v.tensor_tensor(sil4[:, :, 2:4], silc[:, :, :], sil4[:, :, 0:2].bitcast(F32), ALU.subtract).then_inc(signal(sil4_done), 1)
                elif k == "mu":
                    if st == order[0]:
                        for u in range(AHEAD):
                            low(u)
                    low(unit[st] + AHEAD)
                elif k == "mcol":
                    j = st[1]
                    b = jobs[st][0]
                    dve.wait_ge(*filled(st))
                    v.tensor_tensor(mod[:, 0, MB * j:MB * j + MB, :], ps[:, b, 0:2 * MB].rearrange("p (f s) -> p f s", s=2),
                                    bmodT[:, 0, MB * j:MB * j + MB].unsqueeze(2).broadcast_to([P, MB, 2]), ALU.add).then_inc(signal(modc_done), 1)
                elif k == "xin":
                    b = jobs[st][0]
                    dve.wait_ge(*filled(st))
                    v.tensor_copy(hT[:, st[1], :], ps[:, b, :]).then_inc(signal(h_done), 1)
                elif k == "norm":
                    L = st[1]
                    ntok = SEQ if st == ("norm", 1, "ff") else T
                    dve.wait_ge(*latest())
                    sc = (1 if st[2] == "mix" else 4) * KT
                    gains = (gmixT if st[2] == "mix" else gffT)[:, L, :]
                    if norm_n[st]:
                        dve.wait_ge(u_done, KT * norm_n[st])
                    v.scalar_tensor_tensor(out=coefA[:, :, :], in0=mod[:, L, sc:sc + KT, :], scalar=1.0,
                                               in1=gains.unsqueeze(2).broadcast_to([P, KT, 2]), op0=ALU.add, op1=ALU.mult).then_inc(signal(coef_done), 1)
                    rms = rms_of(st)
                    dve.wait_ge(var_done, rms_n[st])
                    v.reciprocal(rms, rms).then_inc(signal(rstd_done), 1)
                    dve.wait_ge(rstd_done, rms_n[st])

                    def scaled(f):
                        n = KT * norm_n[st] + f
                        if n >= 2:
                            dve.wait_ge(u_done, n - 1)
                        ins = v.tensor_tensor(nt[:, f % 2, 0:ntok], hT[:, f, 0:ntok], rms, ALU.mult).then_inc(signal(nt_done), 1)
                    scaled(0)
                    scaled(1)
                    for f in range(KT):
                        dve.wait_ge(u_done, KT * norm_n[st] + f + 1)
                        v.tensor_tensor(a_lo[:, f, 0:ntok], u32[:, f % 2, 0:ntok], a_hi[:, f, 0:ntok].bitcast(F32), ALU.subtract).then_inc(signal(split_done), 1)
                        if f + 2 < KT:
                            scaled(f + 2)
                elif k == "dtraw":
                    dve.wait_ge(wdthi_done, 1)
                    v.tensor_tensor(wdt_lo[:, :, :], wdt[:, :, :], wdt_hi[:, :, :].bitcast(F32), ALU.subtract).then_inc(signal(wdtlo_done), 1)
                    b = jobs[st][0]
                    dve.wait_ge(*filled(st))
                    v.tensor_copy(dtrow[:, :], ps[0:2 * NH, b, :]).then_inc(signal(dtrow_done), 1)
                elif k == "dtcol":
                    b = jobs[st][0]
                    dve.wait_ge(*filled(st))
                    v.tensor_tensor(dts["tmp"][:, :, :], ps[:, b, 0:192].rearrange("p (c h) -> p c h", c=NCH),
                                             bc[:, None, 48:96].broadcast_to([P, NCH, 48]), ALU.add).then_inc(signal(dtv_done), 1)
                    dve.wait_ge(dte_done, 1)
                    v.tensor_scalar(dts["dt"][:, :, :], dts["t3"][:, :, :], 1.0, None, ALU.add).then_inc(signal(dve_seq), 1)
                    dve.wait_ge(*latest())
                    v.tensor_scalar(dts["dt"][:, :, :], dts["dt"][:, :, :], -1.0, None, ALU.add).then_inc(signal(dve_seq), 1)
                    dve.wait_ge(*latest())
                    v.tensor_tensor(dts["dt"][:, :, :], dts["t3"][:, :, :], dts["dt"][:, :, :], ALU.subtract).then_inc(signal(dve_seq), 1)
                    dve.wait_ge(dtln_done, 1)
                    dve.wait_ge(*latest())
                    v.tensor_tensor(dts["dt"][:, :, :], dts["dt"][:, :, :], dts["ea"][:, :, :], ALU.add).then_inc(signal(dve_seq), 1)
                    dve.wait_ge(*latest())
                    v.scalar_tensor_tensor(out=dts["dt"][:, :, :], in0=dts["tmp"][:, :, :], scalar=0.0, in1=dts["dt"][:, :, :],
                                               op0=ALU.max, op1=ALU.add).then_inc(signal(dve_seq), 1)
                    dve.wait_ge(*latest())
                    v.tensor_tensor(dts["dta"][:, :, :], dts["dt"][:, :, :], nega[:, None, :].broadcast_to([P, NCH, 48]), ALU.mult).then_inc(signal(dt_done), 1)
                elif k == "gemm":
                    low(unit[st] + AHEAD)
                    b, _ = jobs[st]
                    if st[1] == "fn":
                        dve.wait_ge(*filled(st))
                        if st[2] >= 2:
                            dve.wait_ge(*filled(("dftw", st[2] - 2, 1)))
                        v.tensor_copy(uf[:, st[2] % 2, :], ps[:, b, :]).then_inc(signal(uf_done), 1)
                    elif st[1] == "z":
                        n, i = z_n[st], st[2] % XT
                        dve.wait_ge(zt_done, n + 1)
                        if i == 0 and n:
                            dve.wait_ge(mix_done, FN_T + n)
                        v.scalar_tensor_tensor(out=gate[:, i, :], in0=zt[:, :], scalar=1.0, in1=ps[:, b, :],
                                                        op0=ALU.add, op1=ALU.mult).then_inc(signal(gate_done), 1)
                    elif st[1] in ("outA", "outB", "outO"):
                        dve.wait_ge(*latest())
                        residual(st, st, st[2], 1 if st[1] == "outO" else 0, 2 * KT + st[2])
                elif k == "taps":
                    t = st[1]
                    n = conv_n[("gemm", "conv", t)]
                    dve.wait_ge(pad_done, n + 1)
                    if n >= 2:
                        dve.wait_ge(th_done, n - 1)
                    acc = cacc[:, n % 2, :].rearrange("p (s t) -> p s t", s=2)
                    dve.wait_ge(*latest())
                    v.tensor_scalar(acc, cpad[:, n % 2, :, 0:SEQ], convwT[:, 0, t:t + 1], convbT[:, t:t + 1], ALU.mult, ALU.add).then_inc(signal(dve_seq), 1)
                    for w in range(1, CONV_W):
                        dve.wait_ge(*latest())
                        v.scalar_tensor_tensor(out=acc, in0=cpad[:, n % 2, :, w:w + SEQ], scalar=convwT[:, w, t:t + 1],
                                                   in1=acc, op0=ALU.mult, op1=ALU.add).then_inc(signal(acc_done if w == CONV_W - 1 else dve_seq), 1)
                elif k == "silu":
                    t = st[1]
                    n = conv_n[("gemm", "conv", t)]
                    g = [t in conv_tiles(g) for g in range(G)].index(True)
                    slot = conv_tiles(g).index(t)
                    dve.wait_ge(th_done, n + 1)
                    if slot == 0 and g >= 2:
                        for q in y_jobs(g - 2, SCAN_F[-1]):
                            dve.wait_ge(*filled(q))
                    dve.wait_ge(*latest())
                    v.scalar_tensor_tensor(out=xbc[:, g % 2, slot, :], in0=cth[:, :], scalar=1.0, in1=cacc[:, n % 2, :],
                                               op0=ALU.add, op1=ALU.mult).then_inc(signal(xbc_done), 1)
                elif k == "dftw":
                    if st[1]:
                        dve.wait_ge(*filled(("dfts", st[1] - 1)))
                    for q in range(2):
                        b = jobs[st + (q,)][0]
                        dve.wait_ge(*filled(st + (q,)))
                        v.tensor_copy(vf[:, 2 * q:2 * q + 2, :], ps[:, b, :].rearrange("p (c f) -> p c f", c=2)).then_inc(signal(vf_done), 1)
                elif k == "dfts":
                    b = jobs[st][0]
                    dve.wait_ge(*filled(st))
                    v.tensor_copy(mixF[:, st[1], :], ps[:, b, :]).then_inc(signal(mix_done), 1)
                elif k == "toks":
                    _, g, ch = st
                    if ch == SCAN_F[0]:
                        if g == 0:
                            dve.wait_ge(*filled(("dfts", FN_T - 1)))
                        else:
                            for q in y_jobs(g - 1, SCAN_F[-1]):
                                dve.wait_ge(*filled(q))
                    b = jobs[st][0]
                    dve.wait_ge(*filled(st))
                    v.tensor_copy(btok[:, ch, :], ps[:, b, GX:GX + NS]).then_inc(signal(dve_seq), 1)
                    for di in range(2):
                        v.tensor_tensor(heads(xdt[:, di, ch, :]), heads(ps[:, b, 0:GX]),
                                            dts["dt"][:, ch, NH * di + R * g:NH * di + R * g + R].unsqueeze(2).broadcast_to([P, R, HD]),
                                            ALU.mult).then_inc(signal(xdt_done if di else dve_seq), 1)
                elif k == "state":
                    _, g, d, ch = st
                    di = dirs[d]
                    old, new = entering(d, ch), scans[d].index(ch)
                    b = jobs[st][0]
                    dve.wait_ge(*filled(st))
                    dve.wait_ge(*latest())
                    if st_n[st] % len(STATES) == 0:
                        dve.wait_ge(dtx_done, 3)
                    if old is None:
                        v.tensor_copy(hent[:, di, new, :], ps[:, b, 0:GX]).then_inc(signal(ent_done), 1)
                    else:
                        v.tensor_tensor(heads(hent[:, di, new, :]), heads(hent[:, di, old, :]),
                                            dts["tot"][:, ch, NH * di + R * g:NH * di + R * g + R].unsqueeze(2).broadcast_to([P, R, HD]), ALU.mult).then_inc(signal(dve_seq), 1)
                        dve.wait_ge(*latest())
                        v.tensor_tensor(hent[:, di, new, :], hent[:, di, new, :], ps[:, b, 0:GX], ALU.add).then_inc(signal(ent_done), 1)
                elif k == "cb":
                    b = jobs[st][0]
                    dve.wait_ge(*filled(st))
                    dve.wait_ge(*latest())
                    v.tensor_tensor(cbm[:, 0, :], ps[:, b, 0:P], tle, ALU.mult).then_inc(signal(dve_seq), 1)
                    v.tensor_tensor(cbm[:, 1, :], ps[:, b, 0:P], tge, ALU.mult).then_inc(freeing(st), 1)
                elif k == "seg":
                    di = dirs[st[2]]
                    dve.wait_ge(seg_done, seg_n[st] + 1)
                    dve.wait_ge(*latest())
                    v.tensor_tensor(ey[:, di, :, :], ey[:, di, :, :], cbm[:, di, None, :].broadcast_to([P, R, P]), ALU.mult).then_inc(signal(g_done), 1)
                elif k == "y":
                    _, g, ch = st
                    if y_n[st]:
                        prev = steps_of("y")[y_n[st] - 1]
                        dve.wait_ge(*filled(("yt",) + prev[1:]))
                    parts = []
                    for di, q in enumerate("fb"):
                        if st + (q,) in jobs:
                            b = jobs[st + (q,)][0]
                            dve.wait_ge(*filled(st + (q,)))
                            v.tensor_tensor(heads(ycomb[:, di, :]), heads(ps[:, b, 0:GX]),
                                                     dts["ea"][:, ch, NH * di + R * g:NH * di + R * g + R].unsqueeze(2).broadcast_to([P, R, HD]),
                                                     ALU.mult).then_inc(freeing(st + (q,)), 1)
                            parts.append(di)
                    dve.wait_ge(*latest())
                    if len(parts) == 2:
                        v.tensor_tensor(ycomb[:, 0, :], ycomb[:, 0, :], ycomb[:, 1, :], ALU.add).then_inc(signal(dve_seq), 1)
                        dve.wait_ge(*latest())
                    b = jobs[st + ("d",)][0]
                    dve.wait_ge(*filled(st + ("d",)))
                    src = parts[0]
                    v.tensor_tensor(ycomb[:, 0, :], ycomb[:, src, :], ps[:, b, 0:GX], ALU.add).then_inc(signal(y_done), 1)
                elif k == "yt":
                    _, g, ch = st
                    b = jobs[st][0]
                    dve.wait_ge(*filled(st))
                    for i in range(XT):
                        v.scalar_tensor_tensor(out=mixF[:, FN_T + XT * g + i, P * ch:P * ch + P],
                                                   in0=xbc[:, g % 2, 2 + i, P * ch:P * ch + P],
                                                   scalar=dsk[:, XT * g + i:XT * g + i + 1],
                                                   in1=ps[:, b, P * i:P * i + P], op0=ALU.mult, op1=ALU.add).then_inc(freeing(st) if i == XT - 1 else signal(dve_seq), 1)
                elif k == "ygate":
                    g = st[1]
                    dve.wait_ge(*latest())
                    mg = mixF[:, FN_T + XT * g:FN_T + XT * g + XT, :]
                    v.tensor_tensor(mg, mg, gate[:, :, :], ALU.mult).then_inc(signal(gated), 1)
                elif k == "hstat":
                    dve.wait_ge(var_done, rms_n[st])
                    v.reciprocal(rms_of(st), rms_of(st)).then_inc(signal(rstd_done), 1)
                elif k == "ynorm":
                    g = st[1]
                    rms = rms_of(("ysum", g))
                    dve.wait_ge(var_done, rms_n[("ysum", g)])
                    v.reciprocal(rms, rms).then_inc(signal(rstd_done), 1)
                    dve.wait_ge(*latest())
                    for i in range(XT):
                        mi = mixF[:, FN_T + XT * g + i, :]
                        ins = v.scalar_tensor_tensor(out=mi, in0=mi, scalar=gssdT[:, XT * g + i:XT * g + i + 1], in1=rms_of(("ysum", g)),
                                                         op0=ALU.mult, op1=ALU.mult).then_inc(signal(mix_done), 1)
                elif k == "mixsplit":
                    hi, lo = ((a_hi, a_lo), (b_hi, b_lo))[st[1]]
                    for f in range(KT):
                        t = KT * st[1] + f
                        dve.wait_ge(mixhi_done, t + 1)
                        dve.wait_ge(*latest())
                        v.tensor_tensor(lo[:, f, :], mixF[:, t, :], hi[:, f, :].bitcast(F32), ALU.subtract).then_inc(signal(split_done), 1)
                elif k == "mlp":
                    L = st[1]
                    ntok = T if L == 0 else SEQ
                    j0 = jobs[st + (B_GEMM[0],)][1], jobs[st + (B_GEMM[1],)][1]
                    u0, plan = unit[st], mlp_plan(L)
                    h0 = FF_CHUNKS * KT * L

                    def one_pass(cc, last):
                        n = 0
                        for i, (kind, m) in enumerate(plan):
                            if not (last and i >= len(plan) - AHEAD):
                                low(u0 + i + AHEAD, cc * len(plan))
                            if i >= 2 and plan[i - 2][0] == "mod" and plan[i - 2][1] % KQ == KQ - 1:
                                jb = plan[i - 2][1] // KQ
                                dve.wait_ge(mcol_done, MBLOCKS + jb + 1 + cc * (MODS_LOOP // KQ))
                                v.tensor_tensor(mod[:, 1, bass.ds(cc * (MODS_LOOP // KQ * MB) + MB * jb, MB), :],
                                                ps[:, B_TR, 0:2 * MB].rearrange("p (f s) -> p f s", s=2),
                                                bmod1[:, bass.ds(cc * (MODS_LOOP // KQ * MB) + MB * jb, MB)].unsqueeze(2).broadcast_to([P, MB, 2]),
                                                ALU.add).then_inc(modc_done, 1)
                            if kind == "mod":
                                continue
                            b = B_GEMM[n % 2]
                            if kind == "ff1":
                                dve.wait_ge(hr_done, h0 + m + 1 + cc * KT)
                                v.tensor_tensor(hq[:, m % 2, 0:ntok], hr[:, m % 2, 0:ntok], hr[:, m % 2, 0:ntok], ALU.mult).then_inc(hq_done, 1)
                                dve.wait_ge(hq_done, h0 + m + 1 + cc * KT)
                                v.tensor_copy(b_hi[:, m, 0:ntok], hq[:, m % 2, 0:ntok]).then_inc(hidhi_done, 1)
                                dve.wait_ge(hidhi_done, h0 + m + 1 + cc * KT)
                                v.tensor_tensor(b_lo[:, m, 0:ntok], hq[:, m % 2, 0:ntok], b_hi[:, m, 0:ntok].bitcast(F32),
                                                ALU.subtract).then_inc(hid_done, 1)
                            else:
                                dve.wait_ge(bank_full[b], j0[n % 2] + n // 2 + cc * KT)
                                dve.wait_ge(h_done, mlp_h[L] + m - KT + 1 + cc * KT)
                                for i in range(ntok // SEQ):
                                    hs = hT[:, m, SEQ * i:SEQ * i + SEQ]
                                    ins = v.scalar_tensor_tensor(out=hs, in0=ps[:, b, SEQ * i:SEQ * i + SEQ],
                                                                 scalar=mod[:, L, 5 * KT + m, i:i + 1], in1=hs, op0=ALU.mult, op1=ALU.add)
                                ins.then_inc(h_done, 1)
                            n += 1
                    if L == 0:
                        with dve.Fori(0, FF_CHUNKS, 1) as cc:
                            one_pass(cc, False)
                        dve.wait_ge(modc_done, 2 * MBLOCKS)
                    else:
                        with dve.Fori(0, FF_CHUNKS - 1, 1) as cc:
                            one_pass(cc, False)
                        one_pass(FF_CHUNKS - 1, True)
                    counts[h_done] += FF_CHUNKS * KT
                elif k == "hnorm":
                    dve.wait_ge(rstd_done, rms_n[("hstat",) + st[1:]])
                    dve.wait_ge(qraw_done, qk_n[st[1:]] + 1)
                    x_ = ktile(*st[1:])
                    v.scalar_tensor_tensor(out=x_, in0=x_, scalar=vt[:, 2, g_q[st[1]]:g_q[st[1]] + 1],
                                           in1=rms_of(("hstat",) + st[1:]), op0=ALU.mult, op1=ALU.mult).then_inc(signal(qn_done), 1)
                elif k == "rot":
                    x_ = ktile(*st[1:])[:, 0:SEQ]
                    b = jobs[st][0]
                    dve.wait_ge(*filled(st))
                    dve.wait_ge(*latest())
                    v.tensor_tensor(rp[:, 0, :], x_, cuts["cos"], ALU.mult).then_inc(signal(dve_seq), 1)
                    v.tensor_tensor(rp[:, 1, :], ps[:, b, 0:SEQ], cuts["sin"], ALU.mult).then_inc(freeing(st), 1)
                    dve.wait_ge(*latest())
                    v.tensor_tensor(x_, rp[:, 0, :], rp[:, 1, :], ALU.add).then_inc(signal(rope_done), 1)
                elif k == "dup":
                    for q in range(2):
                        b = jobs[st + (q,)][0]
                        dve.wait_ge(*filled(st + (q,)))
                        v.tensor_copy(kdup[:, q, :], ps[:, b, :]).then_inc(signal(kd_done), 1)
                elif k == "exp":
                    i = st[1]
                    t, par, qt = ATTN[i]
                    b = jobs[("S", i)][0]
                    dve.wait_ge(*filled(("S", i)))
                    col = lambda r: sm[:, r, i % 2:i % 2 + 1]
                    dve.wait_ge(*latest())
                    v.tensor_reduce(col(3), ps[:, b, :], AX, ALU.max).then_inc(signal(dve_seq), 1)
                    dve.wait_ge(*latest())
                    if t < 4:
                        h = 2 * t + par
                        v.tensor_scalar(col(0), col(3), bc[:, 120 + h:121 + h], -1.0, ALU.max, ALU.mult).then_inc(signal(max_done), 1)
                    else:
                        v.tensor_scalar(col(0), col(3), -1.0, None, ALU.mult).then_inc(signal(max_done), 1)
                elif k == "scale":
                    i = st[1]
                    t, par, qt = ATTN[i]
                    col = lambda r: sm[:, r, i % 2:i % 2 + 1]
                    dve.wait_ge(exp_done, i + 1)
                    src = col(1)
                    if t < 4:
                        v.tensor_tensor(col(5), col(1), col(2), ALU.add).then_inc(signal(dve_seq), 1)
                        dve.wait_ge(*latest())
                        src = col(5)
                    v.reciprocal(col(4), src).then_inc(signal(rs_done), 1)
                elif k == "osplit":
                    t = st[1]
                    dve.wait_ge(ohi_done, t + 1)
                    b, _ = jobs[("Opair", t)]
                    v.tensor_tensor(a_lo[:, t, 0:SEQ], ps[:, b, 0:SEQ], a_hi[:, t, 0:SEQ].bitcast(F32), ALU.subtract).then_inc(signal(split_done), 1)
                elif k == "out":
                    for q in (0, 2):
                        b = jobs[st + (q,)][0]
                        dve.wait_ge(*filled(st + (q,)))
                        v.tensor_copy(fin[:, q // 2, 0:512], ps[:, b, :]).then_inc(signal(finv_done), 1)

        @block.tensor
        def _(pe):
            mm = nc.tensor.matmul

            def product(out_ap, n, hi, lo, ntok, ready=None):
                for k in range(KT):
                    if ready:
                        pe.wait_ge(ready[0], ready[1] + k)
                    for j, (w_, x_) in enumerate(((w_hi, hi), (w_hi, lo), (w_lo, hi))):
                        ins = mm(out_ap, w_[:, n % RING, k, :], x_[:, k, 0:ntok], start=(k == 0 and j == 0), stop=(k == KT - 1 and j == 2))
                return ins

            def row_product(b, u, q):
                for a in range(2):
                    parts = [(w_hi, 4), (w_lo, 2)] if q < KQ - 1 or a == 0 else [(w_lo, 2), (w_hi, 4)]
                    for i, (w_, n) in enumerate(parts):
                        ins = mm(ps[0:n, b, :], sil4[:, 2 * q + a, 0:n], mod_view(w_, u % RING)[:, a, :],
                                 start=(q == 0 and a == 0 and i == 0), stop=(q == KQ - 1 and a == 1 and i == 1), skip_group_check=True)
                return ins

            def columns(b):
                for i in range(MB):
                    ins = mm(ps[:, b, 2 * i:2 * i + 2], mrow[:, P * i:P * i + P], pairs4, start=True, stop=True)
                return ins

            n_sq = 0
            for st in steps:
                k = st[0]
                if k == "vecs":
                    pe.wait_ge(vec_in, 16 * N_VEC)
                    pe.wait_ge(c0_in, 16)
                    for q in range(3):
                        n = (P, 120, 32)[q]
                        b = jobs[st + (q,)][0]
                        if free_before[st + (q,)]:
                            pe.wait_ge(*emptied(st + (q,)))
                        nc.tensor.transpose(ps[:, b, 0:n], vrow[0:n, q, :], ident[0:n, 0:n]).then_inc(filling(st + (q,)), 1)
                    b = jobs[st + (3,)][0]
                    if free_before[st + (3,)]:
                        pe.wait_ge(*emptied(st + (3,)))
                    mm(ps[:, b, 0:P], ones[0:1, :], rowv[:, :], start=True, stop=True).then_inc(filling(st + (3,)), 1)
                elif k == "mu":
                    _, j, q = st
                    b = jobs[("mrow", j)][0]
                    if st == order[0]:
                        pe.wait_ge(sil4_done, 1)
                    if q == 0 and free_before[("mrow", j)]:
                        pe.wait_ge(*emptied(("mrow", j)))
                    pe.wait_ge(lo_done, unit[st] + 1)
                    row_product(b, unit[st], q).then_inc(mu_used, 1)
                elif k == "mcol":
                    b = jobs[st][0]
                    if free_before[st]:
                        pe.wait_ge(*emptied(st))
                    pe.wait_ge(row_done, st[1] + 1)
                    columns(b).then_inc(mcol_done, 1)
                elif k == "xin":
                    f = st[1]
                    if f == 0:
                        for t in range(NCH):
                            pe.wait_ge(x_in[t], 16)
                    b = jobs[st][0]
                    if free_before[st]:
                        pe.wait_ge(*emptied(st))
                    for t in range(NCH):
                        ins = nc.tensor.transpose(ps[:, b, P * t:P * t + P], xload[:, t, P * f:P * f + P], ident)
                    ins.then_inc(filling(st), 1)
                elif k == "norm":
                    ntok = SEQ if st == ("norm", 1, "ff") else T
                    b = jobs[st][0]
                    if free_before[st]:
                        pe.wait_ge(*emptied(st))
                    pe.wait_ge(acc_sq, (KT - 1) * (norm_n[st] + 1))
                    mm(ps[:, b, 0:ntok], ones, sq[:, 0, 0:ntok], start=True, stop=False)
                    n_sq += 1
                    pe.wait_ge(sq_done, n_sq)
                    mm(ps[:, b, 0:ntok], ones, sq[:, 1, 0:ntok], start=False, stop=True).then_inc(filling(st), 1)
                elif k == "dtraw":
                    pe.wait_ge(wdtlo_done, 1)
                    pe.wait_ge(split_done, KT)
                    b = jobs[st][0]
                    if free_before[st]:
                        pe.wait_ge(*emptied(st))
                    for kk in range(KT):
                        for j, (w_, x_) in enumerate(((wdt_hi, a_hi), (wdt_hi, a_lo), (wdt_lo, a_hi))):
                            ins = mm(ps[0:2 * NH, b, :], w_[:, kk, :], x_[:, kk, :], start=(kk == 0 and j == 0), stop=(kk == KT - 1 and j == 2))
                    ins.then_inc(filling(st), 1)
                elif k == "dtcol":
                    pe.wait_ge(dtrow_done, 1)
                    b = jobs[st][0]
                    if free_before[st]:
                        pe.wait_ge(*emptied(st))
                    for ch in range(NCH):
                        ins = nc.tensor.transpose(ps[:, b, 48 * ch:48 * ch + 48], dtrow[:, P * ch:P * ch + P], ident[0:2 * NH, 0:2 * NH])
                    ins.then_inc(filling(st), 1)
                elif k == "dtcum":
                    pe.wait_ge(dt_done, 1)
                    b = jobs[st][0]
                    if free_before[st]:
                        pe.wait_ge(*emptied(st))
                    for ch in range(NCH):
                        for o, (tf, tb) in ((0, (tle, tge)), (192, (tgt, tlt))):
                            for di, tri in enumerate((tf, tb)):
                                c_ = o + 48 * ch + NH * di
                                ins = mm(ps[:, b, c_:c_ + NH], tri, dts["dta"][:, ch, NH * di:NH * di + NH], start=True, stop=True)
                    ins.then_inc(filling(st), 1)
                    b = jobs[st + ("tot",)][0]
                    if free_before[st + ("tot",)]:
                        pe.wait_ge(*emptied(st + ("tot",)))
                    mm(ps[:, b, 0:192], ones, dts["dta"][:, :, :].rearrange("p c h -> p (c h)"), start=True, stop=True).then_inc(filling(st + ("tot",)), 1)
                elif k == "gemm":
                    n = unit[st]
                    b = jobs[st][0]
                    if free_before[st]:
                        pe.wait_ge(*emptied(st))
                    hi, lo = (b_hi, b_lo) if st[1] == "outB" else (a_hi, a_lo)
                    ready = None
                    if st in starts:
                        ready = split_done, starts[st] + 1
                    pe.wait_ge(lo_done, n + 1)
                    product(ps[:, b, 0:tokens(st)], n, hi, lo, tokens(st), ready).then_inc(filling(st), 1)
                elif k == "dftw":
                    pe.wait_ge(uf_done, st[1] + 1)
                    for q in range(2):
                        b = jobs[st + (q,)][0]
                        if free_before[st + (q,)]:
                            pe.wait_ge(*emptied(st + (q,)))
                        for i in range(2):
                            ch = 2 * q + i
                            ins = mm(ps[:, b, 256 * i:256 * i + 256], uf[:, st[1] % 2, P * ch:P * ch + P], dftw, start=True, stop=True)
                        ins.then_inc(filling(st + (q,)), 1)
                elif k == "dfts":
                    pe.wait_ge(vf_done, 2 * st[1] + 2)
                    b = jobs[st][0]
                    if free_before[st]:
                        pe.wait_ge(*emptied(st))
                    for s_ in range(2):
                        for kk in range(2):
                            for c_ in range(2):
                                ins = mm(ps[:, b, SEQ * s_:SEQ * s_ + SEQ], vf[:, 2 * s_ + kk, P * c_:P * c_ + P], dfts[:, kk, c_, :],
                                         start=(kk == 0 and c_ == 0), stop=(kk == 1 and c_ == 1))
                    ins.then_inc(filling(st), 1)
                elif k == "toks":
                    _, g, ch = st
                    pe.wait_ge(xbc_done, 5 * (g + 1))
                    b = jobs[st][0]
                    if free_before[st]:
                        pe.wait_ge(*emptied(st))
                    for i in range(XT):
                        nc.tensor.transpose(ps[:, b, P * i:P * i + P], xbc[:, g % 2, 2 + i, P * ch:P * ch + P], ident)
                    nc.tensor.transpose(ps[:, b, GX:GX + NS], xbc[:, g % 2, 0, P * ch:P * ch + P], ident).then_inc(filling(st), 1)
                elif k == "state":
                    _, g, d, ch = st
                    n = st_n[st]
                    pe.wait_ge(xw_done, n + 1)
                    b = jobs[st][0]
                    if free_before[st]:
                        pe.wait_ge(*emptied(st))
                    mm(ps[:, b, 0:GX], btok[:, ch, :], xw[:, n % 2, :], start=True, stop=True).then_inc(filling(st), 1)
                elif k == "cb":
                    _, g, ch = st
                    b = jobs[st][0]
                    if free_before[st]:
                        pe.wait_ge(*emptied(st))
                    mm(ps[:, b, 0:P], xbc[:, g % 2, 0, P * ch:P * ch + P], xbc[:, g % 2, 1, P * ch:P * ch + P], start=True, stop=True).then_inc(filling(st), 1)
                elif k == "seg":
                    pe.wait_ge(rr_done, seg_n[st] + 1)
                    b = jobs[st][0]
                    if free_before[st]:
                        pe.wait_ge(*emptied(st))
                    for i in range(2):
                        ins = mm(ps[:, b + i, 0:GX], (tgt, tlt)[dirs[st[2]]], rr[:, 3 * i:3 * i + 3, :].rearrange("p h l -> p (h l)"),
                                 start=True, stop=True)
                    ins.then_inc(filling(st), 1)
                elif k == "y":
                    _, g, ch = st
                    pe.wait_ge(ent_done, len(STATES) * (g + 1))
                    for d, di in (("f", 0), ("b", 1)):
                        e = entering(d, ch)
                        if e is not None:
                            b = jobs[st + (d,)][0]
                            if free_before[st + (d,)]:
                                pe.wait_ge(*emptied(st + (d,)))
                            mm(ps[:, b, 0:GX], xbc[:, g % 2, 1, P * ch:P * ch + P], hent[:, di, e, :], start=True, stop=True).then_inc(filling(st + (d,)), 1)
                    pe.wait_ge(g_done, 2 * (y_n[st] + 1))
                    b = jobs[st + ("d",)][0]
                    if free_before[st + ("d",)]:
                        pe.wait_ge(*emptied(st + ("d",)))
                    for r in range(R):
                        for di in range(2):
                            ins = mm(ps[:, b, HD * r:HD * r + HD], ey[:, di, r, :], xdt[:, di, ch, HD * r:HD * r + HD], start=(di == 0), stop=(di == 1))
                    ins.then_inc(filling(st + ("d",)), 1)
                elif k == "yt":
                    pe.wait_ge(y_done, y_n[("y",) + st[1:]] + 1)
                    b = jobs[st][0]
                    if free_before[st]:
                        pe.wait_ge(*emptied(st))
                    for i in range(XT):
                        ins = nc.tensor.transpose(ps[:, b, P * i:P * i + P], ycomb[:, 0, P * i:P * i + P], ident)
                    ins.then_inc(filling(st), 1)
                elif k == "ysum":
                    pe.wait_ge(ysq_done, st[1] + 1)
                    b = jobs[st][0]
                    if free_before[st]:
                        pe.wait_ge(*emptied(st))
                    for i in range(XT):
                        ins = mm(ps[:, b, :], ones, gate[:, i, :], start=(i == 0), stop=(i == XT - 1))
                    ins.then_inc(filling(st), 1)
                elif k == "mlp":
                    L = st[1]
                    ntok = T if L == 0 else SEQ
                    u0, plan = unit[st], mlp_plan(L)
                    base = split_at[("norm", L, "ff")]
                    h0 = 2 + FF_CHUNKS * KT * L
                    if L == 0:
                        for key in (st + ("mrow",), st + ("mcol",)):
                            pe.wait_ge(*emptied(key))
                    with pe.Fori(0, FF_CHUNKS, 1) as cc:
                        n = 0
                        for i, (kind, m) in enumerate(plan):
                            if i >= 2 and plan[i - 2][0] == "mod" and plan[i - 2][1] % KQ == KQ - 1:
                                j = MBLOCKS + plan[i - 2][1] // KQ
                                pe.wait_ge(modc_done, j + cc * (MODS_LOOP // KQ))
                                pe.wait_ge(row_done, j + 1 + cc * (MODS_LOOP // KQ))
                                columns(B_TR).then_inc(mcol_done, 1)
                            if kind == "mod":
                                if m % KQ == 0:
                                    pe.wait_ge(row_done, MBLOCKS + m // KQ + cc * (MODS_LOOP // KQ))
                                pe.wait_ge(lo_done, u0 + i + 1 + cc * len(plan))
                                row_product(B_AUX[1], u0 + i, m % KQ).then_inc(mu_used, 1)
                                continue
                            b = B_GEMM[n % 2]
                            pe.wait_ge(lo_done, u0 + i + 1 + cc * len(plan))
                            if 2 <= n < KT + 2:
                                pe.wait_ge(hr_done, FF_CHUNKS * KT * L + n - 1 + cc * KT)
                            else:
                                pe.wait_ge(h_done, mlp_h[L] + (n - 1 - KT if n >= KT else n - 1) + cc * KT)
                            ready = None
                            if kind == "ff1" and m == 0:
                                ready = split_done, base + 1
                            if kind == "ff2" and m == 0:
                                ready = hid_done, h0 + 1 + cc * KT
                            hi, lo = (a_hi, a_lo) if kind == "ff1" else (b_hi, b_lo)
                            product(ps[:, b, 0:ntok], u0 + i, hi, lo, ntok, ready).then_inc(bank_full[b], 1)
                            n += 1
                elif k == "hstat":
                    ntok = odd_tokens[st[1:]]
                    n_sq += 1
                    pe.wait_ge(sq_done, n_sq)
                    if qk_n[st[1:]] == 0:
                        pe.wait_ge(c1_in, 16)
                    b = jobs[st][0]
                    if free_before[st]:
                        pe.wait_ge(*emptied(st))
                    mm(ps[:, b, 0:ntok], cuts["heads"], sq[:, qk_n[st[1:]] % 2, 0:ntok], start=True, stop=True).then_inc(filling(st), 1)
                elif k == "vtok":
                    pe.wait_ge(vT_done, st[1] + 1)
                    b = jobs[st][0]
                    if free_before[st]:
                        pe.wait_ge(*emptied(st))
                    for ch in range(NCH):
                        ins = nc.tensor.transpose(ps[:, b, P * ch:P * ch + P], vT[:, P * ch:P * ch + P], ident)
                    ins.then_inc(filling(st), 1)
                elif k == "rot":
                    pe.wait_ge(qn_done, hn_n[("hnorm",) + st[1:]] + 1)
                    b = jobs[st][0]
                    if free_before[st]:
                        pe.wait_ge(*emptied(st))
                    mm(ps[:, b, 0:SEQ], cuts["perm"], ktile(*st[1:])[:, 0:SEQ], start=True, stop=True).then_inc(filling(st), 1)
                elif k == "dup":
                    pe.wait_ge(rope_done, len(rot_n))
                    for q in range(2):
                        b = jobs[st + (q,)][0]
                        if free_before[st + (q,)]:
                            pe.wait_ge(*emptied(st + (q,)))
                        mm(ps[:, b, :], cuts[f"dup{q}"], kT[:, 0, :], start=True, stop=True).then_inc(filling(st + (q,)), 1)
                elif k == "attn0":
                    pe.wait_ge(kd_done, 2)
                    pe.wait_ge(qn_done, len(hn_n))
                    pe.wait_ge(vtok_done, 5)
                elif k == "S":
                    i = st[1]
                    t, par, qt = ATTN[i]
                    if t >= 4:
                        pe.wait_ge(bias_done, 2)
                    b = jobs[st][0]
                    if free_before[st]:
                        pe.wait_ge(*emptied(st))
                    r0 = HD * par
                    key = kdup[r0:r0 + HD, t // 2, :] if t < 4 else kT[r0:r0 + HD, 1 + t - 4, :]
                    mm(ps[:, b, :], qT[r0:r0 + HD, t, P * qt:P * qt + P], key, start=True, stop=True)
                    if t < 4:
                        o = P * (1 - qt)
                        ins = mm(ps[:, b, o:o + P], ident, cuts["win"][:, P * qt:P * qt + P], start=False, stop=True, skip_group_check=True)
                    else:
                        ins = mm(ps[:, b, 0:SEQ], cuts["flip"], bias[:, qt, 2 * (t - 4) + par, :], start=False, stop=True, skip_group_check=True)
                    ins.then_inc(filling(st), 1)
                elif k == "PT":
                    i = st[1]
                    pe.wait_ge(prob_done, i + 1)
                    b = jobs[st][0]
                    if free_before[st]:
                        pe.wait_ge(*emptied(st))
                    for kk in range(NCH):
                        ins = nc.tensor.transpose(ps[:, b, P * kk:P * kk + P], prob[:, i % 2, P * kk:P * kk + P], ident)
                    ins.then_inc(filling(st), 1)
                elif k == "O":
                    i = st[1]
                    t, par, qt = ATTN[i]
                    pe.wait_ge(pT_done, i + 1)
                    if i % 4 == 0:
                        if free_before[("Opair", t)]:
                            pe.wait_ge(*emptied(("Opair", t)))
                    b = jobs[("Opair", t)][0]
                    col = HD * (t // 2) if t < 4 else P + HD * (2 * (t - 4) + par)
                    for kk in range(NCH):
                        ins = mm(ps[HD * par:HD * par + HD, b, P * qt:P * qt + P], vtok[:, kk, col:col + HD], pT[:, i % 2, P * kk:P * kk + P],
                                 start=(kk == 0), stop=(kk == NCH - 1))
                    ins.then_inc(pv_done, 1)
                elif k == "out":
                    pe.wait_ge(h_done, mlp_h[1] + FF_CHUNKS * KT)
                    for q in range(4):
                        b = jobs[st + (q,)][0]
                        if free_before[st + (q,)]:
                            pe.wait_ge(*emptied(st + (q,)))
                        for i in range(4):
                            f = 4 * (q % 2) + i
                            ins = nc.tensor.transpose(ps[:, b, P * i:P * i + P], hT[:, f, P * (q // 2):P * (q // 2) + P], ident)
                        ins.then_inc(filling(st + (q,)), 1)


_INS = ["x", "c", "ctx", "c_ctx", "w_mod", "b_mod", "norm_mix_g", "norm_ff_g", "w_ff1", "w_ff2", "w_in_even", "conv_w",
        "conv_b", "dt_bias", "a_log", "d_skip", "ssd_norm_g", "w_out_even", "w_in_odd", "q_norm_win", "k_norm_win",
        "sink_win", "q_norm_na", "k_norm_na", "rpb_na", "w_out_odd"]


def kernel(**inputs):
    import numpy as _np
    import concourse.bacc as _bacc
    from concourse import mybir as _mybir
    from concourse.bass_utils import run_bass_kernel_spmd as _run

    nc = _bacc.Bacc("TRN2", target_bir_lowering=False, num_devices=1)
    arrays = {name: _np.ascontiguousarray(inputs[name]) for name in _INS}
    arrays["tables0"], arrays["tables1"] = constants()
    args, maps = [], {}
    for name, a in arrays.items():
        maps[f"in_{name}"] = a
        args.append(nc.dram_tensor(f"in_{name}", a.shape, _mybir.dt.from_np(a.dtype), kind="ExternalInput").ap())
    args.append(nc.dram_tensor("out_0", (1, SEQ, D), _mybir.dt.float32, kind="ExternalOutput").ap())
    trunk(nc, *args)
    r = _run(nc, [maps], core_ids=[0])
    return r.results[0]["out_0"]
```
